# Optimizing a Trainium2 kernel written in Bass

```python
import math
import jax, jax.numpy as jnp
from jax import lax
import numpy as np

D_MODEL = 1024
BATCH = 1
SEQ = 256
DEPTH = 2

HEAD_DIM = 64
N_HEADS_A = 4
N_HEADS_B = 4
N_HEADS_C = 4
N_HEADS_D = 4
N_KV_D = 2
DIFF_DIM = HEAD_DIM // 2
IDX_HEADS = 8
IDX_DIM = 64
TOPK_MAX = 256
WINDOW = 128
BLOCK = 128
D_FF = 4 * D_MODEL
D_PLE = 256
ROPE_THETA = 10000.0
EPS = 1e-6
NEG_INF = -1e30
MIX_WIDTH = (N_HEADS_A + N_HEADS_B + N_HEADS_C + N_HEADS_D) * HEAD_DIM
SPLIT_WIDTHS = (
    N_HEADS_A * HEAD_DIM, N_HEADS_A * HEAD_DIM, N_HEADS_A * HEAD_DIM,
    IDX_HEADS * IDX_DIM, IDX_DIM, IDX_HEADS,
    N_HEADS_B * HEAD_DIM, N_HEADS_B * HEAD_DIM, N_HEADS_B * HEAD_DIM,
    N_HEADS_B,
    N_HEADS_C * HEAD_DIM, N_HEADS_C * HEAD_DIM, N_HEADS_C * HEAD_DIM,
    N_HEADS_D * HEAD_DIM, N_KV_D * HEAD_DIM, N_KV_D * HEAD_DIM,
)
D_IN = sum(SPLIT_WIDTHS)


def rmsnorm(x, g):
    xf = x.astype(jnp.float32)
    y = xf * lax.rsqrt(jnp.mean(xf * xf, axis=-1, keepdims=True) + EPS)
    return (y * g.astype(jnp.float32)).astype(x.dtype)

def rope_tables(positions, dim):
    half = dim // 2
    inv_freq = ROPE_THETA ** (-jnp.arange(half, dtype=jnp.float32) / half)
    ang = positions.astype(jnp.float32)[..., None] * inv_freq
    return jnp.cos(ang)[:, :, None, :], jnp.sin(ang)[:, :, None, :]

def apply_rope(x, tables):
    cos, sin = tables
    half = x.shape[-1] // 2
    xf = x.astype(jnp.float32)
    x1, x2 = xf[..., :half], xf[..., half:]
    return jnp.concatenate([x1 * cos - x2 * sin, x2 * cos + x1 * sin], axis=-1).astype(x.dtype)

def to_blocks(a):
    b, s = a.shape[:2]
    return jnp.moveaxis(a.reshape(b, s // BLOCK, BLOCK, *a.shape[2:]), 1, 0)

def from_blocks(o):
    nb, b = o.shape[:2]
    return jnp.moveaxis(o, 0, 1).reshape(b, nb * BLOCK, *o.shape[3:])

def dsa_attention(q, k, v, iq, ik, iw):
    s_len = k.shape[1]
    topk = min(TOPK_MAX, s_len // 4)
    key_pos = jnp.arange(s_len)
    scale = HEAD_DIM ** -0.5

    def one_block(args):
        qb, iqb, iwb, n = args
        t = n * BLOCK + jnp.arange(BLOCK)
        causal = key_pos[None, :] <= t[:, None]
        dots = jnp.einsum('bthd,bsd->bths', iqb, ik)
        score = jnp.einsum('bth,bths->bts', iwb, jax.nn.relu(dots)).astype(jnp.float32)
        score = jnp.where(causal[None], score, NEG_INF)
        _, idx = lax.top_k(score, topk)
        valid = idx <= t[None, :, None]
        k_sel = jax.vmap(lambda kk, ii: kk[ii])(k, idx)
        v_sel = jax.vmap(lambda vv, ii: vv[ii])(v, idx)
        logits = jnp.einsum('bthd,btjhd->bhtj', qb, k_sel).astype(jnp.float32) * scale
        logits = jnp.where(valid[:, None], logits, NEG_INF)
        probs = jax.nn.softmax(logits, axis=-1).astype(v.dtype)
        return jnp.einsum('bhtj,btjhd->bthd', probs, v_sel)

    nb = s_len // BLOCK
    out = lax.map(one_block, (to_blocks(q), to_blocks(iq), to_blocks(iw), jnp.arange(nb)))
    return from_blocks(out)

def forgetting_attention(q, k, v, log_f):
    s_len = k.shape[1]
    cum_bsh = jnp.cumsum(log_f, axis=1)
    cum = jnp.moveaxis(cum_bsh, 2, 1)
    key_pos = jnp.arange(s_len)
    scale = HEAD_DIM ** -0.5

    def one_block(args):
        qb, cb, n = args
        t = n * BLOCK + jnp.arange(BLOCK)
        causal = key_pos[None, :] <= t[:, None]
        logits = jnp.einsum('bthd,bshd->bhts', qb, k).astype(jnp.float32) * scale
        decay = jnp.moveaxis(cb, 2, 1)[..., :, None] - cum[:, :, None, :]
        logits = jnp.where(causal[None, None], logits + decay, NEG_INF)
        probs = jax.nn.softmax(logits, axis=-1).astype(v.dtype)
        return jnp.einsum('bhts,bshd->bthd', probs, v)

    nb = s_len // BLOCK
    out = lax.map(one_block, (to_blocks(q), to_blocks(cum_bsh), jnp.arange(nb)))
    return from_blocks(out)

def differential_attention(q, k, v, lam, lam_init, subln_g):
    s_len = k.shape[1]
    key_pos = jnp.arange(s_len)
    scale = DIFF_DIM ** -0.5

    def one_block(args):
        qb, n = args
        t = n * BLOCK + jnp.arange(BLOCK)
        causal = key_pos[None, :] <= t[:, None]
        logits = jnp.einsum('bthmd,bshmd->bmhts', qb, k).astype(jnp.float32) * scale
        logits = jnp.where(causal[None, None, None], logits, NEG_INF)
        probs = jax.nn.softmax(logits, axis=-1)
        diff = probs[:, 0] - lam * probs[:, 1]
        return jnp.einsum('bhts,bshd->bthd', diff.astype(v.dtype), v)

    nb = s_len // BLOCK
    out = from_blocks(lax.map(one_block, (to_blocks(q), jnp.arange(nb))))
    return rmsnorm(out, subln_g) * (1.0 - lam_init)

def sliding_window_sink_attention(q, k, v, sinks):
    b, s_len, n_h, dh = q.shape
    n_kv = k.shape[2]
    grp = n_h // n_kv
    nb = s_len // BLOCK
    qb = q.reshape(b, nb, BLOCK, n_kv, grp, dh)
    kb = k.reshape(b, nb, BLOCK, n_kv, dh)
    vb = v.reshape(b, nb, BLOCK, n_kv, dh)
    pad = ((0, 0), (1, 0), (0, 0), (0, 0), (0, 0))
    k_win = jnp.concatenate([jnp.pad(kb, pad)[:, :-1], kb], axis=2)
    v_win = jnp.concatenate([jnp.pad(vb, pad)[:, :-1], vb], axis=2)
    logits = jnp.einsum('bnikgd,bnjkd->bnkgij', qb, k_win).astype(jnp.float32) * (dh ** -0.5)
    i = jnp.arange(BLOCK)[:, None]
    j = jnp.arange(2 * BLOCK)[None, :]
    rel = i + BLOCK - j
    band = (rel >= 0) & (rel < WINDOW)
    in_range = (jnp.arange(nb)[:, None, None] > 0) | (j[None] >= BLOCK)
    mask = band[None] & in_range
    logits = jnp.where(mask[None, :, None, None], logits, NEG_INF)
    sink = jnp.broadcast_to(sinks.astype(jnp.float32).reshape(n_kv, grp)[None, None, :, :, None, None],
                            logits.shape[:-1] + (1,))
    probs = jax.nn.softmax(jnp.concatenate([logits, sink], axis=-1), axis=-1)[..., :-1]
    out = jnp.einsum('bnkgij,bnjkd->bnikgd', probs.astype(v.dtype), v_win)
    return out.reshape(b, s_len, n_h, dh)

def hybrid_layer(x, p_i, rope64, rope32, lam_init, w_in, b_forget, lq1, lk1, lq2, lk2,
                 diff_subln, sinks, w_out, g_pre_mix, g_post_mix, g_pre_mlp, g_post_mlp,
                 w_up, w_down, w_ple_proj, w_ple_gate):
    b, s_len, _ = x.shape
    h = rmsnorm(x, g_pre_mix)
    proj = h @ w_in
    points = np.cumsum(SPLIT_WIDTHS)[:-1].tolist()
    (a_q, a_k, a_v, a_iq, a_ik, a_iw, b_q, b_k, b_v, b_f,
     c_q, c_k, c_v, d_q, d_k, d_v) = jnp.split(proj, points, axis=-1)

    def heads(t, n, d):
        return t.reshape(b, s_len, n, d)

    iw = a_iw * (IDX_HEADS ** -0.5 * IDX_DIM ** -0.5)
    o_a = dsa_attention(apply_rope(heads(a_q, N_HEADS_A, HEAD_DIM), rope64),
                        apply_rope(heads(a_k, N_HEADS_A, HEAD_DIM), rope64),
                        heads(a_v, N_HEADS_A, HEAD_DIM),
                        apply_rope(heads(a_iq, IDX_HEADS, IDX_DIM), rope64),
                        apply_rope(a_ik[:, :, None, :], rope64)[:, :, 0],
                        iw)
    log_f = jax.nn.log_sigmoid((b_f + b_forget).astype(jnp.float32))
    o_b = forgetting_attention(heads(b_q, N_HEADS_B, HEAD_DIM), heads(b_k, N_HEADS_B, HEAD_DIM),
                               heads(b_v, N_HEADS_B, HEAD_DIM), log_f)
    cq = apply_rope(heads(c_q, 2 * N_HEADS_C, DIFF_DIM), rope32).reshape(b, s_len, N_HEADS_C, 2, DIFF_DIM)
    ck = apply_rope(heads(c_k, 2 * N_HEADS_C, DIFF_DIM), rope32).reshape(b, s_len, N_HEADS_C, 2, DIFF_DIM)
    f32 = jnp.float32
    lam = (jnp.exp(jnp.sum(lq1.astype(f32) * lk1.astype(f32)))
           - jnp.exp(jnp.sum(lq2.astype(f32) * lk2.astype(f32))) + lam_init)
    o_c = differential_attention(cq, ck, heads(c_v, N_HEADS_C, HEAD_DIM), lam, lam_init, diff_subln)
    o_d = sliding_window_sink_attention(apply_rope(heads(d_q, N_HEADS_D, HEAD_DIM), rope64),
                                        apply_rope(heads(d_k, N_KV_D, HEAD_DIM), rope64),
                                        heads(d_v, N_KV_D, HEAD_DIM), sinks)

    mix = jnp.concatenate([o_a.reshape(b, s_len, -1), o_b.reshape(b, s_len, -1),
                           o_c.reshape(b, s_len, -1), o_d.reshape(b, s_len, -1)], axis=-1)
    x = x + rmsnorm(mix @ w_out, g_post_mix)

    h = rmsnorm(x, g_pre_mlp)
    m = jnp.square(jax.nn.relu(h @ w_up)) @ w_down
    x = x + rmsnorm(m, g_post_mlp)

    x = x + jax.nn.sigmoid(x @ w_ple_gate) * (p_i @ w_ple_proj)
    return x

def first_inputs(seed: int = 0) -> dict:
    key = jax.random.key(seed)
    ks = jax.random.split(key, 22)

    def normal(k, shape, scale):
        return jax.random.normal(k, shape, jnp.float32) * scale

    def gain(k, shape):
        return 1.0 + 0.02 * jax.random.normal(k, shape, jnp.float32)

    return {
        'x': normal(ks[0], (BATCH, SEQ, D_MODEL), 1.0),
        'p': normal(ks[1], (DEPTH, BATCH, SEQ, D_PLE), 1.0),
        'positions': jnp.broadcast_to(jnp.arange(SEQ, dtype=jnp.int32), (BATCH, SEQ)),
        'w_in': normal(ks[2], (DEPTH, D_MODEL, D_IN), D_MODEL ** -0.5),
        'b_forget': 2.0 + normal(ks[3], (DEPTH, N_HEADS_B), 0.5),
        'lambda_q1': normal(ks[4], (DEPTH, DIFF_DIM), 0.1),
        'lambda_k1': normal(ks[5], (DEPTH, DIFF_DIM), 0.1),
        'lambda_q2': normal(ks[6], (DEPTH, DIFF_DIM), 0.1),
        'lambda_k2': normal(ks[7], (DEPTH, DIFF_DIM), 0.1),
        'diff_subln': gain(ks[8], (DEPTH, HEAD_DIM)),
        'sinks': normal(ks[9], (DEPTH, N_HEADS_D), 1.0),
        'w_out': normal(ks[10], (DEPTH, MIX_WIDTH, D_MODEL), MIX_WIDTH ** -0.5),
        'norm_pre_mix': gain(ks[11], (DEPTH, D_MODEL)),
        'norm_post_mix': gain(ks[12], (DEPTH, D_MODEL)),
        'norm_pre_mlp': gain(ks[13], (DEPTH, D_MODEL)),
        'norm_post_mlp': gain(ks[14], (DEPTH, D_MODEL)),
        'w_mlp_up': normal(ks[15], (DEPTH, D_MODEL, D_FF), D_MODEL ** -0.5),
        'w_mlp_down': normal(ks[16], (DEPTH, D_FF, D_MODEL), D_FF ** -0.5),
        'w_ple_proj': normal(ks[17], (DEPTH, D_PLE, D_MODEL), D_PLE ** -0.5),
        'w_ple_gate': normal(ks[18], (DEPTH, D_MODEL, D_MODEL), D_MODEL ** -0.5),
    }

def first_block(x, p, positions, w_in, b_forget, lambda_q1, lambda_k1, lambda_q2, lambda_k2,
              diff_subln, sinks, w_out, norm_pre_mix, norm_post_mix, norm_pre_mlp, norm_post_mlp,
              w_mlp_up, w_mlp_down, w_ple_proj, w_ple_gate):
    rope64 = rope_tables(positions, HEAD_DIM)
    rope32 = rope_tables(positions, DIFF_DIM)
    for i in range(DEPTH):
        lam_init = 0.8 - 0.6 * math.exp(-0.3 * i)
        x = hybrid_layer(x, p[i], rope64, rope32, lam_init, w_in[i], b_forget[i],
                         lambda_q1[i], lambda_k1[i], lambda_q2[i], lambda_k2[i],
                         diff_subln[i], sinks[i], w_out[i], norm_pre_mix[i], norm_post_mix[i],
                         norm_pre_mlp[i], norm_post_mlp[i], w_mlp_up[i], w_mlp_down[i],
                         w_ple_proj[i], w_ple_gate[i])
    return x


D_MIX = D_MODEL
A_DIM = D_MIX // 4
A_GROUPS = 4
A_CHUNK = 128
B_HEAD_DIM = 128
B_DIM = D_MIX // 2
B_HEADS = B_DIM // B_HEAD_DIM
B_CONV = 4
B_CHUNK = 64
C_HEAD_DIM = 64
C_DIM = D_MIX - A_DIM - B_DIM
C_HEADS = C_DIM // C_HEAD_DIM
C_CONFIGS = ((128, 1), (512, 4), (2048, 16))
C_QBLOCK = 128
IN_SIZES = (A_DIM, A_DIM, 3 * B_DIM, B_DIM, B_HEADS, B_HEADS, C_DIM, C_DIM, C_DIM)
D_IN_2 = sum(IN_SIZES)
D_FF_2 = ((8 * D_MODEL // 3 + 127) // 128) * 128
N_EXPERTS = 8
TOP_K = 2
N_DENSE = (DEPTH + 1) // 2
N_MOE = DEPTH // 2
DN_ALPHA = (2.0 * DEPTH) ** 0.25
DN_BETA = (8.0 * DEPTH) ** -0.25


def layer_norm(x, g, b, eps=1e-5):
    xf = x.astype(jnp.float32)
    mu = jnp.mean(xf, axis=-1, keepdims=True)
    var = jnp.mean(jnp.square(xf - mu), axis=-1, keepdims=True)
    return ((xf - mu) * lax.rsqrt(var + eps) * g + b).astype(x.dtype)

def rope(x):
    S, dh = x.shape[1], x.shape[-1]
    inv_freq = ROPE_THETA ** (-jnp.arange(0, dh, 2, dtype=jnp.float32) / dh)
    ang = jnp.arange(S, dtype=jnp.float32)[:, None] * inv_freq[None, :]
    cos = jnp.cos(ang)[None, :, None, :]
    sin = jnp.sin(ang)[None, :, None, :]
    x1 = x[..., : dh // 2].astype(jnp.float32)
    x2 = x[..., dh // 2:].astype(jnp.float32)
    return jnp.concatenate([x1 * cos - x2 * sin, x2 * cos + x1 * sin], axis=-1).astype(x.dtype)

def gmlp_spatial_gate(u, v, ln_g, ln_b, w_s, b_s):
    Bsz, S, _ = u.shape
    v = layer_norm(v, ln_g, ln_b)
    causal = jnp.tril(jnp.ones((A_CHUNK, A_CHUNK), dtype=bool))
    w = jnp.where(causal[None], w_s, jnp.zeros_like(w_s)).astype(v.dtype)
    vc = v.reshape(Bsz, S // A_CHUNK, A_CHUNK, A_GROUPS, A_DIM // A_GROUPS)
    mixed = jnp.einsum('gts,bnsgc->bntgc', w, vc) + b_s.T.astype(v.dtype)[None, None, :, :, None]
    return u * mixed.reshape(Bsz, S, A_DIM)

def causal_dwconv(x, w):
    K = w.shape[0]
    return lax.conv_general_dilated(
        x, w[:, None, :].astype(x.dtype), window_strides=(1,), padding=[(K - 1, 0)],
        dimension_numbers=('NWC', 'WIO', 'NWC'), feature_group_count=x.shape[-1])

def gated_deltanet(q, k, v, z, beta_logit, a_logit, a_log, dt_bias, norm_g):
    f32 = jnp.float32
    Bsz, S, _ = q.shape
    H, dk, C = B_HEADS, B_HEAD_DIM, B_CHUNK
    N = S // C
    q = q.reshape(Bsz, S, H, dk).astype(f32)
    k = k.reshape(Bsz, S, H, dk).astype(f32)
    v = v.reshape(Bsz, S, H, dk).astype(f32)
    q = q * lax.rsqrt(jnp.sum(q * q, -1, keepdims=True) + 1e-6) * (dk ** -0.5)
    k = k * lax.rsqrt(jnp.sum(k * k, -1, keepdims=True) + 1e-6)
    beta = jax.nn.sigmoid(beta_logit.astype(f32))
    g = -jnp.exp(a_log.astype(f32)) * jax.nn.softplus(a_logit.astype(f32) + dt_bias.astype(f32))

    def chunk(t):
        return t.reshape(Bsz, N, C, H, -1).transpose(0, 3, 1, 2, 4)

    qc, kc, vc = chunk(q), chunk(k), chunk(v)
    bc = chunk(beta[..., None])
    gc = jnp.cumsum(chunk(g[..., None])[..., 0], axis=-1)
    lower = jnp.tril(jnp.ones((C, C), dtype=bool))
    strict = jnp.tril(jnp.ones((C, C), dtype=bool), -1)
    decay = jnp.exp(jnp.where(lower, gc[..., :, None] - gc[..., None, :], -jnp.inf))
    k_beta = kc * bc
    m = jnp.where(strict, jnp.einsum('bhnid,bhnjd->bhnij', k_beta, kc) * decay, 0.0)
    eye = jnp.eye(C, dtype=f32)
    rhs = jnp.concatenate([vc * bc, k_beta * jnp.exp(gc)[..., None]], axis=-1)
    sol = lax.linalg.triangular_solve(eye + m, rhs, left_side=True, lower=True, unit_diagonal=True)
    u_c, w_c = sol[..., :dk], sol[..., dk:]
    attn_local = jnp.einsum('bhnid,bhnjd->bhnij', qc, kc) * decay
    q_dec = qc * jnp.exp(gc)[..., None]
    k_dec = kc * jnp.exp(gc[..., -1:] - gc)[..., None]
    g_last = jnp.exp(gc[..., -1])

    def step(state, xs):
        u_i, w_i, a_i, qd_i, kd_i, gl_i = xs
        v_new = u_i - jnp.einsum('bhcd,bhde->bhce', w_i, state)
        o = jnp.einsum('bhcd,bhde->bhce', qd_i, state) + jnp.einsum('bhij,bhje->bhie', a_i, v_new)
        state = state * gl_i[..., None, None] + jnp.einsum('bhcd,bhce->bhde', kd_i, v_new)
        return state, o

    xs = tuple(jnp.moveaxis(t, 2, 0) for t in (u_c, w_c, attn_local, q_dec, k_dec, g_last))
    _, o = lax.scan(step, jnp.zeros((Bsz, H, dk, dk), f32), xs)
    o = o.transpose(1, 0, 3, 2, 4).reshape(Bsz, S, H, dk)
    o = o * lax.rsqrt(jnp.mean(o * o, -1, keepdims=True) + 1e-6) * norm_g.astype(f32)
    o = o * jax.nn.silu(z.reshape(Bsz, S, H, dk).astype(f32))
    return o.reshape(Bsz, S, B_DIM).astype(z.dtype)

def dilated_attention(q, k, v):
    f32 = jnp.float32
    Bsz, S, H, dh = q.shape
    nblk = S // C_QBLOCK
    qb = (q * (dh ** -0.5)).reshape(Bsz, nblk, C_QBLOCK, H, dh).transpose(1, 0, 2, 3, 4)

    def block(args):
        blk, q_blk = args
        t = blk * C_QBLOCK + jnp.arange(C_QBLOCK)
        outs, lses = [], []
        for window, dil in C_CONFIGS:
            j = jnp.arange(window // dil + 1)
            idx = t[:, None] - dil * j[None, :]
            valid = idx >= 0
            idx = jnp.maximum(idx, 0)
            kg = jnp.take(k, idx, axis=1)
            vg = jnp.take(v, idx, axis=1)
            s = jnp.einsum('bqhd,bqjhd->bhqj', q_blk, kg).astype(f32)
            s = jnp.where(valid[None, None], s, -jnp.inf)
            mx = jnp.max(s, axis=-1, keepdims=True)
            e = jnp.exp(s - mx)
            den = jnp.sum(e, axis=-1)
            outs.append(jnp.einsum('bhqj,bqjhd->bqhd', e / den[..., None], vg.astype(f32)))
            lses.append(mx[..., 0] + jnp.log(den))
        wts = jax.nn.softmax(jnp.stack(lses, axis=0), axis=0)
        out = jnp.einsum('cbhq,cbqhd->bqhd', wts, jnp.stack(outs, axis=0))
        return out.astype(q_blk.dtype)

    out = lax.map(block, (jnp.arange(nblk), qb))
    return out.transpose(1, 0, 2, 3, 4).reshape(Bsz, S, H * dh)

def token_mixer(x, w_in, conv_w, a_ln_g, a_ln_b, a_ws, a_bs, b_a_log, b_dt_bias, b_norm_g, w_out):
    Bsz, S, _ = x.shape
    h = x @ w_in
    offs = [int(o) for o in np.cumsum(IN_SIZES)[:-1]]
    a_u, a_v, b_qkv, b_z, b_beta, b_a, c_q, c_k, c_v = jnp.split(h, offs, axis=-1)
    y_a = gmlp_spatial_gate(jax.nn.gelu(a_u), jax.nn.gelu(a_v), a_ln_g, a_ln_b, a_ws, a_bs)
    b_qkv = jax.nn.silu(causal_dwconv(b_qkv, conv_w))
    b_q, b_k, b_v = jnp.split(b_qkv, [B_DIM, 2 * B_DIM], axis=-1)
    y_b = gated_deltanet(b_q, b_k, b_v, b_z, b_beta, b_a, b_a_log, b_dt_bias, b_norm_g)
    cq = rope(c_q.reshape(Bsz, S, C_HEADS, C_HEAD_DIM))
    ck = rope(c_k.reshape(Bsz, S, C_HEADS, C_HEAD_DIM))
    cv = c_v.reshape(Bsz, S, C_HEADS, C_HEAD_DIM)
    y_c = dilated_attention(cq, ck, cv)
    return jnp.concatenate([y_a, y_b, y_c], axis=-1) @ w_out

def swiglu(x, w_gate, w_up, w_down):
    return (jax.nn.silu(x @ w_gate) * (x @ w_up)) @ w_down

def moe_swiglu(x, w_router, w_gate, w_up, w_down):
    Bsz, S, D = x.shape
    xt = x.reshape(Bsz * S, D)
    logits = (xt @ w_router).astype(jnp.float32)
    top_vals, top_idx = lax.top_k(logits, TOP_K)
    probs = jax.nn.softmax(top_vals, axis=-1)
    combine = jnp.sum(jax.nn.one_hot(top_idx, N_EXPERTS, dtype=jnp.float32) * probs[..., None], axis=1)

    def expert(acc, params):
        wg, wu, wd, c = params
        return acc + c[:, None].astype(xt.dtype) * swiglu(xt, wg, wu, wd), None

    acc, _ = lax.scan(expert, jnp.zeros_like(xt), (w_gate, w_up, w_down, combine.T))
    return acc.reshape(Bsz, S, D)

def second_inputs(seed: int = 0) -> dict:
    key = jax.random.key(seed)
    ks = jax.random.split(key, 24)
    nrm = jax.random.normal
    x = nrm(ks[0], (BATCH, SEQ, D_MODEL), jnp.float32)
    w_in = nrm(ks[1], (DEPTH, D_MODEL, D_IN_2), jnp.float32) * D_MODEL ** -0.5
    conv_w = nrm(ks[2], (DEPTH, B_CONV, 3 * B_DIM), jnp.float32) * B_CONV ** -0.5
    a_ln_g = 1.0 + 0.02 * nrm(ks[3], (DEPTH, A_DIM), jnp.float32)
    a_ln_b = 0.02 * nrm(ks[4], (DEPTH, A_DIM), jnp.float32)
    a_ws = nrm(ks[5], (DEPTH, A_GROUPS, A_CHUNK, A_CHUNK), jnp.float32) * A_CHUNK ** -0.5
    a_bs = 1.0 + 0.02 * nrm(ks[6], (DEPTH, A_GROUPS, A_CHUNK), jnp.float32)
    b_a_log = jnp.log(jax.random.uniform(ks[7], (DEPTH, B_HEADS), jnp.float32, 1.0, 16.0))
    dt = jnp.exp(jax.random.uniform(ks[8], (DEPTH, B_HEADS), jnp.float32, math.log(1e-3), math.log(1e-1)))
    b_dt_bias = dt + jnp.log(-jnp.expm1(-dt))
    b_norm_g = 1.0 + 0.02 * nrm(ks[9], (DEPTH, B_HEAD_DIM), jnp.float32)
    w_out = nrm(ks[10], (DEPTH, D_MIX, D_MODEL), jnp.float32) * (D_MIX ** -0.5) * DN_BETA
    ln1_g = 1.0 + 0.02 * nrm(ks[11], (DEPTH, D_MODEL), jnp.float32)
    ln1_b = 0.02 * nrm(ks[12], (DEPTH, D_MODEL), jnp.float32)
    ln2_g = 1.0 + 0.02 * nrm(ks[13], (DEPTH, D_MODEL), jnp.float32)
    ln2_b = 0.02 * nrm(ks[14], (DEPTH, D_MODEL), jnp.float32)
    ffn_w_gate = nrm(ks[15], (N_DENSE, D_MODEL, D_FF_2), jnp.float32) * D_MODEL ** -0.5
    ffn_w_up = nrm(ks[16], (N_DENSE, D_MODEL, D_FF_2), jnp.float32) * D_MODEL ** -0.5
    ffn_w_down = nrm(ks[17], (N_DENSE, D_FF_2, D_MODEL), jnp.float32) * (D_FF_2 ** -0.5) * DN_BETA
    moe_router = nrm(ks[18], (N_MOE, D_MODEL, N_EXPERTS), jnp.float32) * D_MODEL ** -0.5
    moe_w_gate = nrm(ks[19], (N_MOE, N_EXPERTS, D_MODEL, D_FF_2), jnp.float32) * D_MODEL ** -0.5
    moe_w_up = nrm(ks[20], (N_MOE, N_EXPERTS, D_MODEL, D_FF_2), jnp.float32) * D_MODEL ** -0.5
    moe_w_down = nrm(ks[21], (N_MOE, N_EXPERTS, D_FF_2, D_MODEL), jnp.float32) * (D_FF_2 ** -0.5) * DN_BETA
    return {"x": x, "w_in": w_in, "conv_w": conv_w, "a_ln_g": a_ln_g, "a_ln_b": a_ln_b,
            "a_ws": a_ws, "a_bs": a_bs, "b_a_log": b_a_log, "b_dt_bias": b_dt_bias,
            "b_norm_g": b_norm_g, "w_out": w_out, "ln1_g": ln1_g, "ln1_b": ln1_b,
            "ln2_g": ln2_g, "ln2_b": ln2_b, "ffn_w_gate": ffn_w_gate, "ffn_w_up": ffn_w_up,
            "ffn_w_down": ffn_w_down, "moe_router": moe_router, "moe_w_gate": moe_w_gate,
            "moe_w_up": moe_w_up, "moe_w_down": moe_w_down}

def second_block(x, w_in, conv_w, a_ln_g, a_ln_b, a_ws, a_bs, b_a_log, b_dt_bias, b_norm_g, w_out,
              ln1_g, ln1_b, ln2_g, ln2_b, ffn_w_gate, ffn_w_up, ffn_w_down,
              moe_router, moe_w_gate, moe_w_up, moe_w_down):
    for layer in range(DEPTH):
        mix = token_mixer(x, w_in[layer], conv_w[layer], a_ln_g[layer], a_ln_b[layer], a_ws[layer],
                          a_bs[layer], b_a_log[layer], b_dt_bias[layer], b_norm_g[layer], w_out[layer])
        x = layer_norm(DN_ALPHA * x + mix, ln1_g[layer], ln1_b[layer])
        i = layer // 2
        if layer % 2 == 0:
            f = swiglu(x, ffn_w_gate[i], ffn_w_up[i], ffn_w_down[i])
        else:
            f = moe_swiglu(x, moe_router[i], moe_w_gate[i], moe_w_up[i], moe_w_down[i])
        x = layer_norm(DN_ALPHA * x + f, ln2_g[layer], ln2_b[layer])
    return x


def setup_inputs(seed=0):
    out = dict(first_inputs(seed))
    for name, value in second_inputs(seed + 1).items():
        if name != "x":
            out[name + "_2"] = value
    return out


def reference(
    x, p, positions, w_in, b_forget, lambda_q1, lambda_k1, lambda_q2, lambda_k2, diff_subln,
    sinks, w_out, norm_pre_mix, norm_post_mix, norm_pre_mlp, norm_post_mlp, w_mlp_up,
    w_mlp_down, w_ple_proj, w_ple_gate, w_in_2, conv_w_2, a_ln_g_2, a_ln_b_2, a_ws_2, a_bs_2,
    b_a_log_2, b_dt_bias_2, b_norm_g_2, w_out_2, ln1_g_2, ln1_b_2, ln2_g_2, ln2_b_2,
    ffn_w_gate_2, ffn_w_up_2, ffn_w_down_2, moe_router_2, moe_w_gate_2, moe_w_up_2,
    moe_w_down_2,
):
    x = first_block(
        x, p, positions, w_in, b_forget, lambda_q1, lambda_k1, lambda_q2, lambda_k2, diff_subln,
        sinks, w_out, norm_pre_mix, norm_post_mix, norm_pre_mlp, norm_post_mlp, w_mlp_up,
        w_mlp_down, w_ple_proj, w_ple_gate,
    )
    return second_block(
        x, w_in_2, conv_w_2, a_ln_g_2, a_ln_b_2, a_ws_2, a_bs_2, b_a_log_2, b_dt_bias_2,
        b_norm_g_2, w_out_2, ln1_g_2, ln1_b_2, ln2_g_2, ln2_b_2, ffn_w_gate_2, ffn_w_up_2,
        ffn_w_down_2, moe_router_2, moe_w_gate_2, moe_w_up_2, moe_w_down_2,
    )


_drawn_inputs = setup_inputs


def setup_inputs(seed=0):
    import zlib

    import numpy as np

    out = dict(_drawn_inputs(seed))
    spreads = {}
    factors = {'lambda_q2': 3.304,
     'a_ln_g_2': 25.028,
     'a_ln_b_2': 28.665,
     'a_bs_2': 7.547,
     'b_norm_g_2': 14.982}
    for name, (base, spread) in spreads.items():
        noise = np.random.default_rng([zlib.crc32(name.encode()), seed]).standard_normal(out[name].shape)
        drawn = base * np.exp(spread * noise) if base else spread * noise
        out[name] = __import__('jax').numpy.asarray(drawn.astype(out[name].dtype))
    for name, factor in factors.items():
        out[name] = (out[name] * factor).astype(out[name].dtype)
    return out
```

```python
import math
from contextlib import ExitStack

import numpy as np

import concourse.bass as bass
from concourse import mybir

F32 = mybir.dt.float32
F32R = mybir.dt.float32r
I32 = mybir.dt.int32
U32 = mybir.dt.uint32
ALU = mybir.AluOpType
ACT = mybir.ActivationFunctionType
AX_X = mybir.AxisListType.X

P = 128
D = 1024
S = 256
NTB = S // P
KT = D // P
DEPTH = 2
EPS = 1e-6
BIG = 1e30
TAKEN = -3e38
HD = 64
TOPK = min(256, S // 4)
D_FF = 4 * D
D_PLE = 256
A_Q, A_K, A_V, A_IQ, A_IK, A_IW = 0, 256, 512, 768, 1280, 1344
B_Q, B_K, B_V, B_F = 1352, 1608, 1864, 2120
C_Q, C_K, C_V = 2124, 2380, 2636
D_Q, D_K, D_V, D_IN = 2892, 3148, 3276, 3404
IDX_HEADS = 8
D_IN2 = 3336
H2 = 4
DK = 128
CHUNK = 64
LEVELS = 6
FF2 = 2816
FT2 = FF2 // P
CH2 = 256
NCH2 = FF2 // CH2
NE = 8
ALPHA = (2.0 * DEPTH) ** 0.25

R = 6
H = 3
SLOT = 2048
DOWN2 = [2] * 8 + [1] * 6
USES_E = 2 * NCH2 + len(DOWN2)
assert sum(DOWN2) == FT2 and USES_E % R == 0 and USES_E % H == 0
CT_N = 2 * NE + 2
GATHER_AT = 5


def consts():
    i = np.arange(P)
    s_, t_ = i[:, None], i[None, :]
    cols, at = [], {}

    def put(name, a):
        a = np.asarray(a, np.float32).reshape(P, -1)
        at[name] = (sum(c.shape[1] for c in cols), a.shape[1])
        cols.append(a)

    put("ident", np.eye(P))
    causal = np.where(i[None, :] <= i[:, None], 0.0, BIG)
    put("nm", np.concatenate([np.zeros((P, P)), causal], 1))
    slide = np.where(i[None, :] > i[:, None], 0.0, BIG)
    put("nm_slide", np.concatenate([slide, causal], 1))
    for tb in range(NTB):
        t = tb * P + i[:, None]
        s = np.arange((tb + 1) * P)[None, :]
        n = np.zeros((P, (tb + 1) * P))
        for window, dil in ((128, 1), (512, 4), (2048, 16)):
            n += (s <= t) & ((t - s) % dil == 0) & (t - s <= window)
        put(f"nm_dil{tb}", np.where(n > 0, -np.log(np.maximum(n, 1)), BIG))
    put("upper1", np.concatenate([s_ <= t_, np.ones((P, P))], 1))
    put("before", s_ < t_)
    same = (s_ // CHUNK) == (t_ // CHUNK)
    put("chunk_upper", same & (s_ <= t_))
    put("chunk_ones", same)
    put("nm_chunk", np.where(same & (s_ <= t_), 0.0, BIG))
    for l in range(LEVELS):
        b = 1 << l
        put(f"level{l}", (s_ // (2 * b) == t_ // (2 * b)) & ((t_ // b) % 2 == 1) & ((s_ // b) % 2 == 0))
    put("iota", np.broadcast_to(i[None, :], (P, P)))
    half = HD // 2
    inv = (np.float32(10000.0) ** (-np.arange(half, dtype=np.float32) / np.float32(half))).astype(np.float32)
    inv32 = (np.float32(10000.0) ** (-np.arange(16, dtype=np.float32) / np.float32(16))).astype(np.float32)
    put("inv_freq", np.broadcast_to(np.concatenate([inv, inv32])[None], (P, 48)))
    tok = np.arange(S, dtype=np.float32).reshape(NTB, P)
    inv2 = (np.float32(10000.0) ** (-np.arange(0, HD, 2, dtype=np.float32) / np.float32(HD))).astype(np.float32)
    ang = (tok[:, :, None] * inv2).astype(np.float32).astype(np.float64)
    put("cos2", np.concatenate([np.cos(ang), np.cos(ang)], 2).transpose(1, 0, 2))
    put("sin2", np.concatenate([-np.sin(ang), np.sin(ang)], 2).transpose(1, 0, 2))
    put("one", np.ones((P, 1)))
    put("eps", np.full((P, 1), EPS))
    put("mhalf", np.full((P, 16), -0.5))
    return np.ascontiguousarray(np.concatenate(cols, 1)), at


class Signal:

    def __init__(self, sem):
        self.sem, self.made, self.seen = sem, 0, {}

    def next(self, who, n=1):
        self.seen[who] = self.seen.get(who, 0) + n
        return self.seen[who]


def build(nc, at, n_const, const_d, w, out_d):
    ctx = ExitStack()

    def sb(name, shape, dt=F32):
        return ctx.enter_context(nc.sbuf_tensor(name, shape, dt))

    def sig(name):
        return Signal(ctx.enter_context(nc.semaphore(name)))

    def base_now():
        return (nc.sbuf_base + 31) // 32 * 32

    def parts_at(name, base, o, shape):
        return nc.alloc_sbuf_tensor_at(name, shape, F32R, offset=base + 4 * o)

    ring_base = base_now()
    ring = sb("ring", [P, R, SLOT])
    ring_lo = parts_at("ring_lo", ring_base, 0, [P, R, SLOT])
    ring_hi = sb("ring_hi", [P, H, SLOT], F32R)
    X = sb("X", [P, NTB, D])
    XN = sb("XN", [P, NTB, D])
    xTh = sb("xTh", [P, KT, S], F32R)
    xTl = sb("xTl", [P, KT, S], F32R)
    RW = sb("RW", [P, KT, NE])
    RWh, RWl = sb("RWh", [P, KT, NE], F32R), sb("RWl", [P, KT, NE], F32R)
    C = sb("C", [P, n_const])
    VEC = sb("VEC", [P, 2, D])
    COLS = sb("COLS", [P, P + 8])
    SM = sb("SM", [P, 900])
    POS = sb("POS", [P, NTB], I32)
    IDX = sb("IDX", [P, NTB, 8], U32)
    FLAG = sb("FLAG", [P, 2], I32)
    ARENA_N = 17472
    arena_base = base_now()
    ARENA = sb("ARENA", [P, ARENA_N])

    G = ctx.enter_context(nc.psum_tensor("G", [P, 4, 512], F32))
    T = [ctx.enter_context(nc.psum_tensor(f"T{i}", [P, 512], F32)) for i in range(2)]
    Sp = ctx.enter_context(nc.psum_tensor("Sp", [P, 2, 512], F32))

    def c(name):
        o, n = at[name]
        return C[:, o:o + n]

    ident = c("ident")
    small_at = [0]

    def small(n):
        o = small_at[0]
        small_at[0] += n
        assert small_at[0] <= 900
        return SM[:, o:o + n]

    p_bf, p_sink = small(8), small(8)
    p_lam = small(256).rearrange("p (v l d) -> p v l d", v=4, l=2)
    p_sub = small(128).rearrange("p (l d) -> p l d", l=2)
    p_alog, p_dt = small(8), small(8)
    p_bn = small(256).rearrange("p (l d) -> p l d", l=2)
    ssq, ms, rstd = small(2), small(2), small(2)
    posf = small(2)
    nmx = small(8).rearrange("p (b m) -> p b m", b=2)
    rsum = small(8).rearrange("p (b m) -> p b m", b=2)
    esk = small(8).rearrange("p (b m) -> p b m", b=2)
    rinv = small(8).rearrange("p (b m) -> p b m", b=2)
    nsink = small(4)
    lamt = small(4)
    top8 = small(8)
    gc16, kds8, eg8, bek8 = small(16), small(8), small(8), small(8)
    EGL = small(16).rearrange("p (t h c) -> p t h c", t=2, h=4)
    iws, cums = small(16).rearrange("p (t h) -> p t h", t=2), small(8).rearrange("p (t h) -> p t h", t=2)
    ea4 = small(4)
    ms8, r8 = small(8), small(8)
    bst = small(24).rearrange("p (t n) -> p t n", t=2)
    mv = small(4).rearrange("p (t n) -> p t n", t=2)

    def ar(o, n):
        assert o + n <= ARENA_N, (o, n)
        return ARENA[:, o:o + n]

    PROWS = ar(1024, P)
    ABS = ar(1024 + P, P)[0:8, :]
    PROJ = ar(0, NTB * D_IN).rearrange("p (t n) -> p t n", t=NTB)
    o = NTB * D_IN
    QKT = ar(o, 21 * S).rearrange("p (b s) -> p b s", b=21)
    o += 21 * S
    L = ar(o, 2 * 4 * S).rearrange("p (b m s) -> p b m s", b=2, m=4)
    ROPE_A = ar(o, 1024)
    ROPE_B = ar(o + 1024, 1024)
    o += 2 * 4 * S
    PT = ar(o, 1024).rearrange("p (k m t) -> p k m t", k=2, m=4)
    o += 1024
    NMB = ar(o, 1536)
    NMB0 = ar(o, 512).rearrange("p (h s) -> p h s", h=4)
    NMB1 = ar(o + 512, 1024).rearrange("p (h s) -> p h s", h=4)
    o += 1536
    NMA = ar(o, 512).rearrange("p (t s) -> p t s", t=2)
    o += 512
    AT_ = sb("AT_", [P, 8, P])
    IKD = AT_[:, 0:6, :].rearrange("p (q t) n -> p q t n", q=3)
    LF = sb("LF", [P, NTB, 4])
    GL = sb("GL", [P, NTB, 4])
    BETA = sb("BETA", [P, NTB, 4])
    ROT = sb("ROT", [P, 384])
    RCOS = ROT[:, 0:128].rearrange("p (t n) -> p t n", t=2)
    RSIN = ROT[:, 128:256].rearrange("p (t n) -> p t n", t=2)
    RCOS32 = ROT[:, 256:320].rearrange("p (t n) -> p t n", t=2)
    RSIN32 = ROT[:, 320:384].rearrange("p (t n) -> p t n", t=2)
    ANG = ar(0, 96).rearrange("p (t n) -> p t n", t=2)
    KK_ = ar(96, 96).rearrange("p (t n) -> p t n", t=2)
    SN = ar(192, 96).rearrange("p (t n) -> p t n", t=2)
    SH = ar(288, 96).rearrange("p (t n) -> p t n", t=2)
    hTh = parts_at("hTh", arena_base, 0, [P, 32, S])
    hTl = parts_at("hTl", arena_base, 32 * S, [P, 32, S])
    HB = XN[:, :, :].rearrange("p b (t n) -> p b t n", t=NTB)
    PLE = ar(64 * S, NTB * D_PLE).rearrange("p (t n) -> p t n", t=NTB)
    PLETh = parts_at("PLETh", arena_base, 0, [P, 2, S])
    PLETl = parts_at("PLETl", arena_base, 2 * S, [P, 2, S])
    P2 = ar(0, NTB * 1800).rearrange("p (t n) -> p t n", t=NTB)
    A2, Z2, BA2, C2 = 0, 512, 1024, 1032
    o2 = 3600
    PAD = ar(o2, 12 * (S + 3)).rearrange("p (b s) -> p b s", b=12)
    TN = ar(o2, 1024).rearrange("p (i t) -> p i t", i=8)
    TT = ar(o2 + 1024, 1024).rearrange("p (i t) -> p i t", i=8)
    WB = ar(o2 + 2048, 1024).rearrange("p (i t) -> p i t", i=8)
    o2 += 12 * (S + 3)
    CV = ar(o2, 12 * S).rearrange("p (b s) -> p b s", b=12)
    o2 += 12 * S
    SQ = ar(o2, 2048)
    MLV = [ar(o2 + 1024 * i, 1024).rearrange("p (i t) -> p i t", i=8) for i in range(2)]
    o2 += 2048
    VB = ar(o2, 1024).rearrange("p (i e) -> p i e", i=8)
    KBE = ar(o2 + 1024, 1024).rearrange("p (i e) -> p i e", i=8)
    KD = ar(o2 + 2048, 1024).rearrange("p (i e) -> p i e", i=8)
    MT = ar(o2 + 3072, 1024).rearrange("p (i t) -> p i t", i=8)
    WSA = ar(o2 + 3072, 512).rearrange("p (g s) -> p g s", g=4)
    WST = ar(o2 + 3584, 512).rearrange("p (g t) -> p g t", g=4)
    o2 += 4096
    EGB = ar(o2 - 4096 + 2048, 1024).rearrange("p (t n) -> p t n", t=2)
    DT = ar(o2, 1024).rearrange("p (i t) -> p i t", i=8)
    o2 += 1024
    WTs = MT
    ST = ar(o2, 512).rearrange("p (h e) -> p h e", h=4)
    o2 += 512
    QKT2 = ar(3600, 4 * S).rearrange("p (b s) -> p b s", b=4)
    L2 = ar(3600 + 1024, 2048).rearrange("p (b m s) -> p b m s", b=2, m=4)
    PT2 = ar(3600 + 3072, 1024).rearrange("p (k m t) -> p k m t", k=2, m=4)
    R2A, R2B = XN[:, 0, 256:768], XN[:, 1, 256:768]
    ALN = sb("ALN", [P, 2, 2, 256])
    hT2h = parts_at("hT2h", arena_base, 0, [P, FT2, S])
    hT2l = parts_at("hT2l", arena_base, FT2 * S, [P, FT2, S])
    HS = ar(2 * FT2 * S, 2 * NTB * CH2).rearrange("p (b t n) -> p b t n", b=2, t=NTB)
    HB2 = ar(2 * FT2 * S + 1024, 2 * NTB * CH2).rearrange("p (b t n) -> p b t n", b=2, t=NTB)
    hEh = parts_at("hEh", arena_base, 0, [P, FT2, P])
    hEl = parts_at("hEl", arena_base, FT2 * P, [P, FT2, P])
    om = 2 * FT2 * P
    Pm = ar(om, NTB * P).rearrange("p (t j) -> p t j", t=NTB)
    PmT = ar(om + 256, NTB * P).rearrange("p (t j) -> p t j", t=NTB)
    ACC = ar(om + 512, NTB * D).rearrange("p (t n) -> p t n", t=NTB)
    YB = ar(om + 2560, D)
    xgTh = parts_at("xgTh", arena_base, om + 3584, [P, KT, P])
    xgTl = parts_at("xgTl", arena_base, 2 * FT2 * S + 2048, [P, KT, P])
    RK = ar(om + 4608, NTB * CT_N).rearrange("p (t e) -> p t e", t=NTB)
    CW = ar(om + 4608 + 64, NTB * CT_N).rearrange("p (t e) -> p t e", t=NTB)
    LG = ar(om + 4608 + 192, NTB * NE).rearrange("p (t e) -> p t e", t=NTB)
    SEL = ar(om + 4608 + 208, NTB * NE).rearrange("p (t e) -> p t e", t=NTB)
    OH = ar(om + 4608 + 224, NTB * NE).rearrange("p (t e) -> p t e", t=NTB)
    TOPV = ar(om + 4608 + 240, NTB * 8).rearrange("p (t e) -> p t e", t=NTB)
    IDXF = ar(om + 4608 + 256, NTB * 8).rearrange("p (t e) -> p t e", t=NTB)
    PR = ar(om + 4608 + 272, NTB * 4).rearrange("p (t e) -> p t e", t=NTB)
    CNT = ar(om + 4608 + 280, 16)

    x_loaded, c_loaded = sig("x_loaded"), sig("tables_loaded")
    rows_loaded = sig("rows_loaded")
    loaded = sig("params_loaded")
    vec_loaded = [sig("vec_loaded0"), sig("vec_loaded1")]
    vec_used = sig("vec_used")
    misc_loaded = sig("misc_loaded")
    misc_used = sig("misc_used")
    w_in_slot = [Signal(ctx.enter_context(nc.semaphore(f"w_in_slot{i}"))) for i in range(R)]
    w_hi, w_lo, w_lo_pool = sig("w_high_part"), sig("w_low_part"), sig("w_low_part_pool")
    w_used = sig("w_used")
    x_full = [sig("x_full0"), sig("x_full1")]
    x_hi = [sig("x_high0"), sig("x_high1")]
    x_taken = [sig("x_taken0"), sig("x_taken1")]
    g_dve, g_act = sig("g_taken_dve"), sig("g_taken_act")
    t_full = [sig("t_full0"), sig("t_full1")]
    t_taken = [sig("t_taken0"), sig("t_taken1")]
    s_ssq, s_rstd, xn_ready = sig("ssq_ready"), sig("rstd_ready"), sig("xn_ready")
    s_ms = sig("ms_ready")
    beta_taken = sig("beta_rows_taken")
    lv_done, pe_own = sig("level_done"), sig("pe_own")
    dstep, astep, pstep = sig("dve_step"), sig("act_step"), sig("pool_step")
    a2d, d2a = sig("act_to_dve"), sig("dve_to_act")
    d2p, p2d = sig("dve_to_pool"), sig("pool_to_dve")
    d2pe = sig("dve_to_pe")
    a2pe = sig("act_to_pe")
    pe2d, pe2a = sig("pe_to_dve"), sig("pe_to_act")
    p2pe = sig("pool_to_pe")
    scores, taken = sig("scores_ready"), sig("scores_taken")
    maxed, probs, comb = sig("max_ready"), sig("probs_ready"), sig("diff_ready")
    pv_done, o_ready = sig("pv_ready"), sig("o_ready")
    idx_s, idx_taken = sig("index_dots"), sig("index_dots_taken")
    silu_ready, hb_ready = sig("silu_ready"), sig("hidden_ready")
    out_done = sig("out_written")
    m_flag, f_out, f_r, f_p = sig("overflow_flag"), sig("result_ready"), sig("final_dve"), sig("final_pool")
    m_chunk, m_silu, m_hb = sig("e_chunk"), sig("e_silu"), sig("e_hidden")
    m_tf, m_tt = [sig("e_t_full0"), sig("e_t_full1")], [sig("e_t_taken0"), sig("e_t_taken1")]
    m_th = [sig("e_t_high0"), sig("e_t_high1")]
    m_p, m_g, m_gd, m_ga = sig("e_slots"), sig("e_gathered"), sig("e_gather_taken_dve"), sig("e_gather_taken_act")
    m_y = sig("e_y_taken")
    m_sc, m_acc = sig("e_scattered"), sig("e_added")


    n_use = {"pe": 0, "dve": 0, "act": 0}
    g_dve_in = []
    vec_free = []
    block = ctx.enter_context(nc.Block())

    def step(eng, ins, s):
        ins.then_inc(s.sem, 1)
        s.made += 1
        eng.wait_ge(s.sem, s.made)

    def uses_cols(W, n0, n1):
        v = W[:, n0:n1].rearrange("(j k p) n -> j p k n", j=2, p=P)
        return [[(v[j], 0, n1 - n0)] for j in range(2)]

    def uses_rows(W, per=2):
        v = W.rearrange("(k p) n -> p k n", p=P)
        n = v.shape[1]
        return [[(v[:, k:k + per], None, per)] for k in range(0, n, per)]

    def uses_pair(Wg, Wu, ch):
        g = Wg[:, ch * CH2:(ch + 1) * CH2].rearrange("(j k p) n -> j p k n", j=2, p=P)
        u = Wu[:, ch * CH2:(ch + 1) * CH2].rearrange("(j k p) n -> j p k n", j=2, p=P)
        return [[(g[j], 0, CH2), (u[j], CH2, CH2)] for j in range(2)]

    def uses_down(Wd):
        v = Wd.rearrange("(k p) n -> p k n", p=P)
        got, k = [], 0
        for m in DOWN2:
            got.append([(v[:, k:k + m], None, m)])
            k += m
        return got

    IN_CHUNKS = [(n, min(n + 512, D_IN)) for n in range(0, D_IN, 512)]
    IN2_CHUNKS = [(0, 512), (512, 1024), (1024, 1536), (1536, 2048), (2048, 2560), (2560, 3072), (3072, D_IN2)]
    SEQ2 = [0, 1, 2, 3, 5, 6, 4]

    TILES = []
    for l in range(DEPTH):
        for n0, n1 in IN_CHUNKS:
            TILES += uses_cols(w["w_in"][l], n0, n1)
        TILES += uses_rows(w["w_out"][l])
        for n0 in range(0, D_FF, 512):
            TILES += uses_cols(w["w_mlp_up"][l], n0, n0 + 512)
        TILES += uses_rows(w["w_mlp_down"][l]) + uses_rows(w["w_ple_gate"][l]) + uses_rows(w["w_ple_proj"][l])
    for l in range(DEPTH):
        for i in SEQ2:
            TILES += uses_cols(w["w_in_2"][l], *IN2_CHUNKS[i])
        TILES += uses_rows(w["w_out_2"][l])
        if l == 0:
            for ch in range(NCH2):
                TILES += uses_pair(w["ffn_w_gate_2"][0], w["ffn_w_up_2"][0], ch)
            TILES += uses_rows(w["ffn_w_down_2"][0])
    U0 = len(TILES)

    def floats_of(use):
        return sum(m * D if c0 is None else 4 * m for _, c0, m in use)

    def e_floats(j):
        return SLOT if j < 2 * NCH2 else DOWN2[j - 2 * NCH2] * D

    def of_dve(m):
        return m * 11 // 32 * 2

    def slot_cols_of(buf, slot, width):
        return buf[:, slot, 0:4 * width].rearrange("p (k n) -> p k n", k=4)

    def slot_rows_of(buf, slot, n):
        return buf[:, slot, 0:n * D].rearrange("p (k n) -> p k n", k=n)

    slot_before = [16 * sum(len(TILES[n]) for n in range(U0) if n % R == q) for q in range(R)]
    slot_turn = [sum((32 if j < 2 * NCH2 else 16) for j in range(USES_E) if (U0 + j) % R == q) for q in range(R)]

    @block.sync
    def _(sp):
        sp.dma_start(C[:, :], const_d).then_inc(c_loaded.sem, 16)
        for n, use in enumerate(TILES):
            if n >= R:
                sp.wait_ge(w_used.sem, n - R + 1)
            width = sum(x[2] for x in use)
            for src, c0, m in use:
                dst = slot_rows_of(ring, n % R, m) if c0 is None else slot_cols_of(ring, n % R, width)[:, :, c0:c0 + m]
                sp.dma_start(dst, src).then_inc(w_in_slot[n % R].sem, 16)
        wg = w["moe_w_gate_2"][0]
        wu = w["moe_w_up_2"][0]
        wd = w["moe_w_down_2"][0]

        def expert(i, e):
            for j in range(USES_E):
                n = U0 + j
                sp.wait_ge(w_used.sem, i * USES_E + (n - R + 1))
                if j < 2 * NCH2:
                    ch, half = j // 2, j % 2
                    rows = slice(half * 512, half * 512 + 512)
                    for wm, c0 in ((wg, 0), (wu, CH2)):
                        src = wm[bass.ds(e, 1), rows, ch * CH2:(ch + 1) * CH2].rearrange("e (k p) n -> p (e k) n", p=P)
                        sp.dma_start(slot_cols_of(ring, n % R, 512)[:, :, c0:c0 + CH2], src).then_inc(w_in_slot[n % R].sem, 16)
                else:
                    k0 = sum(DOWN2[:j - 2 * NCH2])
                    m = DOWN2[j - 2 * NCH2]
                    src = wd[bass.ds(e, 1), k0 * P:(k0 + m) * P, :].rearrange("e (k p) n -> p (e k) n", p=P)
                    sp.dma_start(slot_rows_of(ring, n % R, m), src).then_inc(w_in_slot[n % R].sem, 16)

        with sp.Fori(0, NE) as i:
            expert(i, i)
        sp.wait_ge(m_flag.sem, 1)
        over = sp.value_load(FLAG[0:1, 0:1], min_val=0, max_val=1)
        with sp.If(over > 0):
            with sp.Fori(NE, 2 * NE) as i:
                expert(i, i - NE)
        for tb in range(NTB):
            sp.wait_ge(f_out.sem, tb + 1)
            sp.dma_start(out_d[0, tb * P:(tb + 1) * P, :], XN[:, tb, :]).then_inc(out_done.sem, 16)
        sp.wait_ge(out_done.sem, 16 * NTB)

    ORDER = [0, 2, 1, 3]

    def maps(kind, j=0):
        if kind == "a":
            return [(64 * (h % 2), h // 2, 2 + h // 2, 64, A_V + 64 * h, h) for h in ORDER]
        if kind == "b":
            return [(64 * (h % 2), 9 + h // 2, 11 + h // 2, 64, B_V + 64 * h, h) for h in ORDER]
        if kind == "c":
            return [(32 * i, 13 + j, 15 + j, 32, C_V + 64 * (2 * j + i // 2), i // 2) for i in ORDER]
        if kind == "d":
            return [(64 * (h % 2), 17 + h // 2, 19 + h // 2, 64, D_V + 64 * (h // 2), h) for h in ORDER]
        return [(64 * (h % 2), h // 2, 2 + h // 2, 64, C2 + 512 + 64 * h, h) for h in ORDER]

    UNITS = [(kind, j, tb) for kind, js in (("b", 1), ("c", 2), ("d", 1), ("a", 1)) for j in range(js) for tb in range(NTB)]
    UNITS2 = [("e", 0, tb) for tb in range(NTB)]
    DOTS = [(0, 0, 8), (1, 0, 4), (1, 4, 4)]
    DOT_R = PT.rearrange("p k m t -> p (k m t)")

    def dot_map(buf, tb, h):
        nk = P * (tb + 1)
        return buf[:, (h % 2) * 512 + (h // 2) % (4 // (tb + 1)) * nk:][:, 0:nk]

    O_COL = {"a": 0, "b": 256, "c": 512, "d": 768, "e": 768}
    QK_COLS = [A_Q, A_Q + 128, A_K, A_K + 128, A_IQ, A_IQ + 128, A_IQ + 256, A_IQ + 384, ("twice", A_IK),
               B_Q, B_Q + 128, B_K, B_K + 128, C_Q, C_Q + 128, C_K, C_K + 128, D_Q, D_Q + 128, ("twice", D_K), ("twice", D_K + 64)]

    def g_map(u, nk):
        h = G[:, 2 * (u % 2):2 * (u % 2) + 2, :].rearrange("p b (m s) -> p (b m) s", m=2)
        return h[:, :, 0:nk]

    IN_N = len(IN_CHUNKS)
    G_ACT = IN_N + 8 + 1
    N_LOADED = 16 * 14
    N_ROWS = 16 * 6

    @block.tensor
    def _(pe):
        n_t, n_x = [0, 0], [0, 0]
        t_free = [None, None]
        made = {"dve": 0, "act": 0}
        need = [(0, 0)] * 4

        def weights():
            n = n_use["pe"]
            n_use["pe"] += 1
            pe.wait_ge(w_lo.sem, n + 1)
            pe.wait_ge(w_lo_pool.sem, n + 1)
            return n % H, n % R

        def product(out, ah, al, bh, bl, start, stop, **kw):
            pe.matmul(out, ah, bh, start=start, stop=False, **kw)
            pe.matmul(out, ah, bl, start=False, stop=False, **kw)
            return pe.matmul(out, al, bh, start=False, stop=stop, **kw)

        def banks_free(banks):
            d, a = max(need[b][0] for b in banks), max(need[b][1] for b in banks)
            if d:
                pe.wait_ge(g_dve.sem, d)
            if a:
                pe.wait_ge(g_act.sem, a)

        def chunk_made(banks, by):
            for e in by:
                made[e] += 1
            for b in banks:
                need[b] = (made["dve"], made["act"])

        def bank_free_t(i):
            if t_free[i]:
                pe.wait_ge(t_free[i][0].sem, t_free[i][1])

        def transposes(i, pairs, parts=False):
            bank_free_t(i)
            for dst, src in pairs:
                k = src.shape[0]
                last = pe.transpose(dst, src, ident[0:k, 0:k])
            n = n_x if parts else n_t
            n[i] += 1
            t_free[i] = ((x_taken if parts else t_taken)[i], n[i])
            last.then_inc((x_full if parts else t_full)[i].sem, 1)

        def all_evacuated():
            for i in range(2):
                bank_free_t(i)

        def token_transposes(src, kt_n=KT):
            for b in range(kt_n // 2):
                bank = T[b % 2]
                transposes(b % 2, [(bank[:, k * 256 + tb * P:k * 256 + tb * P + P],
                                    src[:, tb, (2 * b + k) * P:(2 * b + k + 1) * P]) for k in range(2) for tb in range(NTB)], parts=True)

        def chunk_cols(width, banks, by):
            banks_free(banks)
            for j in range(2):
                sh, sl = weights()
                bh, bl = slot_cols_of(ring_hi, sh, width), slot_cols_of(ring_lo, sl, width)
                for k in range(4):
                    for tb in range(NTB):
                        toks = slice(tb * P, (tb + 1) * P)
                        last = product(G[:, banks[tb], 0:width], xTh[:, 4 * j + k, toks], xTl[:, 4 * j + k, toks], bh[:, k, :], bl[:, k, :],
                                       j == 0 and k == 0, j == 1 and k == 3)
                last.then_inc(w_used.sem, 1)
            chunk_made(banks, by)

        def product_rows(ah, al, tiles, by):
            banks_free(range(4))
            n, k0 = sum(tiles), 0
            for m in tiles:
                sh, sl = weights()
                bh, bl = slot_rows_of(ring_hi, sh, m), slot_rows_of(ring_lo, sl, m)
                for k in range(m):
                    for tb in range(NTB):
                        toks = slice(tb * P, (tb + 1) * P)
                        for h in range(2):
                            cs = slice(h * 512, (h + 1) * 512)
                            last = product(G[:, 2 * tb + h, :], ah[:, k0 + k, toks], al[:, k0 + k, toks], bh[:, k, cs], bl[:, k, cs],
                                           k0 + k == 0, k0 + k == n - 1)
                last.then_inc(w_used.sem, 1)
                k0 += m
            chunk_made(range(4), by)

        def units(us, qkt, pt, v_of, nmaps_of):
            def logits(u):
                kind, j, tb = us[u]
                nk = P * (tb + 1)
                if u >= 2:
                    pe.wait_ge(taken.sem, taken.seen["pe0"] + u - 1)
                out = g_map(u, nk)
                mp = maps(kind, j)
                for n, m in enumerate(ORDER):
                    p0, qb, kb, kd = mp[m][:4]
                    if kind == "c" and n == 2:
                        last.then_inc(pe_own.sem, 1)
                        pe_own.made += 1
                        pe.wait_ge(pe_own.sem, pe_own.made)
                    last = pe.matmul(out[:, m, :], qkt[p0:p0 + kd, qb, tb * P:(tb + 1) * P], qkt[p0:p0 + kd, kb, 0:nk],
                                     start=True, stop=True)
                last.then_inc(scores.sem, 1)

            def prob_transposes(u):
                kind, j, tb = us[u]
                n = 2 if kind == "c" else 4
                lbuf = L if us is UNITS else L2
                s = comb if kind == "c" else probs
                pe.wait_ge(s.sem, s.next("pe"))
                if kind == "c":
                    probs.next("pe")
                for kb in range(tb + 1):
                    transposes(kb, [(T[kb][:, m * P:(m + 1) * P], lbuf[:, u % 2, m, kb * P:(kb + 1) * P])
                                    for m in range(n)])

            def values(u, base):
                kind, j, tb = us[u]
                n = 2 if kind == "c" else 4
                all_evacuated()
                if u >= 2:
                    pe.wait_ge(o_ready.sem, base + u - 1)
                mp = maps(kind, j)
                for m in range(n):
                    vcol, head = mp[m][4:]
                    for kb in range(tb + 1):
                        last = pe.matmul(Sp[:, u % 2, head * 64:(head + 1) * 64], pt[:, kb, m, :], v_of(kb, vcol),
                                         start=(kb == 0), stop=(kb == tb))
                last.then_inc(pv_done.sem, 1)

            taken.seen.setdefault("pe0", 0)
            base = o_ready.seen.get("pe", 0)
            logits(0)
            logits(1)
            for u in range(len(us)):
                prob_transposes(u)
                if u + 2 < len(us):
                    logits(u + 2)
                values(u, base)
            taken.seen["pe0"] += len(us)
            o_ready.seen["pe"] = base + len(us)

        pe.wait_ge(c_loaded.sem, 16)
        pe.wait_ge(rows_loaded.sem, N_ROWS)
        transposes(0, [(T[0][:, 0:P], PROWS[:, :]), (T[0][:, P:P + 8], ABS[:, :])])

        for l in range(DEPTH):
            pe.wait_ge(xn_ready.sem, xn_ready.next("pe", 2))
            token_transposes(XN)
            all_evacuated()
            sp2 = Sp[:, :, :].rearrange("p b n -> p (b n)")

            def qk_transposes(blocks):
                for b in blocks:
                    pairs = []
                    for k in range(2 if b < 10 else 1):
                        col = QK_COLS[2 * b + k]
                        for tb in range(NTB):
                            if isinstance(col, tuple):
                                src = IKD[:, {A_IK: 0, D_K: 1, D_K + 64: 2}[col[1]], tb, :]
                            else:
                                src = PROJ[:, tb, col:col + P]
                            pairs.append((T[b % 2][:, k * 256 + tb * P:k * 256 + tb * P + P], src))
                    transposes(b % 2, pairs)

            def index_dots(r):
                tb, h0, n = DOTS[r]
                if r:
                    pe.wait_ge(idx_taken.sem, len(DOTS) * l + r)
                for h in range(h0, h0 + n):
                    p0 = 64 * (h % 2)
                    last = pe.matmul(dot_map(sp2, tb, h), QKT[p0:p0 + 64, 4 + h // 2, tb * P:(tb + 1) * P], QKT[p0:p0 + 64, 8, 0:P * (tb + 1)],
                                     start=True, stop=True)
                last.then_inc(idx_s.sem, 1)

            for i, (n0, n1) in enumerate(IN_CHUNKS):
                b = 2 * (i % 2)
                chunk_cols(n1 - n0, [b, b + 1], ("dve", "act"))
                if i == 3:
                    pe.wait_ge(d2pe.sem, d2pe.next("pe"))
                    qk_transposes(range(5))
                if i == 4:
                    all_evacuated()
                if i >= 4:
                    index_dots(i - 4)
            pe.wait_ge(d2pe.sem, d2pe.next("pe"))
            qk_transposes(range(5, 8))
            banks_free(range(4))
            up = c("upper1")
            pe.matmul(G[:, 0, 0:4], up[:, 0:P], LF[:, 0, :], start=True, stop=True)
            pe.matmul(G[:, 0, 4:8], up[:, P:2 * P], LF[:, 0, :], start=True, stop=False)
            pe.matmul(G[:, 0, 4:8], up[:, 0:P], LF[:, 1, :], start=False, stop=True)
            gb = G[:, 2:4, :].rearrange("p b (m s) -> p (b m) s", m=2)
            for h in range(4):
                pe.matmul(gb[:, h, :], LF[:, 0, h:h + 1].to_broadcast([P, P]), up, start=True, stop=False)
                last = pe.matmul(gb[:, h, P:2 * P], LF[:, 1, h:h + 1].to_broadcast([P, P]), up[:, 0:P], start=False, stop=True)
            last.then_inc(pe2d.sem, 1)
            pe.wait_ge(p2pe.sem, p2pe.next("pe"))
            qk_transposes(range(8, 11))
            all_evacuated()
            pe.wait_ge(d2pe.sem, d2pe.next("pe"))
            pe.wait_ge(idx_taken.sem, len(DOTS) * (l + 1))
            units(UNITS, QKT, PT, lambda kb, vcol: PROJ[:, kb, vcol:vcol + 64], None)
            pe.wait_ge(o_ready.sem, o_ready.seen["pe"])
            token_transposes(XN)
            all_evacuated()
            product_rows(xTh, xTl, [2] * 4, ("dve",))
            pe.wait_ge(xn_ready.sem, xn_ready.next("pe", 2))
            token_transposes(XN)
            all_evacuated()

            def hidden(ch):
                pe.wait_ge(hb_ready.sem, hb_ready.next("pe"))
                for j in range(2):
                    transposes(j, [(T[j][:, k * 256 + tb * P:k * 256 + tb * P + P],
                                    HB[:, ch % 2, tb, (2 * j + k) * P:(2 * j + k + 1) * P]) for k in range(2) for tb in range(NTB)], parts=True)

            for ch in range(8):
                b = 2 * (ch % 2)
                chunk_cols(512, [b, b + 1], ("act",))
                if ch:
                    hidden(ch - 1)
            hidden(7)
            all_evacuated()
            product_rows(hTh, hTl, [2] * 16, ("dve",))
            pe.wait_ge(d2pe.sem, d2pe.next("pe"))
            token_transposes(X)
            pe.wait_ge(misc_loaded.sem, 16 * (l + 1))
            transposes(0, [(T[0][:, k * 256 + tb * P:k * 256 + tb * P + P], PLE[:, tb, k * P:(k + 1) * P])
                           for k in range(2) for tb in range(NTB)], parts=True)
            all_evacuated()
            product_rows(xTh, xTl, [2] * 4, ("act",))
            product_rows(PLETh, PLETl, [2], ("dve",))

        for l in range(DEPTH):
            if l == 0:
                pe.wait_ge(d2pe.sem, d2pe.next("pe"))
            else:
                pe.wait_ge(vec_used.sem, l + 1)
            token_transposes(X)
            all_evacuated()
            ones = c("upper1")[:, P:2 * P]
            for q, i in enumerate(SEQ2):
                n0, n1 = IN2_CHUNKS[i]
                b = 2 * (q % 2)
                if 1 <= i <= 3:
                    banks_free([b, b + 1])
                    out = G[:, b:b + 2, :].rearrange("p b (m s) -> p (b m) s", m=2)
                    for j in range(2):
                        sh, sl = weights()
                        wh, wl = slot_cols_of(ring_hi, sh, 512), slot_cols_of(ring_lo, sl, 512)
                        for m in range(4):
                            ms_ = slice(m * P, (m + 1) * P)
                            for k in range(4):
                                first = j == 0 and k == 0
                                last = product(out[:, m, :], wh[:, k, ms_], wl[:, k, ms_], xTh[:, 4 * j + k, :], xTl[:, 4 * j + k, :],
                                               first and m % 2 == 0, j == 1 and k == 3, skip_group_check=True)
                        last.then_inc(w_used.sem, 1)
                    chunk_made([b, b + 1], ("dve", "act"))
                else:
                    chunk_cols(n1 - n0, [b, b + 1], ("act",) if i in (0, 4) else ("dve", "act"))
                if i == 1:
                    pe.wait_ge(misc_loaded.sem, 16 * (DEPTH + l + 1))
                    transposes(0, [(T[0][:, g * P:(g + 1) * P], WSA[:, g, :]) for g in range(4)])
                if i == 2:
                    bank_free_t(0)
                    for g in range(4):
                        last = pe.matmul(Sp[:, 0, g * P:(g + 1) * P], WST[:, g, :], P2[:, :, A2 + 256 + g * 64:A2 + 256 + (g + 1) * 64],
                                         start=True, stop=True)
                    last.then_inc(pe2d.sem, 1)
                if i in (3, 5):
                    if i == 3:
                        pe.wait_ge(d2pe.sem, d2pe.next("pe"))
                    pe.wait_ge(a2pe.sem, a2pe.next("pe"))
                    for b in range(2):
                        o_ = (b + (2 if i == 5 else 0)) * 512
                        last = pe.matmul(Sp[:, b, :], ones, SQ[:, o_:o_ + 512], start=True, stop=True)
                    last.then_inc(pe2a.sem, 1)
                if i == 6:
                    pe.wait_ge(d2pe.sem, d2pe.next("pe"))
                    bank_free_t(0)
                    for tb in range(NTB):
                        pe.matmul(T[0][:, tb * 4:tb * 4 + 4], c("chunk_upper"), GL[:, tb, :], start=True, stop=True)
                    for tb in range(NTB):
                        last = pe.matmul(T[0][:, 8 + tb * 4:12 + tb * 4], c("chunk_ones"), GL[:, tb, :], start=True, stop=True)
                    n_t[0] += 1
                    t_free[0] = (t_taken[0], n_t[0])
                    last.then_inc(t_full[0].sem, 1)
                    for tb in range(NTB):
                        for h in range(H2):
                            last = pe.matmul(Sp[:, tb, h * P:(h + 1) * P], GL[:, tb, h:h + 1].to_broadcast([P, P]), c("chunk_upper"),
                                             start=True, stop=True)
                    last.then_inc(pe2d.sem, 1)
                    for tb in (1, 0):
                        bank_free_t(tb)
                        for h in range(H2):
                            last = pe.matmul(T[tb][:, h * P:(h + 1) * P], BETA[:, tb, h:h + 1].to_broadcast([P, P]), ident,
                                             start=True, stop=True)
                        t_free[tb] = (beta_taken, l + 1)
                    last.then_inc(pe2d.sem, 1)
            banks_free([2, 3])
            for i in range(8):
                tb, h = i // 4, i % 4
                kT_ = CV[:, 4 + h, tb * P:(tb + 1) * P]
                last = pe.matmul(G[:, 2 + tb, h * P:(h + 1) * P], kT_, kT_, start=True, stop=True)
            last.then_inc(pe2d.sem, 1)
            banks_free([0, 1])
            for i in range(8):
                tb, h = i // 4, i % 4
                last = pe.matmul(G[:, tb, h * P:(h + 1) * P], CV[:, 4 + h, tb * P:(tb + 1) * P], CV[:, h, tb * P:(tb + 1) * P], start=True, stop=True)
            last.then_inc(pe2a.sem, 1)
            for tb in range(NTB):
                if tb == 0:
                    pe.wait_ge(d2pe.sem, d2pe.next("pe"))
                else:
                    pe.wait_ge(lv_done.sem, lv_done.next("pe"))
                transposes(tb, [(T[tb][:, h * P:(h + 1) * P], TT[:, tb * 4 + h, :]) for h in range(H2)])
            lv_done.next("pe", LEVELS - 3)
            all_evacuated()
            pe.wait_ge(a2pe.sem, a2pe.next("pe"))
            for lv in range(1, LEVELS):
                pe.wait_ge(p2pe.sem, p2pe.next("pe"))
                for tb in range(NTB):
                    if lv > 1:
                        pe.wait_ge(d2pe.sem, d2pe.next("pe", 1 + tb))
                    for h in range(H2):
                        last = pe.matmul(G[:, tb, h * P:(h + 1) * P], MLV[lv % 2][:, 4 * tb + h, :], TN[:, 4 * tb + h, :], start=True, stop=True)
                    last.then_inc(pe2a.sem, 1)
                for tb in range(NTB):
                    pe.wait_ge(a2pe.sem, a2pe.next("pe"))
                    if lv > 1 and tb == 1:
                        pe.wait_ge(d2pe.sem, d2pe.next("pe"))
                    for h in range(H2):
                        i, cs = 4 * tb + h, slice(h * P, (h + 1) * P)
                        if lv < LEVELS - 1:
                            pe.matmul(G[:, 2 + tb, cs], TT[:, i, :], WB[:, i, :], start=True, stop=True)
                        last = pe.matmul(Sp[:, tb, cs], WB[:, i, :], TT[:, i, :], start=True, stop=True)
                    last.then_inc(pe2d.sem, 1)
                if lv <= NTB:
                    tb = lv - 1
                    transposes(0, [(T[0][:, h * P:(h + 1) * P], CV[:, 4 + h, tb * P:(tb + 1) * P]) for h in range(H2)])
                    transposes(1, [(T[1][:, h * P:(h + 1) * P], CV[:, 8 + h, tb * P:(tb + 1) * P]) for h in range(H2)])
            pe.wait_ge(d2pe.sem, d2pe.next("pe", 2))
            all_evacuated()
            for i in range(8):
                cs = slice((i % 4) * P, (i % 4 + 1) * P)
                last = pe.matmul(G[:, i // 4, cs], TT[:, i, :], VB[:, i, :], start=True, stop=True)
            last.then_inc(pe2d.sem, 1)
            for i in range(8):
                cs = slice((i % 4) * P, (i % 4 + 1) * P)
                last = pe.matmul(G[:, 2 + i // 4, cs], KBE[:, i, :], TT[:, i, :], start=True, stop=True)
            last.then_inc(pe2a.sem, 1)
            pe.wait_ge(d2pe.sem, d2pe.next("pe"))
            pe.wait_ge(a2pe.sem, a2pe.next("pe"))
            for tb in range(NTB):
                for half in range(2):
                    rows = slice(half * CHUNK, (half + 1) * CHUNK)
                    toks = slice(tb * P + half * CHUNK, tb * P + (half + 1) * CHUNK)
                    for h in range(H2):
                        last = pe.matmul(G[:, 0, h * P:(h + 1) * P], WTs[:, tb * 4 + h, :], ST[:, h, :], start=True, stop=True)
                    last.then_inc(pe2d.sem, 1)
                    for h in range(H2):
                        pe.matmul(Sp[rows, tb, h * P:(h + 1) * P], CV[:, h, toks], ST[:, h, :],
                                  start=(h == 0), stop=False, skip_group_check=True)
                    pe.wait_ge(d2pe.sem, d2pe.next("pe"))
                    if not (tb == 1 and half == 1):
                        for h in range(H2):
                            last = pe.matmul(G[:, 1, h * P:(h + 1) * P], KD[rows, tb * 4 + h, :], DT[rows, tb * 4 + h, :],
                                             start=True, stop=True)
                        last.then_inc(pe2d.sem, 1)
                    if half == 1:
                        for h in range(H2):
                            last = pe.matmul(Sp[:, tb, h * P:(h + 1) * P], AT_[:, tb * 4 + h, :], DT[:, tb * 4 + h, :],
                                             start=False, stop=True, skip_group_check=True)
                        last.then_inc(pe2a.sem, 1)
                    if not (tb == 1 and half == 1):
                        pe.wait_ge(d2pe.sem, d2pe.next("pe"))
            for b in range(2):
                transposes(b, [(T[b][:, k * 256 + tb * P:k * 256 + tb * P + P], P2[:, tb, C2 + (2 * b + k) * P:C2 + (2 * b + k + 1) * P])
                               for k in range(2) for tb in range(NTB)])
            all_evacuated()
            units(UNITS2, QKT2, PT2, lambda kb, vcol: P2[:, kb, vcol:vcol + 64], None)
            pe.wait_ge(o_ready.sem, o_ready.seen["pe"])
            token_transposes(XN)
            all_evacuated()
            product_rows(xTh, xTl, [2] * 4, ("dve",))
            if l == 0:
                pe.wait_ge(d2pe.sem, d2pe.next("pe"))
                token_transposes(X)
                all_evacuated()

                def hidden2(ch):
                    pe.wait_ge(hb_ready.sem, hb_ready.next("pe"))
                    i = ch % 2
                    transposes(i, [(T[i][:, k * 256 + tb * P:k * 256 + tb * P + P], HB2[:, i, tb, k * P:(k + 1) * P])
                                   for k in range(2) for tb in range(NTB)], parts=True)

                for ch in range(NCH2):
                    b = 2 * (ch % 2)
                    chunk_cols(512, [b, b + 1], ())
                    if ch:
                        hidden2(ch - 1)
                hidden2(NCH2 - 1)
                all_evacuated()
                product_rows(hT2h, hT2l, [2] * (FT2 // 2), ("dve",))

        pe.wait_ge(d2pe.sem, d2pe.next("pe"))
        token_transposes(X)
        all_evacuated()
        for tb in range(NTB):
            for k in range(KT):
                toks = slice(tb * P, (tb + 1) * P)
                last = product(Sp[:, 0, tb * 8:tb * 8 + 8], xTh[:, k, toks], xTl[:, k, toks], RWh[:, k, :], RWl[:, k, :], k == 0, k == KT - 1)
        last.then_inc(pe2d.sem, 1)
        pe.wait_ge(d2pe.sem, d2pe.next("pe"))
        ones = c("upper1")[:, P:2 * P]
        pe.matmul(Sp[:, 1, 0:8], c("before"), SEL[:, 0, :], start=True, stop=True)
        pe.matmul(Sp[:, 1, 8:16], ones, SEL[:, 0, :], start=True, stop=False)
        pe.matmul(Sp[:, 1, 8:16], c("before"), SEL[:, 1, :], start=False, stop=True)
        pe.matmul(Sp[:, 1, 16:24], ones, SEL[:, 0, :], start=True, stop=False)
        last = pe.matmul(Sp[:, 1, 16:24], ones, SEL[:, 1, :], start=False, stop=True)
        last.then_inc(pe2d.sem, 1)

        def gather():
            g8 = Sp[:, :, :].rearrange("p b (k j) -> p (b k) j", k=4)
            for k in range(KT):
                for tb in range(NTB):
                    last = pe.matmul(g8[:, k, :], X[:, tb, k * P:(k + 1) * P], Pm[:, tb, :], start=(tb == 0), stop=(tb == 1))
            last.then_inc(m_g.sem, 1)

        def scatter(tb):
            for h in range(2):
                last = pe.matmul(Sp[:, h, :], PmT[:, tb, :], YB[:, h * 512:(h + 1) * 512], start=True, stop=True)
            last.then_inc(m_sc.sem, 1)

        banks_free(range(4))
        pe.wait_ge(m_p.sem, 1)
        gather()
        assert n_use["pe"] == U0

        def expert_pe(i):
            def w_slots(j):
                pe.wait_ge(w_lo.sem, i * USES_E + (U0 + j + 1))
                pe.wait_ge(w_lo_pool.sem, i * USES_E + (U0 + j + 1))
                return (U0 + j) % H, (U0 + j) % R

            def hidden_e(ch):
                pe.wait_ge(m_hb.sem, i * NCH2 + (ch + 1))
                k = ch % 2
                if ch >= 2:
                    pe.wait_ge(m_tt[k].sem, 6 * i + (ch // 2))
                for q in range(2):
                    last = pe.transpose(T[k][:, q * P:(q + 1) * P], HB2[:, k, 0, q * P:(q + 1) * P], ident)
                last.then_inc(m_tf[k].sem, 1)

            pe.wait_ge(m_gd.sem, i + 1)
            for ch in range(NCH2):
                if ch >= 2:
                    pe.wait_ge(m_hb.sem, i * NCH2 + (ch - 1))
                for j in range(2):
                    sh, sl = w_slots(2 * ch + j)
                    bh, bl = slot_cols_of(ring_hi, sh, 512), slot_cols_of(ring_lo, sl, 512)
                    for k in range(4):
                        last = product(G[:, ch % 2, :], xgTh[:, 4 * j + k, :], xgTl[:, 4 * j + k, :], bh[:, k, :], bl[:, k, :],
                                       j == 0 and k == 0, j == 1 and k == 3)
                    last.then_inc(w_used.sem, 1)
                if ch:
                    hidden_e(ch - 1)
                if ch == 1:
                    pe.wait_ge(m_y.sem, i + 1)
                    scatter(0)
                if ch == 4:
                    pe.wait_ge(m_acc.sem, 2 * i + 2)
                    scatter(1)
            hidden_e(NCH2 - 1)
            pe.wait_ge(m_tt[1].sem, 6 * i + 5)
            for tb in range(NTB):
                last = pe.transpose(T[1][:, tb * P:(tb + 1) * P], Pm[:, tb, :], ident)
            last.then_inc(m_tf[1].sem, 1)
            pe.wait_ge(m_tt[0].sem, 6 * i + 6)
            pe.wait_ge(m_tt[1].sem, 6 * i + 5)
            k0 = 0
            for q, m in enumerate(DOWN2):
                sh, sl = w_slots(2 * NCH2 + q)
                bh, bl = slot_rows_of(ring_hi, sh, m), slot_rows_of(ring_lo, sl, m)
                for k in range(m):
                    for h in range(2):
                        cs = slice(h * 512, (h + 1) * 512)
                        last = product(G[:, 2 + h, :], hEh[:, k0 + k, :], hEl[:, k0 + k, :], bh[:, k, cs], bl[:, k, cs],
                                       k0 + k == 0, k0 + k == FT2 - 1)
                last.then_inc(w_used.sem, 1)
                k0 += m
                if q == GATHER_AT:
                    pe.wait_ge(m_acc.sem, 2 * i + 3)
                    pe.wait_ge(m_p.sem, i + 2)
                    gather()
            pe.wait_ge(m_tt[1].sem, 6 * i + 6)

        with pe.Fori(0, NE) as i:
            expert_pe(i)
        pe.wait_ge(m_flag.sem, 1)
        over = pe.value_load(FLAG[0:1, 0:1], min_val=0, max_val=1)
        with pe.If(over > 0):
            with pe.Fori(NE, 2 * NE) as i:
                expert_pe(i)
        n_all = pe.value_load(FLAG[0:1, 1:2], min_val=NE, max_val=2 * NE)
        for tb in range(NTB):
            if tb == 0:
                pe.wait_ge(m_y.sem, n_all + 1)
                pe.wait_ge(m_gd.sem, n_all + 1)
                pe.wait_ge(m_tt[1].sem, n_all * 6)
            pe.wait_ge(m_acc.sem, n_all * 2 + (1 + tb))
            scatter(tb)

    @block.scalar
    def _(act):
        n_t, n_x = [0], [0, 0]
        slot_count = [0] * R
        n_hi = [0]

        def high_parts(upto):
            while n_hi[0] < min(upto, U0):
                n = n_hi[0]
                n_hi[0] += 1
                m = floats_of(TILES[n])
                slot_count[n % R] += 16 * len(TILES[n])
                act.wait_ge(w_in_slot[n % R].sem, slot_count[n % R])
                if n >= H:
                    act.wait_ge(w_used.sem, n - H + 1)
                nc.scalar.activation(ring_hi[:, n % H, 0:m], ring[:, n % R, 0:m], ACT.Copy).then_inc(w_hi.sem, 1)

        def met(n):
            n_use["act"] += n
            high_parts(n_use["act"] + H - 1)

        def full(n):
            met(n)
            act.wait_ge(w_used.sem, n_use["act"])

        def evac(dst):
            n_t[0] += 1
            act.wait_ge(t_full[1].sem, n_t[0])
            n = dst.free_size()
            nc.scalar.activation(dst, T[1][:, 0:n].rearrange("p (k s) -> p k s", k=dst.shape[1]), ACT.Copy).then_inc(t_taken[1].sem, 1)

        def high_evac(i, dst, gains=None):
            n_x[i] += 1
            act.wait_ge(x_full[i].sem, n_x[i])
            if gains is None:
                last = nc.scalar.activation(dst, T[i][:, 0:2 * S].rearrange("p (k s) -> p k s", k=2), ACT.Copy)
            else:
                for k in range(2):
                    last = nc.scalar.activation(dst[:, k, :], T[i][:, k * S:(k + 1) * S], ACT.Copy, scale=gains[:, k:k + 1])
            last.then_inc(x_hi[i].sem, 1)

        def token_evac(gains=None):
            for b in range(KT // 2):
                high_evac(b % 2, xTh[:, 2 * b:2 * b + 2, :], None if gains is None else gains[:, 2 * b:2 * b + 2])

        def square_sums(src, junk):
            for tb in range(NTB):
                nc.scalar.activation(junk[:, tb, :], src(tb), ACT.Square, accum_out=ssq[:, tb:tb + 1]).then_inc(s_ssq.sem, 1)

        def units(us, lbuf, pt):
            def exps(u):
                kind, j, tb = us[u]
                nk = P * (tb + 1)
                act.wait_ge(maxed.sem, maxed.next("act"))
                if kind == "d":
                    nc.scalar.activation(esk[:, u % 2, :], esk[:, u % 2, :], ACT.Exp)
                for m in range(4):
                    last = nc.scalar.activation(lbuf[:, u % 2, m, 0:nk], lbuf[:, u % 2, m, 0:nk], ACT.Exp,
                                                bias=nmx[:, u % 2, m:m + 1], accum_out=rsum[:, u % 2, m:m + 1])
                last.then_inc(probs.sem, 1)

            exps(0)
            exps(1)
            for u in range(len(us)):
                if us[u][2] == 1:
                    evac(pt[:, 1, 0:2 if us[u][0] == "c" else 4, :])
                if u + 2 < len(us):
                    exps(u + 2)

        act.dma_start(X[:, :, :], w["x"][0].rearrange("(t p) d -> p t d", p=P)).then_inc(x_loaded.sem, 16)
        for l in range(DEPTH):
            act.dma_start(PROWS[l * 16:l * 16 + 8, :], w["norm_pre_mix"][l].rearrange("(k p) -> k p", p=P)).then_inc(rows_loaded.sem, 16)
            act.dma_start(PROWS[l * 16 + 8:l * 16 + 16, :], w["norm_pre_mlp"][l].rearrange("(k p) -> k p", p=P)).then_inc(rows_loaded.sem, 16)
        act.dma_start(PROWS[32:128, :], w["conv_w_2"].rearrange("l j (b p) -> (l j b) p", p=P)).then_inc(rows_loaded.sem, 16)
        act.dma_start(ABS[:, :], w["a_bs_2"].rearrange("l g t -> (l g) t")).then_inc(rows_loaded.sem, 16)
        for l in range(DEPTH):
            if l:
                act.wait_ge(d2a.sem, d2a.next("act"))
            else:
                act.wait_ge(x_loaded.sem, 16)
            square_sums(lambda tb: X[:, tb, :], XN)
            token_evac(COLS[:, l * 16:l * 16 + 8])
            if l == 0:
                high_parts(H)
                act.wait_ge(d2a.sem, d2a.next("act"))
                nc.scalar.activation(lamt, lamt, ACT.Exp)
                nc.scalar.activation(SN[:, :, :], KK_[:, :, :], ACT.Sin)
                nc.scalar.activation(SH[:, :, :], KK_[:, :, :], ACT.Sin, scale=0.5).then_inc(a2d.sem, 1)
            for i, (n0, n1) in enumerate(IN_CHUNKS):
                full(2)
                nc.scalar.activation(PROJ[:, 1, n0:n1], G[:, 2 * (i % 2) + 1, 0:n1 - n0], ACT.Copy).then_inc(g_act.sem, 1)
                if i == 3:
                    for b in (1, 3):
                        evac(QKT[:, 2 * b:2 * b + 2, :])
                if i == 5:
                    act.wait_ge(d2a.sem, d2a.next("act"))
                    step(act, nc.scalar.activation(GL[:, :, :], GL[:, :, :], ACT.Abs), astep)
                    step(act, nc.scalar.activation(GL[:, :, :], GL[:, :, :], ACT.Exp, scale=-1.0), astep)
                    nc.scalar.activation(GL[:, :, :], GL[:, :, :], ACT.Ln, bias=c("one")).then_inc(a2d.sem, 1)
                if i >= 4:
                    act.wait_ge(idx_s.sem, idx_s.next("act"))
                    if i > 4:
                        act.wait_ge(d2a.sem, d2a.next("act"))
                    nc.scalar.activation(DOT_R, Sp[:, :, :].rearrange("p b n -> p (b n)"), ACT.Relu).then_inc(idx_taken.sem, 1)
            for b in (5, 7, 9):
                evac(QKT[:, 2 * b:2 * b + 2, :])
            units(UNITS, L, PT)
            token_evac()
            full(4)
            square_sums(lambda tb: G[:, 2 * tb:2 * tb + 2, :].rearrange("p b n -> p (b n)"), XN)
            act.wait_ge(d2a.sem, d2a.next("act"))
            square_sums(lambda tb: X[:, tb, :], XN)
            token_evac(COLS[:, l * 16 + 8:l * 16 + 16])
            for ch in range(9):
                if ch < 8:
                    full(2)
                    b = 2 * (ch % 2)
                    nc.scalar.activation(HB[:, ch % 2, :, :], G[:, b:b + 2, :], ACT.Relu).then_inc(g_act.sem, 1)
                if ch:
                    for j in range(2):
                        high_evac(j, hTh[:, 4 * ch - 4 + 2 * j:4 * ch - 2 + 2 * j, :])
            full(16)
            square_sums(lambda tb: G[:, 2 * tb:2 * tb + 2, :].rearrange("p b n -> p (b n)"), XN)
            token_evac()
            high_evac(0, PLETh[:, :, :])
            full(4)
            for tb in range(NTB):
                last = nc.scalar.activation(XN[:, tb, :], G[:, 2 * tb:2 * tb + 2, :].rearrange("p b n -> p (b n)"), ACT.Sigmoid)
            last.then_inc(g_act.sem, 1)
            met(1)

        for l in range(DEPTH):
            token_evac()
            def norms(o_):
                act.wait_ge(pe2a.sem, pe2a.next("act"))
                sq = SQ[:, o_:o_ + 1024]
                step(act, nc.scalar.activation(sq, Sp[:, :, :].rearrange("p b n -> p (b n)"), ACT.Ln, bias=c("eps")), astep)
                nc.scalar.activation(sq, sq, ACT.Exp, scale=-0.5).then_inc(a2d.sem, 1)

            def conv_silu(g):
                act.wait_ge(d2a.sem, d2a.next("act"))
                cv = CV[:, 4 * g:4 * g + 4, :]
                step(act, nc.scalar.activation(cv, cv, ACT.Silu), astep)
                if g < 2:
                    nc.scalar.activation(SQ[:, 1024 * g:1024 * (g + 1)], cv.rearrange("p b s -> p (b s)"), ACT.Square).then_inc(a2pe.sem, 1)

            for q, i in enumerate(SEQ2):
                n0, n1 = IN2_CHUNKS[i]
                b = 2 * (q % 2)
                full(2)
                if i in (0, 4):
                    for tb in range(NTB):
                        o_ = A2 if i == 0 else Z2
                        last = nc.scalar.activation(P2[:, tb, o_:o_ + 512], G[:, b + tb, :], ACT.Gelu_apprx_tanh if i == 0 else ACT.Silu)
                    last.then_inc(g_act.sem, 1)
                elif i <= 3:
                    nc.scalar.activation(PAD[:, 4 * (i - 1) + 2:4 * i, 3:], G[:, b + 1, :].rearrange("p (m s) -> p m s", m=2), ACT.Copy).then_inc(g_act.sem, 1)
                else:
                    o_ = BA2 + (n0 - 2560)
                    nc.scalar.activation(P2[:, 1, o_:o_ + n1 - n0], G[:, b + 1, 0:n1 - n0], ACT.Copy).then_inc(g_act.sem, 1)
                if i == 2:
                    conv_silu(0)
                if i == 3:
                    norms(0)
                    conv_silu(1)
                if i == 5:
                    norms(1024)
                    act.wait_ge(d2a.sem, d2a.next("act"))
                    nc.scalar.activation(BETA[:, :, :], P2[:, :, BA2:BA2 + 4], ACT.Sigmoid)
                    step(act, nc.scalar.activation(GL[:, :, :], GL[:, :, :], ACT.Abs), astep)
                    step(act, nc.scalar.activation(GL[:, :, :], GL[:, :, :], ACT.Exp, scale=-1.0), astep)
                    nc.scalar.activation(ea4, p_alog[:, 4 * l:4 * l + 4], ACT.Exp)
                    nc.scalar.activation(GL[:, :, :], GL[:, :, :], ACT.Ln, bias=c("one")).then_inc(a2d.sem, 1)
                if i == 6:
                    conv_silu(2)
                    act.wait_ge(d2a.sem, d2a.next("act"))
                    nc.scalar.activation(kds8, ms8, ACT.Exp)
                    nc.scalar.activation(eg8, gc16[:, 0:8], ACT.Exp)
                    for half in range(2):
                        nc.scalar.activation(EGL[:, :, :, half], Sp[:, :, :].rearrange("p t (h s) -> p t h s", h=4)[:, :, :, half * CHUNK + CHUNK - 1], ACT.Exp)
                    nc.scalar.activation(EGB[:, :, :], Sp[:, :, :], ACT.Exp)
                    nc.scalar.activation(DT, DT, ACT.Exp).then_inc(a2d.sem, 1)
            act.wait_ge(pe2a.sem, pe2a.next("act"))
            nc.scalar.activation(AT_[:, :, :], G[:, 0:2, :].rearrange("p b (i t) -> p (b i) t", i=4), ACT.Copy).then_inc(a2pe.sem, 1)
            evac(TN[:, 4:8, :])
            for lv in range(1, LEVELS):
                for tb in range(NTB):
                    act.wait_ge(pe2a.sem, pe2a.next("act"))
                    nc.scalar.activation(WB[:, 4 * tb:4 * tb + 4, :], G[:, tb, :].rearrange("p (i t) -> p i t", i=4), ACT.Copy).then_inc(a2pe.sem, 1)
                if lv <= NTB:
                    tb = lv - 1
                    n_t[0] += 1
                    act.wait_ge(t_full[1].sem, n_t[0])
                    for h in range(H2):
                        last = nc.scalar.activation(VB[:, tb * 4 + h, :], T[1][:, h * P:(h + 1) * P], ACT.Copy, scale=BETA[:, tb, h:h + 1])
                    last.then_inc(t_taken[1].sem, 1)
            act.wait_ge(pe2a.sem, pe2a.next("act"))
            nc.scalar.activation(WTs[:, :, :], G[:, 2:4, :].rearrange("p b (i t) -> p (b i) t", i=4), ACT.Copy).then_inc(a2pe.sem, 1)
            for tb in range(NTB):
                act.wait_ge(pe2a.sem, pe2a.next("act"))
                nc.scalar.activation(SQ[:, tb * 512:(tb + 1) * 512], Sp[:, tb, :], ACT.Square).then_inc(a2d.sem, 1)
            evac(QKT2[:, 2:4, :])
            units(UNITS2, L2, PT2)
            token_evac()
            met(4)
            if l == 0:
                token_evac()
                for ch in range(NCH2 + 1):
                    if ch < NCH2:
                        full(2)
                        if ch >= 2:
                            act.wait_ge(hb_ready.sem, 8 * DEPTH + ch - 1)
                        b = 2 * (ch % 2)
                        nc.scalar.activation(HS[:, ch % 2, :, :], G[:, b:b + 2, 0:CH2], ACT.Silu).then_inc(silu_ready.sem, 1)
                    if ch:
                        high_evac((ch - 1) % 2, hT2h[:, 2 * ch - 2:2 * ch, :])
                met(FT2 // 2)

        act.wait_ge(loaded.sem, N_LOADED)
        nc.scalar.activation(RWh[:, :, :], RW[:, :, :], ACT.Copy).then_inc(a2d.sem, 1)
        token_evac()
        act.wait_ge(d2a.sem, d2a.next("act"))
        nc.scalar.activation(PR[:, :, 0:1], PR[:, :, 0:1], ACT.Exp).then_inc(a2d.sem, 1)

        def gather_act(i):
            act.wait_ge(m_g.sem, i + 1)
            nc.scalar.activation(xgTh[:, :, :], Sp[:, :, :].rearrange("p b (k j) -> p (b k) j", k=4), ACT.Copy).then_inc(m_ga.sem, 1)

        gather_act(0)

        def result(n):
            act.wait_ge(w_used.sem, n * USES_E + U0)
            nc.scalar.activation(YB, G[:, 2:4, :].rearrange("p b n -> p (b n)"), ACT.Copy).then_inc(m_y.sem, 1)

        def expert_act(i):
            n_met = [0] * R

            def high_part(j):
                q, m = (U0 + j) % R, e_floats(j)
                n_met[q] += 32 if j < 2 * NCH2 else 16
                act.wait_ge(w_in_slot[q].sem, i * slot_turn[q] + (slot_before[q] + n_met[q]))
                act.wait_ge(w_used.sem, i * USES_E + (U0 + j - H + 1))
                nc.scalar.activation(ring_hi[:, (U0 + j) % H, 0:m], ring[:, q, 0:m], ACT.Copy).then_inc(w_hi.sem, 1)

            def hidden_e(ch):
                k = ch % 2
                act.wait_ge(m_tf[k].sem, 6 * i + (ch // 2 + 1))
                nc.scalar.activation(hEh[:, 2 * ch:2 * ch + 2, :], T[k][:, 0:2 * P].rearrange("p (k j) -> p k j", k=2), ACT.Copy).then_inc(m_th[k].sem, 1)

            for j in range(H - 1):
                high_part(j)
            result(i)
            for ch in range(NCH2):
                for j in range(2):
                    high_part(2 * ch + H - 1 + j)
                act.wait_ge(w_used.sem, i * USES_E + (U0 + 2 * ch + 2))
                if ch >= 2:
                    act.wait_ge(m_hb.sem, i * NCH2 + (ch - 1))
                nc.scalar.activation(HS[:, ch % 2, 0, :], G[:, ch % 2, 0:CH2], ACT.Silu).then_inc(m_silu.sem, 1)
                if ch:
                    hidden_e(ch - 1)
            hidden_e(NCH2 - 1)
            act.wait_ge(m_tf[1].sem, 6 * i + 6)
            nc.scalar.activation(PmT[:, :, :], T[1][:, 0:2 * P].rearrange("p (t j) -> p t j", t=2), ACT.Copy).then_inc(m_tt[1].sem, 1)
            for q in range(H - 1, len(DOWN2)):
                high_part(2 * NCH2 + q)
                if q == GATHER_AT + H - 1:
                    gather_act(i + 1)

        with act.Fori(0, NE) as i:
            expert_act(i)
        act.wait_ge(m_flag.sem, 1)
        over = act.value_load(FLAG[0:1, 0:1], min_val=0, max_val=1)
        with act.If(over > 0):
            with act.Fori(NE, 2 * NE) as i:
                expert_act(i)
        n_all = act.value_load(FLAG[0:1, 1:2], min_val=NE, max_val=2 * NE)
        result(n_all)

    TWO_PI = 2 * math.pi
    PI_A = float(np.float32(6.28125))
    PI_B = float(np.float32(TWO_PI - PI_A))
    PI_C = float(np.float32(TWO_PI - PI_A - np.float64(np.float32(TWO_PI - PI_A))))
    PI_MAX = 3.1415925
    ROUND = 12582912.0

    @block.vector
    def _(dve):
        v = nc.vector
        n_t, n_x = [0], [0, 0]
        n_lo = [0]

        def do(ins, s=None):
            step(dve, ins, s or dstep)

        def low_parts(upto):
            while n_lo[0] < min(upto, U0):
                n = n_lo[0]
                n_lo[0] += 1
                m = floats_of(TILES[n])
                dve.wait_ge(w_hi.sem, n + 1)
                cs = slice(0, of_dve(m))
                v.tensor_tensor(ring_lo[:, n % R, cs], ring[:, n % R, cs], ring_hi[:, n % H, cs].bitcast(F32), ALU.subtract).then_inc(w_lo.sem, 1)

        def met(n):
            n_use["dve"] += n
            low_parts(n_use["dve"] + H - 1)

        def full(n):
            met(n)
            dve.wait_ge(w_used.sem, n_use["dve"])

        def low_evac(i, dst, high, gains=None):
            n_x[i] += 1
            dve.wait_ge(x_hi[i].sem, n_x[i])
            if gains is None:
                last = v.tensor_tensor(dst, T[i][:, 0:2 * S].rearrange("p (k s) -> p k s", k=2), high.bitcast(F32), ALU.subtract)
            else:
                for k in range(2):
                    last = v.scalar_tensor_tensor(dst[:, k, :], T[i][:, k * S:(k + 1) * S], gains[:, k:k + 1], high[:, k, :].bitcast(F32), ALU.mult, ALU.subtract)
            last.then_inc(x_taken[i].sem, 1)

        def t0():
            n_t[0] += 1
            dve.wait_ge(t_full[0].sem, n_t[0])

        def evac(dst):
            t0()
            n = dst.free_size()
            do(v.tensor_copy(dst, T[0][:, 0:n].rearrange("p (k s) -> p k s", k=dst.shape[1])), t_taken[0])

        def token_evac(gains=None):
            for b in range(KT // 2):
                ks = slice(2 * b, 2 * b + 2)
                low_evac(b % 2, xTl[:, ks, :], xTh[:, ks, :], None if gains is None else gains[:, ks])

        def rope(x, cos, sin, heads, width, ra, rb):
            xv = x.rearrange("p (h d) -> p h d", h=heads)
            n = heads * width
            a, b = ra[:, 0:n].rearrange("p (h d) -> p h d", h=heads), rb[:, 0:n].rearrange("p (h d) -> p h d", h=heads)
            hw = width // 2
            do(v.tensor_tensor(a, xv, cos.unsqueeze(1).to_broadcast([P, heads, width]), ALU.mult))
            do(v.tensor_tensor(b[:, :, 0:hw], xv[:, :, hw:], sin[:, 0:hw].unsqueeze(1).to_broadcast([P, heads, hw]), ALU.mult))
            do(v.tensor_tensor(b[:, :, hw:], xv[:, :, 0:hw], sin[:, hw:].unsqueeze(1).to_broadcast([P, heads, hw]), ALU.mult))
            return v.tensor_tensor(xv, a, b, ALU.add)

        def g_tokens(tb):
            return G[:, 2 * tb:2 * tb + 2, :].rearrange("p b n -> p (b n)")

        def normed_to_x(gain, s):
            dve.wait_ge(s_rstd.sem, s_rstd.next("dve"))
            for tb in range(NTB):
                do(v.scalar_tensor_tensor(XN[:, tb, :], g_tokens(tb), rstd[:, tb:tb + 1], gain, ALU.mult, ALU.mult), g_dve if tb else None)
            do(v.tensor_tensor(X[:, :, :], X[:, :, :], XN[:, :, :], ALU.add), s)

        def pre_norm():
            dve.wait_ge(s_rstd.sem, s_rstd.next("dve"))
            for tb in range(NTB):
                do(v.tensor_scalar(XN[:, tb, :], X[:, tb, :], rstd[:, tb:tb + 1], None, ALU.mult), xn_ready)

        def units(us, lbuf, pt, nm_of, scale_of, nlam, between=None):
            def masked(u):
                kind, j, tb = us[u]
                nk = P * (tb + 1)
                li = u % 2
                dve.wait_ge(scores.sem, scores.next("dve"))
                do(v.scalar_tensor_tensor(lbuf[:, li, :, 0:nk], g_map(u, nk), scale_of(kind), nm_of(kind, tb), ALU.mult, ALU.subtract), taken)
                if kind == "d":
                    do(v.tensor_reduce(nmx[:, li, :], lbuf[:, li, :, 0:nk], AX_X, ALU.max, negate=True))
                    do(v.tensor_tensor(nmx[:, li, :], nmx[:, li, :], nsink, ALU.min))
                    do(v.tensor_tensor(esk[:, li, :], nmx[:, li, :], nsink, ALU.subtract), maxed)
                else:
                    do(v.tensor_reduce(nmx[:, li, :], lbuf[:, li, :, 0:nk], AX_X, ALU.max, negate=True), maxed)

            def weigh(u):
                kind, j, tb = us[u]
                nk = P * (tb + 1)
                li = u % 2
                dve.wait_ge(probs.sem, probs.next("dve"))
                if kind == "d":
                    do(v.tensor_tensor(rsum[:, li, :], rsum[:, li, :], esk[:, li, :], ALU.add))
                do(v.reciprocal(rinv[:, li, :] if kind == "c" else rinv[:, li, :].rearrange("p (j i) -> p i j", i=2),
                                rsum[:, li, :] if kind == "c" else rsum[:, li, :].rearrange("p (i j) -> p i j", i=2)))
                if kind == "c":
                    for q in range(2):
                        do(v.tensor_scalar(lbuf[:, li, 2 + q, 0:nk], lbuf[:, li, 2 + q, 0:nk], rinv[:, li, 2 + q:3 + q], nlam, ALU.mult, ALU.mult))
                        do(v.scalar_tensor_tensor(lbuf[:, li, q, 0:nk], lbuf[:, li, q, 0:nk], rinv[:, li, q:q + 1],
                                                  lbuf[:, li, 2 + q, 0:nk], ALU.mult, ALU.add), comb if q else None)

            def out(u):
                kind, j, tb = us[u]
                li = u % 2
                n = 2 if kind == "c" else 4
                dve.wait_ge(pv_done.sem, pv_done.next("dve"))
                o0 = O_COL[kind] + 128 * j
                dst = XN[:, tb, o0:o0 + 64 * n].rearrange("p (m d) -> p m d", m=n)
                src = Sp[:, u % 2, 0:64 * n].rearrange("p (m d) -> p m d", m=n)
                if kind == "c":
                    do(v.tensor_copy(dst, src), o_ready)
                else:
                    do(v.tensor_tensor(dst, src, rinv[:, li, :].unsqueeze(2).to_broadcast([P, 4, 64]), ALU.mult), o_ready)

            masked(0)
            masked(1)
            weigh(0)
            for u in range(len(us)):
                evac(pt[:, 0, 0:2 if us[u][0] == "c" else 4, :])
                if u + 2 < len(us):
                    masked(u + 2)
                if u + 1 < len(us):
                    weigh(u + 1)
                if between:
                    between(u)
                out(u)

        dve.wait_ge(c_loaded.sem, 16)
        t0()
        do(v.tensor_copy(COLS[:, :], T[0][:, 0:P + 8]), t_taken[0])

        def first_tables():
            dve.wait_ge(loaded.sem, N_LOADED)
            do(v.tensor_copy(posf, POS[:, :]))
            for tb in range(NTB):
                do(v.tensor_scalar(ANG[:, tb, :], c("inv_freq"), posf[:, tb:tb + 1], None, ALU.mult))
            do(v.tensor_scalar(KK_, ANG, 1.0 / TWO_PI, ROUND, ALU.mult, ALU.add))
            do(v.tensor_scalar(KK_, KK_, ROUND, None, ALU.subtract))
            do(v.scalar_tensor_tensor(ANG, KK_, -PI_A, ANG, ALU.mult, ALU.add))
            do(v.scalar_tensor_tensor(ANG, KK_, -PI_B, ANG, ALU.mult, ALU.add))
            do(v.scalar_tensor_tensor(ANG, KK_, -PI_C, ANG, ALU.mult, ALU.add))
            do(v.tensor_scalar(KK_, ANG, PI_MAX, -PI_MAX, ALU.min, ALU.max))
            for q in range(2):
                do(v.tensor_tensor(p_lam[:, 2 * q], p_lam[:, 2 * q], p_lam[:, 2 * q + 1], ALU.mult))
            do(v.tensor_reduce(lamt[:, 0:2], p_lam[:, 0], AX_X, ALU.add))
            do(v.tensor_reduce(lamt[:, 2:4], p_lam[:, 2], AX_X, ALU.add), d2a)
            dve.wait_ge(a2d.sem, a2d.next("dve"))
            do(v.tensor_tensor(SH, SH, SH, ALU.mult))
            do(v.tensor_scalar(SH, SH, -2.0, 1.0, ALU.mult, ALU.add))
            for k in range(2):
                do(v.tensor_copy(RCOS[:, :, 32 * k:32 * k + 32], SH[:, :, 0:32]))
                do(v.tensor_copy(RCOS32[:, :, 16 * k:16 * k + 16], SH[:, :, 32:48]))
                do(v.tensor_scalar(RSIN[:, :, 32 * k:32 * k + 32], SN[:, :, 0:32], 1.0 if k else -1.0, None, ALU.mult))
                do(v.tensor_scalar(RSIN32[:, :, 16 * k:16 * k + 16], SN[:, :, 32:48], 1.0 if k else -1.0, None, ALU.mult))
            do(v.tensor_tensor(lamt[:, 0:2], lamt[:, 2:4], lamt[:, 0:2], ALU.subtract))
            for l in range(DEPTH):
                lam0 = 0.8 - 0.6 * math.exp(-0.3 * l)
                do(v.tensor_scalar(lamt[:, l:l + 1], lamt[:, l:l + 1], lam0, None, ALU.subtract))
                do(v.tensor_scalar(p_sub[:, l, :], p_sub[:, l, :], 1.0 - lam0, None, ALU.mult))
            do(v.tensor_scalar(p_sink, p_sink, -1.0, None, ALU.mult))

        for l in range(DEPTH):
            lsl = slice(4 * l, 4 * l + 4)
            pre_norm()
            token_evac(COLS[:, l * 16:l * 16 + 8])
            if l == 0:
                low_parts(H)
                first_tables()
            def rotate(col, heads, width):
                cos, sin = (RCOS32, RSIN32) if width == 32 else (RCOS, RSIN)
                for tb in range(NTB):
                    do(rope(PROJ[:, tb, col:col + heads * width], cos[:, tb, :], sin[:, tb, :], heads, width, ROPE_A, ROPE_B))

            def add_dots(r, s=None):
                tb, h0, n = DOTS[r]
                sc = NMA[:, tb, 0:P * (tb + 1)]
                dve.wait_ge(idx_taken.sem, len(DOTS) * l + r + 1)
                for h in range(h0, h0 + n):
                    d = dot_map(DOT_R, tb, h)
                    if h == 0:
                        do(v.tensor_scalar(sc, d, iws[:, tb, 0:1], None, ALU.mult))
                    else:
                        do(v.scalar_tensor_tensor(sc, d, iws[:, tb, h:h + 1], sc, ALU.mult, ALU.add), s if h == h0 + n - 1 else None)

            for i, (n0, n1) in enumerate(IN_CHUNKS):
                full(2)
                do(v.tensor_copy(PROJ[:, 0, n0:n1], G[:, 2 * (i % 2), 0:n1 - n0]), g_dve)
                dve.wait_ge(g_act.sem, l * G_ACT + i + 1)
                if i == 0:
                    rotate(A_Q, 8, 64)
                if i == 2:
                    rotate(A_IQ, 9, 64)
                    do(v.tensor_scalar(iws, PROJ[:, :, A_IW:A_IW + 8], IDX_HEADS ** -0.5 * HD ** -0.5, None, ALU.mult))
                    for tb in range(NTB):
                        do(v.tensor_copy(IKD[:, 0, tb, :].rearrange("p (r d) -> p r d", r=2),
                                         PROJ[:, tb, A_IK:A_IK + 64].unsqueeze(1).to_broadcast([P, 2, 64])), d2pe if tb else None)
                if i == 3:
                    for b in (0, 2, 4):
                        evac(QKT[:, 2 * b:2 * b + 2, :])
                if i == 4:
                    do(v.tensor_tensor(LF[:, :, :], PROJ[:, :, B_F:B_F + 4], p_bf[:, lsl].unsqueeze(1).to_broadcast([P, NTB, 4]), ALU.add))
                    do(v.tensor_copy(GL[:, :, :], LF[:, :, :]), d2a)
                if i == 5:
                    rotate(C_Q, 16, 32)
                    add_dots(0, d2a)
            g_dve_in.append(g_dve.made)
            dve.wait_ge(a2d.sem, a2d.next("dve"))
            do(v.scalar_tensor_tensor(LF[:, :, :], LF[:, :, :], 0.0, GL[:, :, :], ALU.min, ALU.subtract), d2pe)
            add_dots(1, d2a)
            evac(QKT[:, 12:14, :])
            dve.wait_ge(pe2d.sem, pe2d.next("dve"))
            do(v.tensor_copy(cums.rearrange("p t h -> p (t h)"), G[:, 0, 0:8]))
            gb = G[:, 2:4, :].rearrange("p b (m s) -> p (b m) s", m=2)
            for h in range(4):
                do(v.scalar_tensor_tensor(NMB0[:, ORDER[h], :], gb[:, h, 0:P], cums[:, 0, h:h + 1], c("nm")[:, P:2 * P], ALU.subtract, ALU.add))
                do(v.scalar_tensor_tensor(NMB1[:, ORDER[h], :], gb[:, h, :], cums[:, 1, h:h + 1], c("nm"), ALU.subtract, ALU.add), d2pe if h == 3 else None)
            for b in (8, 10):
                evac(QKT[:, 2 * b:min(2 * b + 2, 21), :])
            add_dots(2)
            do(v.tensor_copy(nsink.rearrange("p (i j) -> p i j", i=2), p_sink[:, lsl].rearrange("p (j i) -> p i j", i=2)))

            def choose(tb, first, last):
                nk = P * (tb + 1)
                sc = NMA[:, tb, 0:nk]
                nm = c("nm")[:, 2 * P - nk:2 * P]
                n = TOPK // 8
                if first == 0:
                    do(v.tensor_tensor(sc, sc, nm, ALU.subtract))
                for _ in range(first, last):
                    do(v.max(top8, sc))
                    do(v.match_replace(sc, top8, sc, TAKEN))
                if last == n:
                    do(v.tensor_scalar(sc, sc, TAKEN, BIG, ALU.not_equal, ALU.mult))
                    do(v.tensor_tensor(sc, sc, nm, ALU.add))

            def between(u):
                n = TOPK // 8
                if u < 2:
                    choose(0, u * n // 2, (u + 1) * n // 2)
                elif u < 6:
                    choose(1, (u - 2) * n // 4, (u - 1) * n // 4)
                elif u == 6:
                    sq = AT_[:, 0:4, :].rearrange("p (t i) n -> p t (i n)", t=2)
                    oc = XN[:, :, 512:768]
                    do(v.tensor_tensor(sq, oc, oc, ALU.mult))
                    do(v.tensor_reduce(ms8, AT_[:, 0:4, :].rearrange("p i (j n) -> p (i j) n", j=2), AX_X, ALU.add))
                    do(v.tensor_scalar(ms8, ms8, 1.0 / HD, EPS, ALU.mult, ALU.add), d2p)
                elif u == 8:
                    dve.wait_ge(p2d.sem, p2d.next("dve"))
                    for tb in range(NTB):
                        oh = XN[:, tb, 512:768].rearrange("p (h d) -> p h d", h=4)
                        do(v.tensor_tensor(oh, oh, r8[:, 4 * tb:4 * tb + 4].unsqueeze(2).to_broadcast([P, 4, 64]), ALU.mult))
                        do(v.tensor_tensor(oh, oh, p_sub[:, l, :].unsqueeze(1).to_broadcast([P, 4, 64]), ALU.mult))

            def nm_of(kind, tb):
                nk = P * (tb + 1)
                if kind == "b":
                    return (NMB0 if tb == 0 else NMB1)
                m = NMA[:, tb, 0:nk] if kind == "a" else c("nm_slide" if kind == "d" else "nm")[:, 2 * P - nk:2 * P]
                return m.unsqueeze(1).to_broadcast([P, 4, nk])

            units(UNITS, L, PT, nm_of, lambda kind: 32 ** -0.5 if kind == "c" else HD ** -0.5, lamt[:, l:l + 1], between)
            token_evac()
            full(4)
            normed_to_x(VEC[:, 0, :], d2a)
            pre_norm()
            token_evac(COLS[:, l * 16 + 8:l * 16 + 16])
            for ch in range(9):
                if ch < 8:
                    met(2)
                    dve.wait_ge(g_act.sem, l * G_ACT + IN_N + ch + 1)
                    do(v.tensor_tensor(HB[:, ch % 2, :, :], HB[:, ch % 2, :, :], HB[:, ch % 2, :, :], ALU.mult), hb_ready)
                if ch:
                    for j in range(2):
                        ks = slice(4 * ch - 4 + 2 * j, 4 * ch - 2 + 2 * j)
                        low_evac(j, hTl[:, ks, :], hTh[:, ks, :])
            full(16)
            normed_to_x(VEC[:, 1, :], d2pe)
            token_evac()
            low_evac(0, PLETl[:, :, :], PLETh[:, :, :])
            met(4)
            full(1)
            for tb in range(NTB):
                do(v.tensor_tensor(XN[:, tb, :], XN[:, tb, :], g_tokens(tb), ALU.mult), g_dve if tb else None)
            for tb in range(NTB):
                last = l == DEPTH - 1
                do(v.tensor_tensor(X[:, tb, :], X[:, tb, :], XN[:, tb, :], ALU.add), (d2pe if last else d2a) if tb else (vec_used if last else None))

        def layer_norm(src, width, eps, s_out, s_back):
            for tb in range(NTB):
                n = max(1, width // 512)
                wd_ = width // n
                for q in range(n):
                    do(v.bn_stats(bst[:, tb, 6 * q:6 * q + 6], src[:, tb, q * wd_:(q + 1) * wd_]))
                do(v.bn_aggr(mv[:, tb, :], bst[:, tb, 0:6 * n]))
            do(v.tensor_scalar(ms, mv[:, :, 1], eps, None, ALU.add), s_out)
            dve.wait_ge(s_back.sem, s_back.next("dve"))
            for tb in range(NTB):
                do(v.tensor_scalar(src[:, tb, :], src[:, tb, :], mv[:, tb, 0:1], rstd[:, tb:tb + 1], ALU.subtract, ALU.mult))

        def post_norm(s_out, s_back, dst, s_tb0, s_tb1):
            layer_norm(XN, D, 1e-5, s_out, s_back)
            do(v.tensor_tensor(XN[:, :, :], XN[:, :, :], VEC[:, 0, :].unsqueeze(1).to_broadcast([P, NTB, D]), ALU.mult))
            for tb in range(NTB):
                do(v.tensor_tensor(dst[:, tb, :], XN[:, tb, :], VEC[:, 1, :], ALU.add), s_tb1 if tb else s_tb0)

        for l in range(DEPTH):
            lsl = slice(4 * l, 4 * l + 4)
            token_evac()
            do(v.memset(PAD[:, :, 0:3], 0.0))
            av = P2[:, :, A2 + 256:A2 + 512]
            g2 = G[:, :, :].rearrange("p b (i t) -> p (b i) t", i=4)

            def conv(blocks, s):
                for b in blocks:
                    for j in range(4):
                        tap = COLS[:, 32 + l * 48 + j * 12 + b:32 + l * 48 + j * 12 + b + 1]
                        if j == 0:
                            do(v.tensor_scalar(CV[:, b, :], PAD[:, b, 0:S], tap, None, ALU.mult))
                        else:
                            do(v.scalar_tensor_tensor(CV[:, b, :], PAD[:, b, j:j + S], tap, CV[:, b, :], ALU.mult, ALU.add),
                               s if (b == blocks[-1] and j == 3) else None)

            for q, i in enumerate(SEQ2):
                n0, n1 = IN2_CHUNKS[i]
                b = 2 * (q % 2)
                if i == 4:
                    met(2)
                    continue
                full(2)
                if 1 <= i <= 3:
                    do(v.tensor_copy(PAD[:, 4 * (i - 1):4 * (i - 1) + 2, 3:], G[:, b, :].rearrange("p (m s) -> p m s", m=2)), g_dve)
                elif i >= 5:
                    o_ = BA2 + (n0 - 2560)
                    do(v.tensor_copy(P2[:, 0, o_:o_ + n1 - n0], G[:, b, 0:n1 - n0]), g_dve)
                dve.wait_ge(g_act.sem, DEPTH * G_ACT + l * len(IN2_CHUNKS) + q + 1)
                if i == 0:
                    layer_norm(av, 256, 1e-5, d2p, p2d)
                    do(v.tensor_tensor(av, av, ALN[:, 0, l, :].unsqueeze(1).to_broadcast([P, NTB, 256]), ALU.mult))
                    do(v.tensor_tensor(av, av, ALN[:, 1, l, :].unsqueeze(1).to_broadcast([P, NTB, 256]), ALU.add))
                if i == 1:
                    t0()
                    do(v.tensor_tensor(WST, T[0][:, :].rearrange("p (g t) -> p g t", g=4), c("upper1")[:, 0:P].unsqueeze(1).to_broadcast([P, 4, P]), ALU.mult),
                       t_taken[0])
                    conv(range(0, 4), d2a)
                if i == 2:
                    conv(range(4, 8), d2a)
                    dve.wait_ge(pe2d.sem, pe2d.next("dve"))
                    for g in range(4):
                        do(v.scalar_tensor_tensor(XN[:, :, g * 64:(g + 1) * 64], Sp[:, 0, g * P:(g + 1) * P].rearrange("p (t d) -> p t d", t=2),
                                                  COLS[:, P + 4 * l + g:P + 4 * l + g + 1], P2[:, :, A2 + g * 64:A2 + (g + 1) * 64], ALU.add, ALU.mult),
                           d2pe if g == 3 else None)
                if i == 3:
                    conv(range(8, 10), None)
                if i == 5:
                    do(v.tensor_tensor(LF[:, :, :], P2[:, :, BA2 + 4:BA2 + 8], p_dt[:, lsl].unsqueeze(1).to_broadcast([P, NTB, 4]), ALU.add))
                    do(v.tensor_copy(GL[:, :, :], LF[:, :, :]), d2a)
                    conv(range(10, 12), d2a)
                    dve.wait_ge(a2d.sem, a2d.next("dve"))
                    do(v.scalar_tensor_tensor(CV[:, 0:4, :].rearrange("p b s -> p (b s)"), CV[:, 0:4, :].rearrange("p b s -> p (b s)"), DK ** -0.5,
                                              SQ[:, 0:1024], ALU.mult, ALU.mult))
                    dve.wait_ge(a2d.sem, a2d.next("dve"))
                    do(v.tensor_tensor(CV[:, 4:8, :].rearrange("p b s -> p (b s)"), CV[:, 4:8, :].rearrange("p b s -> p (b s)"), SQ[:, 1024:2048], ALU.mult))
                    dve.wait_ge(a2d.sem, a2d.next("dve"))
                    do(v.scalar_tensor_tensor(GL[:, :, :], LF[:, :, :], 0.0, GL[:, :, :], ALU.max, ALU.add))
                    do(v.scalar_tensor_tensor(GL[:, :, :], GL[:, :, :], -1.0, ea4.unsqueeze(1).to_broadcast([P, NTB, 4]), ALU.mult, ALU.mult), d2pe)
                if i == 6:
                    t0()
                    do(v.tensor_copy(gc16, T[0][:, 0:16]), t_taken[0])
                    do(v.tensor_tensor(ms8, gc16[:, 8:16], gc16[:, 0:8], ALU.subtract))
                    dve.wait_ge(pe2d.sem, pe2d.next("dve"))
                    for k in range(8):
                        do(v.scalar_tensor_tensor(DT[:, k, :], Sp[:, k // 4, (k % 4) * P:(k % 4 + 1) * P], gc16[:, k:k + 1], c("nm_chunk"), ALU.subtract, ALU.subtract),
                           d2a if k == 7 else None)
                    for tb in range(NTB):
                        cos2 = c("cos2").rearrange("p (t n) -> p t n", t=2)[:, tb, :]
                        sin2 = c("sin2").rearrange("p (t n) -> p t n", t=2)[:, tb, :]
                        do(rope(P2[:, tb, C2:C2 + 512], cos2, sin2, 8, 64, R2A, R2B))
            dve.wait_ge(a2d.sem, a2d.next("dve"))
            dve.wait_ge(pe2d.sem, pe2d.next("dve"))
            for tb in range(NTB):
                do(v.tensor_tensor(MT[:, 4 * tb:4 * tb + 4, :], DT[:, 4 * tb:4 * tb + 4, :], T[tb][:, :].rearrange("p (i t) -> p i t", i=4), ALU.mult),
                   beta_taken if tb else None)
            dve.wait_ge(pe2d.sem, pe2d.next("dve"))
            do(v.tensor_tensor(MT, MT, g2[:, 8:16, :], ALU.mult), d2p)
            do(v.tensor_tensor(MLV[0], MT, c("level0").unsqueeze(1).to_broadcast([P, 8, P]), ALU.mult))
            for tb in range(NTB):
                do(v.tensor_tensor(TT[:, 4 * tb:4 * tb + 4, :], ident.unsqueeze(1).to_broadcast([P, 4, P]), MLV[0][:, 4 * tb:4 * tb + 4, :], ALU.subtract),
                   lv_done if tb else d2pe)
            evac(TN[:, 0:4, :])
            for lv in range(1, LEVELS):
                for tb in range(NTB):
                    cs = slice(4 * tb, 4 * tb + 4)
                    dve.wait_ge(pe2d.sem, pe2d.next("dve"))
                    if lv < LEVELS - 1:
                        do(v.tensor_tensor(TN[:, cs, :], TN[:, cs, :], g2[:, 8 + 4 * tb:12 + 4 * tb, :], ALU.subtract), d2pe)
                    do(v.tensor_tensor(TT[:, cs, :], TT[:, cs, :], Sp[:, tb, :].rearrange("p (i t) -> p i t", i=4), ALU.subtract), d2pe)
                if lv == 1:
                    do(v.tensor_tensor(AT_[:, :, :], AT_[:, :, :], DT, ALU.mult), lv_done)
                    do(v.tensor_tensor(bek8, BETA[:, :, :].rearrange("p t h -> p (t h)"), eg8, ALU.mult))
                    for tb in range(NTB):
                        q_ = CV[:, 0:4, tb * P:(tb + 1) * P]
                        do(v.tensor_tensor(q_, q_, EGB[:, tb, :].rearrange("p (h t) -> p h t", h=4), ALU.mult))
                if lv <= NTB:
                    t0()
                    src = T[0][:, :].rearrange("p (h d) -> p h d", h=4)
                    cs = slice(4 * (lv - 1), 4 * lv)
                    do(v.tensor_tensor(KBE[:, cs, :], src, bek8[:, cs].unsqueeze(2).to_broadcast([P, 4, P]), ALU.mult), lv_done if lv == 2 else None)
                    do(v.tensor_tensor(KD[:, cs, :], src, kds8[:, cs].unsqueeze(2).to_broadcast([P, 4, P]), ALU.mult), t_taken[0])
                if lv == 3:
                    do(v.memset(ST, 0.0), lv_done)
            dve.wait_ge(pe2d.sem, pe2d.next("dve"))
            do(v.tensor_copy(VB, g2[:, 0:8, :]), d2pe)
            for tb in range(NTB):
                for half in range(2):
                    rows = slice(half * CHUNK, (half + 1) * CHUNK)
                    cs = slice(4 * tb, 4 * tb + 4)
                    dve.wait_ge(pe2d.sem, pe2d.next("dve"))
                    do(v.tensor_tensor(DT[rows, cs, :], VB[rows, cs, :], G[rows, 0, :].rearrange("p (h e) -> p h e", h=4), ALU.subtract), d2pe)
                    if not (tb == 1 and half == 1):
                        dve.wait_ge(pe2d.sem, pe2d.next("dve"))
                        for h in range(H2):
                            do(v.scalar_tensor_tensor(ST[:, h, :], ST[:, h, :], EGL[:, tb, h, half:half + 1], G[:, 1, h * P:(h + 1) * P], ALU.mult, ALU.add),
                               d2pe if h == 3 else None)
            for tb in range(NTB):
                dve.wait_ge(a2d.sem, a2d.next("dve"))
                do(v.tensor_reduce(ms8[:, 4 * tb:4 * tb + 4], SQ[:, tb * 512:(tb + 1) * 512].rearrange("p (h e) -> p h e", h=4), AX_X, ALU.add))
            do(v.tensor_scalar(ms8, ms8, 1.0 / DK, 1e-6, ALU.mult, ALU.add), d2p)
            dve.wait_ge(p2d.sem, p2d.next("dve"))
            for tb in range(NTB):
                oh = XN[:, tb, 256:768].rearrange("p (h e) -> p h e", h=4)
                do(v.tensor_tensor(oh, Sp[:, tb, :].rearrange("p (h e) -> p h e", h=4), r8[:, 4 * tb:4 * tb + 4].unsqueeze(2).to_broadcast([P, 4, P]), ALU.mult))
                do(v.tensor_tensor(oh, oh, p_bn[:, l, :].unsqueeze(1).to_broadcast([P, 4, P]), ALU.mult))
                do(v.tensor_tensor(XN[:, tb, 256:768], XN[:, tb, 256:768], P2[:, tb, Z2:Z2 + 512], ALU.mult))
            evac(QKT2[:, 0:2, :])
            units(UNITS2, L2, PT2, lambda kind, tb: c(f"nm_dil{tb}").unsqueeze(1).to_broadcast([P, 4, P * (tb + 1)]),
                  lambda kind: HD ** -0.5, None)
            token_evac()
            full(4)
            for tb in range(NTB):
                do(v.scalar_tensor_tensor(XN[:, tb, :], X[:, tb, :], ALPHA, g_tokens(tb), ALU.mult, ALU.add), g_dve if tb else None)
            post_norm(d2p, p2d, X, None, d2pe)
            vec_free.append(d2pe.made)
            if l == 0:
                token_evac()
                for ch in range(NCH2 + 1):
                    if ch < NCH2:
                        met(2)
                        dve.wait_ge(silu_ready.sem, silu_ready.next("dve"))
                        b = 2 * (ch % 2)
                        do(v.tensor_tensor(HB2[:, ch % 2, :, :], HS[:, ch % 2, :, :], G[:, b:b + 2, CH2:2 * CH2], ALU.mult), hb_ready)
                    if ch:
                        ks = slice(2 * ch - 2, 2 * ch)
                        low_evac((ch - 1) % 2, hT2l[:, ks, :], hT2h[:, ks, :])
                full(FT2 // 2)
                for tb in range(NTB):
                    do(v.scalar_tensor_tensor(XN[:, tb, :], X[:, tb, :], ALPHA, g_tokens(tb), ALU.mult, ALU.add), g_dve if tb else None)
                post_norm(d2p, p2d, X, None, vec_used)

        dve.wait_ge(a2d.sem, a2d.next("dve"))
        do(v.tensor_tensor(RWl[:, :, :], RW[:, :, :], RWh[:, :, :].bitcast(F32), ALU.subtract))
        token_evac()
        dve.wait_ge(pe2d.sem, pe2d.next("dve"))
        do(v.tensor_copy(LG, Sp[:, 0, 0:16].rearrange("p (t e) -> p t e", t=2)))
        for tb in range(NTB):
            do(v.max(TOPV[:, tb, :], LG[:, tb, :]))
            do(v.max_index(IDX[:, tb, :], TOPV[:, tb, :], LG[:, tb, :]))
        do(v.tensor_copy(IDXF, IDX[:, :, :]))
        do(v.tensor_tensor(PR[:, :, 0:1], TOPV[:, :, 1:2], TOPV[:, :, 0:1], ALU.subtract), d2a)
        for tb in range(NTB):
            do(v.tensor_scalar(SEL[:, tb, :], c("iota")[:, 0:8], IDXF[:, tb, 0:1], None, ALU.is_equal))
            do(v.tensor_scalar(OH[:, tb, :], c("iota")[:, 0:8], IDXF[:, tb, 1:2], None, ALU.is_equal))
        dve.wait_ge(a2d.sem, a2d.next("dve"))
        do(v.tensor_scalar(PR[:, :, 1:2], PR[:, :, 0:1], 1.0, None, ALU.add))
        do(v.reciprocal(PR[:, :, 2:3], PR[:, :, 1:2]))
        do(v.tensor_tensor(PR[:, :, 3:4], PR[:, :, 0:1], PR[:, :, 2:3], ALU.mult))
        do(v.memset(CW, 0.0))
        for tb in range(NTB):
            do(v.tensor_scalar(CW[:, tb, 1:9], SEL[:, tb, :], PR[:, tb, 2:3], None, ALU.mult))
            do(v.scalar_tensor_tensor(CW[:, tb, 1:9], OH[:, tb, :], PR[:, tb, 3:4], CW[:, tb, 1:9], ALU.mult, ALU.add))
        do(v.tensor_copy(CW[:, :, 9:17], CW[:, :, 1:9]))
        do(v.tensor_tensor(SEL, SEL, OH, ALU.add), d2pe)
        do(v.memset(RK, 1e6))
        do(v.tensor_scalar(OH, SEL, -1e6, 1e6, ALU.mult, ALU.add))
        dve.wait_ge(pe2d.sem, pe2d.next("dve"))
        do(v.tensor_tensor(RK[:, :, 0:8], OH, Sp[:, 1, 0:16].rearrange("p (t e) -> p t e", t=2), ALU.add))
        do(v.tensor_scalar(RK[:, :, 8:16], RK[:, :, 0:8], float(P), None, ALU.subtract))
        do(v.tensor_reduce(CNT[:, 0:1], Sp[:, 1, 16:24], AX_X, ALU.max))
        do(v.tensor_scalar(CNT[:, 1:2], CNT[:, 0:1], float(P), None, ALU.is_gt))
        do(v.tensor_scalar(CNT[:, 2:3], CNT[:, 1:2], float(NE), float(NE), ALU.mult, ALU.add))
        do(v.tensor_copy(FLAG[:, :], CNT[:, 1:3]), m_flag)
        do(v.memset(PmT, 0.0))
        do(v.memset(ACC, 0.0), m_acc)

        def slots(i):
            for tb in range(NTB):
                last = v.tensor_scalar(Pm[:, tb, :], c("iota"), RK[:, tb, bass.ds(i, 1)], None, ALU.is_equal)
            last.then_inc(m_p.sem, 1)

        def gather_dve(i):
            dve.wait_ge(m_ga.sem, i + 1)
            v.tensor_tensor(xgTl[:, :, :], Sp[:, :, :].rearrange("p b (k j) -> p (b k) j", k=4), xgTh[:, :, :].bitcast(F32), ALU.subtract).then_inc(m_gd.sem, 1)

        def add_back(i, tb):
            dve.wait_ge(m_sc.sem, i * 2 + (tb + 1))
            dve.wait_ge(m_acc.sem, i * 2 + (tb + 1))
            v.scalar_tensor_tensor(ACC[:, tb, :], Sp[:, :, :].rearrange("p b n -> p (b n)"), CW[:, tb, bass.ds(i, 1)], ACC[:, tb, :],
                                   ALU.mult, ALU.add).then_inc(m_acc.sem, 1)

        slots(0)
        gather_dve(0)

        def expert_dve(i):
            def low_part(j):
                q, m = (U0 + j) % R, of_dve(e_floats(j))
                dve.wait_ge(w_hi.sem, i * USES_E + (U0 + j + 1))
                v.tensor_tensor(ring_lo[:, q, 0:m], ring[:, q, 0:m], ring_hi[:, (U0 + j) % H, 0:m].bitcast(F32), ALU.subtract).then_inc(w_lo.sem, 1)

            def hidden_e(ch):
                k = ch % 2
                dve.wait_ge(m_th[k].sem, i * ((NCH2 + 1 - k) // 2) + (ch // 2 + 1))
                v.tensor_tensor(hEl[:, 2 * ch:2 * ch + 2, :], T[k][:, 0:2 * P].rearrange("p (k j) -> p k j", k=2),
                                hEh[:, 2 * ch:2 * ch + 2, :].bitcast(F32), ALU.subtract).then_inc(m_tt[k].sem, 1)

            for j in range(H - 1):
                low_part(j)
            for ch in range(NCH2):
                for j in range(2):
                    low_part(2 * ch + H - 1 + j)
                dve.wait_ge(m_silu.sem, i * NCH2 + (ch + 1))
                v.tensor_tensor(HB2[:, ch % 2, 0, :], HS[:, ch % 2, 0, :], G[:, ch % 2, CH2:2 * CH2], ALU.mult).then_inc(m_hb.sem, 1)
                if ch:
                    hidden_e(ch - 1)
                if ch == 2:
                    add_back(i, 0)
                if ch == 5:
                    add_back(i, 1)
            hidden_e(NCH2 - 1)
            dve.wait_ge(m_tf[1].sem, 6 * i + 6)
            slots(i + 1)
            for q in range(H - 1, len(DOWN2)):
                low_part(2 * NCH2 + q)
                if q == GATHER_AT + H - 1:
                    gather_dve(i + 1)

        with dve.Fori(0, NE) as i:
            expert_dve(i)
        over = dve.value_load(FLAG[0:1, 0:1], min_val=0, max_val=1)
        with dve.If(over > 0):
            with dve.Fori(NE, 2 * NE) as i:
                expert_dve(i)
        n_all = dve.value_load(FLAG[0:1, 1:2], min_val=NE, max_val=2 * NE)
        for tb in range(NTB):
            add_back(n_all, tb)
        dve.wait_ge(m_acc.sem, n_all * 2 + 3)
        for tb in range(NTB):
            do(v.scalar_tensor_tensor(XN[:, tb, :], X[:, tb, :], ALPHA, ACC[:, tb, :], ALU.mult, ALU.add))
        post_norm(f_r, f_p, XN, f_out, f_out)

    @block.gpsimd
    def _(pool):
        g = nc.gpsimd

        def load(dst, src, s=loaded):
            pool.dma_start(dst, src, allow_slow_non_contiguous=True).then_inc(s.sem, 16)

        def rows_everywhere(ap, n):
            return ap.partition_broadcast(n)

        def power(dst, src, n, s):
            g.tensor_tensor(dst, src, c("mhalf")[:, 0:n], ALU.pow).then_inc(s.sem, 1)

        def rms():
            pool.wait_ge(s_ssq.sem, s_ssq.next("pool", 2))
            step(pool, g.tensor_scalar(ms, ssq, 1.0 / D, EPS, ALU.mult, ALU.add), pstep)
            power(rstd, ms, 2, s_rstd)

        def asked(dst, src, n, s_in=d2p, s_out=p2d):
            pool.wait_ge(s_in.sem, s_in.next("pool"))
            power(dst, src, n, s_out)

        n_lo = [0, 0]

        def met(n):
            n_lo[1] += n
            while n_lo[0] < min(n_lo[1] + H - 1, U0):
                t = n_lo[0]
                n_lo[0] += 1
                m = floats_of(TILES[t])
                cs = slice(of_dve(m), m)
                pool.wait_ge(w_hi.sem, t + 1)
                g.tensor_tensor(ring_lo[:, t % R, cs], ring[:, t % R, cs], ring_hi[:, t % H, cs].bitcast(F32), ALU.subtract).then_inc(w_lo_pool.sem, 1)

        def rope(x, cos, sin, heads, width, a, b):
            xv = x.rearrange("p (h d) -> p h d", h=heads)
            a, b = a.rearrange("p (h d) -> p h d", h=heads), b.rearrange("p (h d) -> p h d", h=heads)
            hw = width // 2
            step(pool, g.tensor_tensor(a, xv, cos.unsqueeze(1).to_broadcast([P, heads, width]), ALU.mult), pstep)
            step(pool, g.tensor_tensor(b[:, :, 0:hw], xv[:, :, hw:], sin[:, 0:hw].unsqueeze(1).to_broadcast([P, heads, hw]), ALU.mult), pstep)
            step(pool, g.tensor_tensor(b[:, :, hw:], xv[:, :, 0:hw], sin[:, hw:].unsqueeze(1).to_broadcast([P, heads, hw]), ALU.mult), pstep)
            step(pool, g.tensor_tensor(xv, a, b, ALU.add), pstep)

        def gains(q, name, l):
            vec_loaded[q].made += 16
            pool.dma_start(VEC[:, q, :], w[name][l].partition_broadcast(P)).then_inc(vec_loaded[q].sem, 16)

        def gains_loaded(q):
            pool.wait_ge(vec_loaded[q].sem, vec_loaded[q].made)

        load(POS[:, :], w["positions"][0].rearrange("(t p) -> p t", p=P))
        for q, name in enumerate(("lambda_q1", "lambda_k1", "lambda_q2", "lambda_k2")):
            load(p_lam[:, q], w[name].partition_broadcast(P))
        pool.wait_ge(c_loaded.sem, 16)
        rms()
        load(p_bf, w["b_forget"].rearrange("l h -> (l h)").partition_broadcast(P))
        load(p_sink, w["sinks"].rearrange("l h -> (l h)").partition_broadcast(P))
        load(p_sub, w["diff_subln"].partition_broadcast(P))
        load(p_alog, w["b_a_log_2"].rearrange("l h -> (l h)").partition_broadcast(P))
        load(p_dt, w["b_dt_bias_2"].rearrange("l h -> (l h)").partition_broadcast(P))
        load(p_bn, w["b_norm_g_2"].partition_broadcast(P))
        load(ALN[:, 0], w["a_ln_g_2"].partition_broadcast(P))
        load(ALN[:, 1], w["a_ln_b_2"].partition_broadcast(P))
        load(RW[:, :, :], w["moe_router_2"][0].rearrange("(k p) e -> p k e", p=P))
        gains(0, "norm_post_mix", 0)
        for l in range(DEPTH):
            if l:
                rms()
            gains(1, "norm_post_mlp", l)
            met(2 * IN_N)
            pool.wait_ge(g_dve.sem, g_dve_in[l])
            pool.wait_ge(g_act.sem, l * G_ACT + IN_N)
            for tb in range(NTB):
                rope(PROJ[:, tb, D_Q:D_Q + 384], RCOS[:, tb, :], RSIN[:, tb, :], 6, 64, XN[:, 0, 512:896], XN[:, 1, 512:896])
            for q, col in enumerate((D_K, D_K + 64)):
                for tb in range(NTB):
                    last = g.tensor_copy(IKD[:, 1 + q, tb, :].rearrange("p (r d) -> p r d", r=2),
                                         PROJ[:, tb, col:col + 64].unsqueeze(1).to_broadcast([P, 2, 64]))
            last.then_inc(p2pe.sem, 1)
            asked(r8, ms8, 8)
            gains_loaded(0)
            met(4)
            rms()
            rms()
            gains(0, *(("norm_post_mix", l + 1) if l + 1 < DEPTH else ("ln1_g_2", 0)))
            load(PLE, w["p"][l, 0].rearrange("(t p) d -> p t d", p=P), misc_loaded)
            gains_loaded(1)
            met(32)
            rms()
            met(5)
        for l in range(DEPTH):
            pool.wait_ge(vec_used.sem, l + 1)
            if l:
                gains(0, "ln1_g_2", l)
            gains(1, "ln1_b_2", l)
            load(WSA, w["a_ws_2"][l].rearrange("g t s -> t g s"), misc_loaded)
            met(2)
            asked(rstd, ms, 2)
            met(2 * len(IN2_CHUNKS) - 2)
            pool.wait_ge(d2p.sem, d2p.next("pool"))
            for lv in range(1, LEVELS):
                if lv >= 2:
                    pool.wait_ge(lv_done.sem, lv_done.next("pool"))
                m = c(f"level{lv}").unsqueeze(1).to_broadcast([P, 8, P])
                g.tensor_tensor(MLV[lv % 2], MT, m, ALU.mult).then_inc(p2pe.sem, 1)
            asked(r8, ms8, 8)
            for q in range(2):
                gains_loaded(q)
            met(4)
            asked(rstd, ms, 2)
            pool.wait_ge(d2pe.sem, vec_free[l])
            gains(0, "ln2_g_2", l)
            gains(1, "ln2_b_2", l)
            for q in range(2):
                gains_loaded(q)
            if l == 0:
                met(2 * NCH2 + FT2 // 2)
                asked(rstd, ms, 2)

        def expert_pool(i):
            for j in range(USES_E):
                q, m = (U0 + j) % R, e_floats(j)
                pool.wait_ge(w_hi.sem, i * USES_E + (U0 + j + 1))
                cs = slice(of_dve(m), m)
                g.tensor_tensor(ring_lo[:, q, cs], ring[:, q, cs], ring_hi[:, (U0 + j) % H, cs].bitcast(F32), ALU.subtract).then_inc(w_lo_pool.sem, 1)

        with pool.Fori(0, NE) as i:
            expert_pool(i)
        pool.wait_ge(m_flag.sem, 1)
        over = pool.value_load(FLAG[0:1, 0:1], min_val=0, max_val=1)
        with pool.If(over > 0):
            with pool.Fori(NE, 2 * NE) as i:
                expert_pool(i)
        asked(rstd, ms, 2, f_r, f_p)

    ctx.close()


_INS = ["x", "p", "positions", "w_in", "b_forget", "lambda_q1", "lambda_k1", "lambda_q2", "lambda_k2", "diff_subln",
        "sinks", "w_out", "norm_pre_mix", "norm_post_mix", "norm_pre_mlp", "norm_post_mlp", "w_mlp_up", "w_mlp_down",
        "w_ple_proj", "w_ple_gate", "w_in_2", "conv_w_2", "a_ln_g_2", "a_ln_b_2", "a_ws_2", "a_bs_2", "b_a_log_2",
        "b_dt_bias_2", "b_norm_g_2", "w_out_2", "ln1_g_2", "ln1_b_2", "ln2_g_2", "ln2_b_2", "ffn_w_gate_2", "ffn_w_up_2",
        "ffn_w_down_2", "moe_router_2", "moe_w_gate_2", "moe_w_up_2", "moe_w_down_2"]


def kernel(**inputs):
    import concourse.bacc as _bacc
    from concourse.bass_utils import run_bass_kernel_spmd as _run

    nc = _bacc.Bacc("TRN2", target_bir_lowering=False, num_devices=1)
    table, at = consts()
    arrays, w = {}, {}
    for name in _INS:
        a = np.ascontiguousarray(inputs[name])
        arrays[f"in_{name}"] = a
        w[name] = nc.dram_tensor(f"in_{name}", a.shape, mybir.dt.from_np(a.dtype), kind="ExternalInput").ap()
    arrays["shape_tables"] = table
    const_d = nc.dram_tensor("shape_tables", table.shape, F32, kind="ExternalInput").ap()
    out_d = nc.dram_tensor("out", (1, S, D), F32, kind="ExternalOutput").ap()
    build(nc, at, table.shape[1], const_d, w, out_d)
    r = _run(nc, [arrays], core_ids=[0])
    return r.results[0]["out"]
```

```python
import math
from contextlib import ExitStack

import numpy as np

import concourse.bass as bass
from concourse import mybir

F32 = mybir.dt.float32
F32R = mybir.dt.float32r
I32 = mybir.dt.int32
U32 = mybir.dt.uint32
ALU = mybir.AluOpType
ACT = mybir.ActivationFunctionType
AX_X = mybir.AxisListType.X

P = 128
D = 1024
S = 256
NTB = S // P
KT = D // P
DEPTH = 2
EPS = 1e-6
BIG = 1e30
TAKEN = -3e38
HD = 64
TOPK = min(256, S // 4)
D_FF = 4 * D
D_PLE = 256
A_Q, A_K, A_V, A_IQ, A_IK, A_IW = 0, 256, 512, 768, 1280, 1344
B_Q, B_K, B_V, B_F = 1352, 1608, 1864, 2120
C_Q, C_K, C_V = 2124, 2380, 2636
D_Q, D_K, D_V, D_IN = 2892, 3148, 3276, 3404
IDX_HEADS = 8
D_IN2 = 3336
H2 = 4
DK = 128
CHUNK = 64
LEVELS = 6
FF2 = 2816
FT2 = FF2 // P
CH2 = 256
NCH2 = FF2 // CH2
NE = 8
N_TAPS = DEPTH * 4 * 12
ALPHA = (2.0 * DEPTH) ** 0.25

R = 6
H = 3
SLOT = 2048
DOWN2 = [1] * 6 + [2] * 8
USES_E = 2 * NCH2 + len(DOWN2)
assert sum(DOWN2) == FT2 and USES_E % R == 0 and USES_E % H == 0
CT_N = 2 * NE + 2
GATHER_AT = 8


def consts():
    i = np.arange(P)
    s_, t_ = i[:, None], i[None, :]
    cols, at = [], {}

    def put(name, a):
        a = np.asarray(a, np.float32).reshape(P, -1)
        at[name] = (sum(c.shape[1] for c in cols), a.shape[1])
        cols.append(a)

    put("ident", np.eye(P))
    causal = np.where(i[None, :] <= i[:, None], 0.0, BIG)
    put("nm", np.concatenate([np.zeros((P, P)), causal], 1))
    slide = np.where(i[None, :] > i[:, None], 0.0, BIG)
    put("nm_slide", np.concatenate([slide, causal], 1))
    for tb in range(NTB):
        t = tb * P + i[:, None]
        s = np.arange((tb + 1) * P)[None, :]
        n = np.zeros((P, (tb + 1) * P))
        for window, dil in ((128, 1), (512, 4), (2048, 16)):
            n += (s <= t) & ((t - s) % dil == 0) & (t - s <= window)
        put(f"nm_dil{tb}", np.where(n > 0, -np.log(np.maximum(n, 1)), BIG))
    put("upper1", np.concatenate([s_ <= t_, np.ones((P, P))], 1))
    put("before", s_ < t_)
    same = (s_ // CHUNK) == (t_ // CHUNK)
    put("chunk_upper", same & (s_ <= t_))
    put("chunk_ones", same)
    put("nm_chunk", np.where(same & (s_ <= t_), 0.0, BIG))
    for l in range(LEVELS):
        b = 1 << l
        put(f"level{l}", (s_ // (2 * b) == t_ // (2 * b)) & ((t_ // b) % 2 == 1) & ((s_ // b) % 2 == 0))
    put("iota", np.broadcast_to(i[None, :], (P, P)))
    half = HD // 2
    inv = (np.float32(10000.0) ** (-np.arange(half, dtype=np.float32) / np.float32(half))).astype(np.float32)
    inv32 = (np.float32(10000.0) ** (-np.arange(16, dtype=np.float32) / np.float32(16))).astype(np.float32)
    put("inv_freq", np.broadcast_to(np.concatenate([inv, inv32])[None], (P, 48)))
    tok = np.arange(S, dtype=np.float32).reshape(NTB, P)
    inv2 = (np.float32(10000.0) ** (-np.arange(0, HD, 2, dtype=np.float32) / np.float32(HD))).astype(np.float32)
    ang = (tok[:, :, None] * inv2).astype(np.float32).astype(np.float64)
    put("cos2", np.concatenate([np.cos(ang), np.cos(ang)], 2).transpose(1, 0, 2))
    put("sin2", np.concatenate([-np.sin(ang), np.sin(ang)], 2).transpose(1, 0, 2))
    put("one", np.ones((P, 1)))
    put("eps", np.full((P, 1), EPS))
    put("mhalf", np.full((P, 16), -0.5))
    return np.ascontiguousarray(np.concatenate(cols, 1)), at


class Signal:

    def __init__(self, sem):
        self.sem, self.made, self.seen = sem, 0, {}

    def next(self, who, n=1):
        self.seen[who] = self.seen.get(who, 0) + n
        return self.seen[who]


def build(nc, at, n_const, const_d, w, out_d):
    ctx = ExitStack()

    def sb(name, shape, dt=F32):
        return ctx.enter_context(nc.sbuf_tensor(name, shape, dt))

    def sig(name):
        return Signal(ctx.enter_context(nc.semaphore(name)))

    def base_now():
        return (nc.sbuf_base + 31) // 32 * 32

    def parts_at(name, base, o, shape):
        return nc.alloc_sbuf_tensor_at(name, shape, F32R, offset=base + 4 * o)

    ring_base = base_now()
    ring = sb("ring", [P, R, SLOT])
    ring_lo = parts_at("ring_lo", ring_base, 0, [P, R, SLOT])
    ring_hi = sb("ring_hi", [P, H, SLOT], F32R)
    X = sb("X", [P, NTB, D])
    XN = sb("XN", [P, NTB, D])
    xTh = sb("xTh", [P, KT, S], F32R)
    xTl = sb("xTl", [P, KT, S], F32R)
    RW = sb("RW", [P, KT, NE])
    RWh, RWl = sb("RWh", [P, KT, NE], F32R), sb("RWl", [P, KT, NE], F32R)
    C = sb("C", [P, n_const])
    VEC = sb("VEC", [P, 2, D])
    COLS = sb("COLS", [P, N_TAPS + 8])
    SM = sb("SM", [P, 900])
    POS = sb("POS", [P, NTB], I32)
    IDX = sb("IDX", [P, NTB, 8], U32)
    FLAG = sb("FLAG", [P, 2], I32)
    ARENA_N = 17472
    arena_base = base_now()
    ARENA = sb("ARENA", [P, ARENA_N])

    G = ctx.enter_context(nc.psum_tensor("G", [P, 4, 512], F32))
    T = [ctx.enter_context(nc.psum_tensor(f"T{i}", [P, 512], F32)) for i in range(2)]
    Sp = ctx.enter_context(nc.psum_tensor("Sp", [P, 2, 512], F32))

    def c(name):
        o, n = at[name]
        return C[:, o:o + n]

    ident = c("ident")
    small_at = [0]

    def small(n):
        o = small_at[0]
        small_at[0] += n
        assert small_at[0] <= 900
        return SM[:, o:o + n]

    p_bf, p_sink = small(8), small(8)
    p_lam = small(256).rearrange("p (v l d) -> p v l d", v=4, l=2)
    p_sub = small(128).rearrange("p (l d) -> p l d", l=2)
    p_alog, p_dt = small(8), small(8)
    p_bn = small(256).rearrange("p (l d) -> p l d", l=2)
    ssq, ms, rstd = small(2), small(2), small(2)
    posf = small(2)
    nmx = small(8).rearrange("p (b m) -> p b m", b=2)
    rsum = small(8).rearrange("p (b m) -> p b m", b=2)
    esk = small(8).rearrange("p (b m) -> p b m", b=2)
    rinv = small(8).rearrange("p (b m) -> p b m", b=2)
    nsink = small(4)
    lamt = small(4)
    top8 = small(8)
    gc16, kds8, eg8, bek8 = small(16), small(8), small(8), small(8)
    EGL = small(16).rearrange("p (t h c) -> p t h c", t=2, h=4)
    iws, cums = small(16).rearrange("p (t h) -> p t h", t=2), small(8).rearrange("p (t h) -> p t h", t=2)
    ea4 = small(4)
    ms8, r8 = small(8), small(8)
    bst = small(24).rearrange("p (t n) -> p t n", t=2)
    mv = small(4).rearrange("p (t n) -> p t n", t=2)

    def ar(o, n):
        assert o + n <= ARENA_N, (o, n)
        return ARENA[:, o:o + n]

    PROJ = ar(0, NTB * D_IN).rearrange("p (t n) -> p t n", t=NTB)
    o = NTB * D_IN
    QKT = ar(o, 21 * S).rearrange("p (b s) -> p b s", b=21)
    o += 21 * S
    L = ar(o, 2 * 4 * S).rearrange("p (b m s) -> p b m s", b=2, m=4)
    ROPE_A = ar(o, 1024)
    ROPE_B = ar(o + 1024, 1024)
    o += 2 * 4 * S
    PT = ar(o, 1024).rearrange("p (k m t) -> p k m t", k=2, m=4)
    o += 1024
    NMB = ar(o, 1536)
    NMB0 = ar(o, 512).rearrange("p (h s) -> p h s", h=4)
    NMB1 = ar(o + 512, 1024).rearrange("p (h s) -> p h s", h=4)
    o += 1536
    NMA = ar(o, 512).rearrange("p (t s) -> p t s", t=2)
    o += 512
    AT_ = sb("AT_", [P, 8, P])
    TAPS = AT_[0:N_TAPS, 6, :]
    ABS = AT_[0:8, 7, :]
    PLE = AT_[:, 0:4, :].rearrange("p (t k) n -> p t (k n)", t=NTB)
    IKD = AT_[:, 0:6, :].rearrange("p (q t) n -> p q t n", q=3)
    LF = sb("LF", [P, NTB, 4])
    GL = sb("GL", [P, NTB, 4])
    BETA = sb("BETA", [P, NTB, 4])
    ROT = sb("ROT", [P, 384])
    RCOS = ROT[:, 0:128].rearrange("p (t n) -> p t n", t=2)
    RSIN = ROT[:, 128:256].rearrange("p (t n) -> p t n", t=2)
    RCOS32 = ROT[:, 256:320].rearrange("p (t n) -> p t n", t=2)
    RSIN32 = ROT[:, 320:384].rearrange("p (t n) -> p t n", t=2)
    ANG = ar(0, 96).rearrange("p (t n) -> p t n", t=2)
    KK_ = ar(96, 96).rearrange("p (t n) -> p t n", t=2)
    SN = ar(192, 96).rearrange("p (t n) -> p t n", t=2)
    SH = ar(288, 96).rearrange("p (t n) -> p t n", t=2)
    hTh = parts_at("hTh", arena_base, 0, [P, 32, S])
    hTl = parts_at("hTl", arena_base, 32 * S, [P, 32, S])
    HB = XN[:, :, :].rearrange("p b (t n) -> p b t n", t=NTB)
    PLETh = parts_at("PLETh", arena_base, 64 * S, [P, 2, S])
    PLETl = parts_at("PLETl", arena_base, 66 * S, [P, 2, S])
    PLR = ar(0, NTB * D).rearrange("p (t n) -> p t n", t=NTB)
    P2 = ar(0, NTB * 1800).rearrange("p (t n) -> p t n", t=NTB)
    A2, Z2, BA2, C2 = 0, 512, 1024, 1032
    o2 = 3600
    PAD = ar(o2, 12 * (S + 3)).rearrange("p (b s) -> p b s", b=12)
    TN = ar(o2, 1024).rearrange("p (i t) -> p i t", i=8)
    TT = ar(o2 + 1024, 1024).rearrange("p (i t) -> p i t", i=8)
    WB = ar(o2 + 2048, 1024).rearrange("p (i t) -> p i t", i=8)
    o2 += 12 * (S + 3)
    CV = ar(o2, 12 * S).rearrange("p (b s) -> p b s", b=12)
    o2 += 12 * S
    SQ = ar(o2, 2048)
    MLV = [ar(o2 + 1024 * i, 1024).rearrange("p (i t) -> p i t", i=8) for i in range(2)]
    o2 += 2048
    VB = ar(o2, 1024).rearrange("p (i e) -> p i e", i=8)
    KBE = ar(o2 + 1024, 1024).rearrange("p (i e) -> p i e", i=8)
    KD = ar(o2 + 2048, 1024).rearrange("p (i e) -> p i e", i=8)
    MT = ar(o2 + 3072, 1024).rearrange("p (i t) -> p i t", i=8)
    WSA = ar(o2 + 3072, 512).rearrange("p (g s) -> p g s", g=4)
    WST = ar(o2 + 3584, 512).rearrange("p (g t) -> p g t", g=4)
    o2 += 4096
    EGB = ar(o2 - 4096 + 2048, 1024).rearrange("p (t n) -> p t n", t=2)
    DT = ar(o2, 1024).rearrange("p (i t) -> p i t", i=8)
    o2 += 1024
    WTs = MT
    ST = ar(o2, 512).rearrange("p (h e) -> p h e", h=4)
    o2 += 512
    QKT2 = ar(3600, 4 * S).rearrange("p (b s) -> p b s", b=4)
    L2 = ar(3600 + 1024, 2048).rearrange("p (b m s) -> p b m s", b=2, m=4)
    PT2 = ar(3600 + 3072, 1024).rearrange("p (k m t) -> p k m t", k=2, m=4)
    R2A, R2B = XN[:, 0, 256:768], XN[:, 1, 256:768]
    ALN = sb("ALN", [P, 2, 2, 256])
    hT2h = parts_at("hT2h", arena_base, 0, [P, FT2, S])
    hT2l = parts_at("hT2l", arena_base, FT2 * S, [P, FT2, S])
    HS = ar(2 * FT2 * S, 2 * NTB * CH2).rearrange("p (b t n) -> p b t n", b=2, t=NTB)
    HB2 = ar(2 * FT2 * S + 1024, 2 * NTB * CH2).rearrange("p (b t n) -> p b t n", b=2, t=NTB)
    hEh = parts_at("hEh", arena_base, 0, [P, FT2, P])
    hEl = parts_at("hEl", arena_base, FT2 * P, [P, FT2, P])
    om = 2 * FT2 * P
    Pm = ar(om, NTB * P).rearrange("p (t j) -> p t j", t=NTB)
    PmT = parts_at("PmT", arena_base, om + 256, [P, NTB, P])
    ACC = ar(om + 512, NTB * D).rearrange("p (t n) -> p t n", t=NTB)
    YBh = parts_at("YBh", arena_base, om + 2560, [P, D])
    YBl = parts_at("YBl", arena_base, 2 * FT2 * S + 3072, [P, D])
    xgTh = parts_at("xgTh", arena_base, om + 3584, [P, KT, P])
    xgTl = parts_at("xgTl", arena_base, 2 * FT2 * S + 2048, [P, KT, P])
    RK = ar(om + 4608, NTB * CT_N).rearrange("p (t e) -> p t e", t=NTB)
    CW = ar(om + 4608 + 64, NTB * CT_N).rearrange("p (t e) -> p t e", t=NTB)
    LG = ar(om + 4608 + 192, NTB * NE).rearrange("p (t e) -> p t e", t=NTB)
    SEL = ar(om + 4608 + 208, NTB * NE).rearrange("p (t e) -> p t e", t=NTB)
    OH = ar(om + 4608 + 224, NTB * NE).rearrange("p (t e) -> p t e", t=NTB)
    TOPV = ar(om + 4608 + 240, NTB * 8).rearrange("p (t e) -> p t e", t=NTB)
    IDXF = ar(om + 4608 + 256, NTB * 8).rearrange("p (t e) -> p t e", t=NTB)
    PR = ar(om + 4608 + 272, NTB * 4).rearrange("p (t e) -> p t e", t=NTB)
    CNT = ar(om + 4608 + 280, 16)
    ANY = ar(om + 4608 + 296, NTB * NE).rearrange("p (t e) -> p t e", t=NTB)

    x_loaded, c_loaded = sig("x_loaded"), sig("tables_loaded")
    rows_loaded = sig("rows_loaded")
    loaded = sig("params_loaded")
    vec_loaded = [sig("vec_loaded0"), sig("vec_loaded1")]
    misc_loaded = sig("misc_loaded")
    misc_used = sig("misc_used")
    w_in_slot = [Signal(ctx.enter_context(nc.semaphore(f"w_in_slot{i}"))) for i in range(R)]
    w_hi, w_lo, w_lo_pool = sig("w_high_part"), sig("w_low_part"), sig("w_low_part_pool")
    w_used = sig("w_used")
    g_half = sig("g_first_half")
    x_full = [sig("x_full0"), sig("x_full1")]
    x_hi = [sig("x_high0"), sig("x_high1")]
    x_taken = [sig("x_taken0"), sig("x_taken1")]
    g_dve, g_act = sig("g_taken_dve"), sig("g_taken_act")
    t_full = [sig("t_full0"), sig("t_full1")]
    t_taken = [sig("t_taken0"), sig("t_taken1")]
    s_ssq, s_rstd, xn_ready = sig("ssq_ready"), sig("rstd_ready"), sig("xn_ready")
    s_ms = sig("ms_ready")
    beta_taken = sig("beta_rows_taken")
    lv_done, pe_own = sig("level_done"), sig("pe_own")
    dstep, astep, pstep = sig("dve_step"), sig("act_step"), sig("pool_step")
    a2d, d2a = sig("act_to_dve"), sig("dve_to_act")
    d2p, p2d = sig("dve_to_pool"), sig("pool_to_dve")
    d2pe = sig("dve_to_pe")
    a2pe = sig("act_to_pe")
    pe2d, pe2a = sig("pe_to_dve"), sig("pe_to_act")
    p2pe = sig("pool_to_pe")
    scores, taken = sig("scores_ready"), sig("scores_taken")
    maxed, probs, comb = sig("max_ready"), sig("probs_ready"), sig("diff_ready")
    pv_done, o_ready = sig("pv_ready"), sig("o_ready")
    idx_s, idx_taken = sig("index_dots"), sig("index_dots_taken")
    silu_ready, hb_ready = sig("silu_ready"), sig("hidden_ready")
    out_done = sig("out_written")
    m_flag, f_out, f_r, f_p = sig("overflow_flag"), sig("result_ready"), sig("final_dve"), sig("final_pool")
    m_chunk, m_silu, m_hb = sig("e_chunk"), sig("e_silu"), sig("e_hidden")
    m_tf, m_tt = [sig("e_t_full0"), sig("e_t_full1")], [sig("e_t_taken0"), sig("e_t_taken1")]
    m_th = [sig("e_t_high0"), sig("e_t_high1")]
    m_p, m_g, m_gd, m_ga = sig("e_slots"), sig("e_gathered"), sig("e_gather_taken_dve"), sig("e_gather_taken_act")
    m_yh, m_y = sig("e_y_high_part"), sig("e_y_taken")
    m_sc, m_acc = sig("e_scattered"), sig("e_added")


    n_use = {"pe": 0, "dve": 0, "act": 0}
    g_dve_in = []
    vec_free = []
    block = ctx.enter_context(nc.Block())

    def step(eng, ins, s):
        ins.then_inc(s.sem, 1)
        s.made += 1
        eng.wait_ge(s.sem, s.made)

    def uses_cols(W, n0, n1):
        v = W[:, n0:n1].rearrange("(j k p) n -> j p k n", j=2, p=P)
        return [[(v[j], 0, n1 - n0)] for j in range(2)]

    def uses_rows(W, per=2):
        v = W.rearrange("(k p) n -> p k n", p=P)
        n = v.shape[1]
        return [[(v[:, k:k + per], None, per)] for k in range(0, n, per)]

    def uses_pair(Wg, Wu, ch):
        g = Wg[:, ch * CH2:(ch + 1) * CH2].rearrange("(j k p) n -> j p k n", j=2, p=P)
        u = Wu[:, ch * CH2:(ch + 1) * CH2].rearrange("(j k p) n -> j p k n", j=2, p=P)
        return [[(g[j], 0, CH2), (u[j], CH2, CH2)] for j in range(2)]

    def uses_down(Wd):
        v = Wd.rearrange("(k p) n -> p k n", p=P)
        got, k = [], 0
        for m in DOWN2:
            got.append([(v[:, k:k + m], None, m)])
            k += m
        return got

    IN_CHUNKS = [(n, min(n + 512, D_IN)) for n in range(0, D_IN, 512)]
    IN2_CHUNKS = [(0, 512), (512, 1024), (1024, 1536), (1536, 2048), (2048, 2560), (2560, 3072), (3072, D_IN2)]
    SEQ2 = [0, 1, 2, 3, 5, 6, 4]

    TILES = []
    for l in range(DEPTH):
        for n0, n1 in IN_CHUNKS:
            TILES += uses_cols(w["w_in"][l], n0, n1)
        TILES += uses_rows(w["w_out"][l])
        for n0 in range(0, D_FF, 512):
            TILES += uses_cols(w["w_mlp_up"][l], n0, n0 + 512)
        TILES += uses_rows(w["w_mlp_down"][l]) + uses_rows(w["w_ple_proj"][l]) + uses_rows(w["w_ple_gate"][l])
    for l in range(DEPTH):
        for i in SEQ2:
            TILES += uses_cols(w["w_in_2"][l], *IN2_CHUNKS[i])
        TILES += uses_rows(w["w_out_2"][l])
        if l == 0:
            for ch in range(NCH2):
                TILES += uses_pair(w["ffn_w_gate_2"][0], w["ffn_w_up_2"][0], ch)
            TILES += uses_rows(w["ffn_w_down_2"][0])
    U0 = len(TILES)

    def floats_of(use):
        return sum(m * D if c0 is None else 4 * m for _, c0, m in use)

    def e_floats(j):
        return SLOT if j < 2 * NCH2 else DOWN2[j - 2 * NCH2] * D

    def of_dve(m):
        return m * 11 // 32 * 2

    def slot_cols_of(buf, slot, width):
        return buf[:, slot, 0:4 * width].rearrange("p (k n) -> p k n", k=4)

    def slot_rows_of(buf, slot, n):
        return buf[:, slot, 0:n * D].rearrange("p (k n) -> p k n", k=n)

    slot_before = [16 * sum(len(TILES[n]) for n in range(U0) if n % R == q) for q in range(R)]
    slot_turn = [sum((32 if j < 2 * NCH2 else 16) for j in range(USES_E) if (U0 + j) % R == q) for q in range(R)]

    @block.sync
    def _(sp):
        sp.dma_start(C[:, :], const_d).then_inc(c_loaded.sem, 16)
        for n, use in enumerate(TILES):
            if n >= R:
                sp.wait_ge(w_used.sem, n - R + 1)
            width = sum(x[2] for x in use)
            for src, c0, m in use:
                dst = slot_rows_of(ring, n % R, m) if c0 is None else slot_cols_of(ring, n % R, width)[:, :, c0:c0 + m]
                sp.dma_start(dst, src).then_inc(w_in_slot[n % R].sem, 16)
        wg = w["moe_w_gate_2"][0]
        wu = w["moe_w_up_2"][0]
        wd = w["moe_w_down_2"][0]

        def expert(i, e):
            for j in range(USES_E):
                n = U0 + j
                sp.wait_ge(w_used.sem, i * USES_E + (n - R + 1))
                if j < 2 * NCH2:
                    ch, half = j // 2, j % 2
                    rows = slice(half * 512, half * 512 + 512)
                    for wm, c0 in ((wg, 0), (wu, CH2)):
                        src = wm[bass.ds(e, 1), rows, ch * CH2:(ch + 1) * CH2].rearrange("e (k p) n -> p (e k) n", p=P)
                        sp.dma_start(slot_cols_of(ring, n % R, 512)[:, :, c0:c0 + CH2], src).then_inc(w_in_slot[n % R].sem, 16)
                else:
                    k0 = sum(DOWN2[:j - 2 * NCH2])
                    m = DOWN2[j - 2 * NCH2]
                    src = wd[bass.ds(e, 1), k0 * P:(k0 + m) * P, :].rearrange("e (k p) n -> p (e k) n", p=P)
                    sp.dma_start(slot_rows_of(ring, n % R, m), src).then_inc(w_in_slot[n % R].sem, 16)

        with sp.Fori(0, NE) as i:
            expert(i, i)
        sp.wait_ge(m_flag.sem, 1)
        over = sp.value_load(FLAG[0:1, 0:1], min_val=0, max_val=1)
        with sp.If(over > 0):
            with sp.Fori(NE, 2 * NE) as i:
                expert(i, i - NE)
        for tb in range(NTB):
            sp.wait_ge(f_out.sem, tb + 1)
            sp.dma_start(out_d[0, tb * P:(tb + 1) * P, :], XN[:, tb, :]).then_inc(out_done.sem, 16)
        sp.wait_ge(out_done.sem, 16 * NTB)

    ORDER = [0, 2, 1, 3]

    def maps(kind, j=0):
        if kind == "a":
            return [(64 * (h % 2), h // 2, 2 + h // 2, 64, A_V + 64 * h, h) for h in ORDER]
        if kind == "b":
            return [(64 * (h % 2), 9 + h // 2, 11 + h // 2, 64, B_V + 64 * h, h) for h in ORDER]
        if kind == "c":
            return [(32 * i, 13 + j, 15 + j, 32, C_V + 64 * (2 * j + i // 2), i // 2) for i in ORDER]
        if kind == "d":
            return [(64 * (h % 2), 17 + h // 2, 19 + h // 2, 64, D_V + 64 * (h // 2), h) for h in ORDER]
        return [(64 * (h % 2), h // 2, 2 + h // 2, 64, C2 + 512 + 64 * h, h) for h in ORDER]

    UNITS = [(kind, j, tb) for kind, js in (("b", 1), ("c", 2), ("d", 1), ("a", 1)) for j in range(js) for tb in range(NTB)]
    UNITS2 = [("e", 0, tb) for tb in range(NTB)]
    DOTS = [(0, 0, 8), (1, 0, 4), (1, 4, 4)]
    DOT_R = PT.rearrange("p k m t -> p (k m t)")

    def dot_map(buf, tb, h):
        nk = P * (tb + 1)
        return buf[:, (h % 2) * 512 + (h // 2) % (4 // (tb + 1)) * nk:][:, 0:nk]

    O_COL = {"a": 0, "b": 256, "c": 512, "d": 768, "e": 768}
    QK_COLS = [A_Q, A_Q + 128, A_K, A_K + 128, A_IQ, A_IQ + 128, A_IQ + 256, A_IQ + 384, ("twice", A_IK),
               B_Q, B_Q + 128, B_K, B_K + 128, C_Q, C_Q + 128, C_K, C_K + 128, D_Q, D_Q + 128, ("twice", D_K), ("twice", D_K + 64)]

    def g_map(u, nk):
        h = G[:, 2 * (u % 2):2 * (u % 2) + 2, :].rearrange("p b (m s) -> p (b m) s", m=2)
        return h[:, :, 0:nk]

    IN_N = len(IN_CHUNKS)
    G_ACT = IN_N + 8 + NTB
    N_LOADED = 16 * 14
    N_ROWS = 16 * 2

    @block.tensor
    def _(pe):
        n_t, n_x = [0, 0], [0, 0]
        t_free = [None, None]
        made = {"dve": 0, "act": 0}
        need = [(0, 0)] * 4

        def weights():
            n = n_use["pe"]
            n_use["pe"] += 1
            pe.wait_ge(w_lo.sem, n + 1)
            pe.wait_ge(w_lo_pool.sem, n + 1)
            return n % H, n % R

        def product(out, ah, al, bh, bl, start, stop, **kw):
            pe.matmul(out, ah, bh, start=start, stop=False, **kw)
            pe.matmul(out, ah, bl, start=False, stop=False, **kw)
            return pe.matmul(out, al, bh, start=False, stop=stop, **kw)

        def banks_free(banks):
            d, a = max(need[b][0] for b in banks), max(need[b][1] for b in banks)
            if d:
                pe.wait_ge(g_dve.sem, d)
            if a:
                pe.wait_ge(g_act.sem, a)

        def chunk_made(banks, by, times=1):
            for e in by:
                made[e] += times
            for b in banks:
                need[b] = (made["dve"], made["act"])

        def bank_free_t(i):
            if t_free[i]:
                pe.wait_ge(t_free[i][0].sem, t_free[i][1])

        def transposes(i, pairs, parts=False):
            bank_free_t(i)
            for dst, src in pairs:
                k = src.shape[0]
                last = pe.transpose(dst, src, ident[0:k, 0:k])
            n = n_x if parts else n_t
            n[i] += 1
            t_free[i] = ((x_taken if parts else t_taken)[i], n[i])
            last.then_inc((x_full if parts else t_full)[i].sem, 1)

        def all_evacuated():
            for i in range(2):
                bank_free_t(i)

        def token_transposes(src, tb):
            for i in range(2):
                transposes(i, [(T[i][:, k * P:(k + 1) * P], src[:, tb, (4 * i + k) * P:(4 * i + k + 1) * P]) for k in range(4)], parts=True)

        def cols_tile(slots, j, tb, width, bank):
            bh, bl = slot_cols_of(ring_hi, slots[0], width), slot_cols_of(ring_lo, slots[1], width)
            toks = slice(tb * P, (tb + 1) * P)
            for k in range(4):
                last = product(G[:, bank, 0:width], xTh[:, 4 * j + k, toks], xTl[:, 4 * j + k, toks], bh[:, k, :], bl[:, k, :],
                               j == 0 and k == 0, j == 1 and k == 3)
            return last

        def rows_tile(slots, m, ah, al, k0, n, tb, out):
            bh, bl = slot_rows_of(ring_hi, slots[0], m), slot_rows_of(ring_lo, slots[1], m)
            toks = slice(tb * P, (tb + 1) * P)
            for k in range(m):
                for h in range(2):
                    cs = slice(h * 512, (h + 1) * 512)
                    last = product(out[:, h, :], ah[:, k0 + k, toks], al[:, k0 + k, toks], bh[:, k, cs], bl[:, k, cs],
                                   k0 + k == 0, k0 + k == n - 1)
            return last

        def g_of(tb):
            return G[:, 2 * tb:2 * tb + 2, :]

        def transposed_in(src, ready, part, between=None):
            ready(0)
            token_transposes(src, 0)
            if between:
                between()
            all_evacuated()
            first = weights()
            part(first, 0, 0)
            ready(1)
            token_transposes(src, 1)
            second = weights()
            part(second, 1, 0)
            all_evacuated()
            part(first, 0, 1).then_inc(w_used.sem, 1)
            part(second, 1, 1).then_inc(w_used.sem, 1)

        def first_cols(src, ready, width, banks, by):
            banks_free(banks)
            transposed_in(src, ready, lambda slots, j, tb: cols_tile(slots, j, tb, width, banks[tb]))
            chunk_made(banks, by)

        def chunk_cols(width, banks, by):
            banks_free(banks)
            for j in range(2):
                slots = weights()
                for tb in range(NTB):
                    last = cols_tile(slots, j, tb, width, banks[tb])
                last.then_inc(w_used.sem, 1)
            chunk_made(banks, by)

        def product_rows(ah, al, n_tiles, by, first=0, times=1):
            if not first:
                banks_free(range(4))
            for t in range(first, n_tiles):
                slots = weights()
                for tb in range(NTB):
                    last = rows_tile(slots, 2, ah, al, 2 * t, 2 * n_tiles, tb, g_of(tb))
                    if t == n_tiles - 1 and tb == 0:
                        last.then_inc(g_half.sem, 1)
                last.then_inc(w_used.sem, 1)
            chunk_made(range(4), by, times)

        def product_tokens(src, ready, by, between=None, times=1):
            banks_free(range(4))
            transposed_in(src, ready, lambda slots, j, tb: rows_tile(slots, 2, xTh, xTl, 2 * j, KT, tb, g_of(tb)), between)
            product_rows(xTh, xTl, KT // 2, by, 2, times)

        def units(us, qkt, pt, v_of, nmaps_of):
            def logits(u):
                kind, j, tb = us[u]
                nk = P * (tb + 1)
                if u >= 2:
                    pe.wait_ge(taken.sem, taken.seen["pe0"] + u - 1)
                out = g_map(u, nk)
                mp = maps(kind, j)
                for n, m in enumerate(ORDER):
                    p0, qb, kb, kd = mp[m][:4]
                    if kind == "c" and n == 2:
                        last.then_inc(pe_own.sem, 1)
                        pe_own.made += 1
                        pe.wait_ge(pe_own.sem, pe_own.made)
                    last = pe.matmul(out[:, m, :], qkt[p0:p0 + kd, qb, tb * P:(tb + 1) * P], qkt[p0:p0 + kd, kb, 0:nk],
                                     start=True, stop=True)
                last.then_inc(scores.sem, 1)

            def prob_transposes(u):
                kind, j, tb = us[u]
                n = 2 if kind == "c" else 4
                lbuf = L if us is UNITS else L2
                s = comb if kind == "c" else probs
                pe.wait_ge(s.sem, s.next("pe"))
                if kind == "c":
                    probs.next("pe")
                for kb in range(tb + 1):
                    transposes(kb, [(T[kb][:, m * P:(m + 1) * P], lbuf[:, u % 2, m, kb * P:(kb + 1) * P])
                                    for m in range(n)])

            def values(u, base):
                kind, j, tb = us[u]
                n = 2 if kind == "c" else 4
                all_evacuated()
                if u >= 2:
                    pe.wait_ge(o_ready.sem, base + u - 1)
                mp = maps(kind, j)
                for m in range(n):
                    vcol, head = mp[m][4:]
                    for kb in range(tb + 1):
                        last = pe.matmul(Sp[:, u % 2, head * 64:(head + 1) * 64], pt[:, kb, m, :], v_of(kb, vcol),
                                         start=(kb == 0), stop=(kb == tb))
                last.then_inc(pv_done.sem, 1)

            taken.seen.setdefault("pe0", 0)
            base = o_ready.seen.get("pe", 0)
            logits(0)
            logits(1)
            for u in range(len(us)):
                prob_transposes(u)
                if u + 2 < len(us):
                    logits(u + 2)
                values(u, base)
            taken.seen["pe0"] += len(us)
            o_ready.seen["pe"] = base + len(us)

        pe.wait_ge(c_loaded.sem, 16)
        for l in range(DEPTH):
            def xn_block(tb):
                pe.wait_ge(xn_ready.sem, xn_ready.next("pe"))

            first_cols(XN, xn_block, IN_CHUNKS[0][1] - IN_CHUNKS[0][0], [0, 1], ("dve", "act"))
            if l == 0:
                pe.wait_ge(rows_loaded.sem, N_ROWS)
                transposes(0, [(T[0][:, 0:N_TAPS], TAPS), (T[0][:, N_TAPS:N_TAPS + 8], ABS)])
            sp2 = Sp[:, :, :].rearrange("p b n -> p (b n)")

            def qk_transposes(blocks):
                for b in blocks:
                    pairs = []
                    for k in range(2 if b < 10 else 1):
                        col = QK_COLS[2 * b + k]
                        for tb in range(NTB):
                            if isinstance(col, tuple):
                                src = IKD[:, {A_IK: 0, D_K: 1, D_K + 64: 2}[col[1]], tb, :]
                            else:
                                src = PROJ[:, tb, col:col + P]
                            pairs.append((T[b % 2][:, k * 256 + tb * P:k * 256 + tb * P + P], src))
                    transposes(b % 2, pairs)

            def index_dots(r):
                tb, h0, n = DOTS[r]
                if r:
                    pe.wait_ge(idx_taken.sem, len(DOTS) * l + r)
                for h in range(h0, h0 + n):
                    p0 = 64 * (h % 2)
                    last = pe.matmul(dot_map(sp2, tb, h), QKT[p0:p0 + 64, 4 + h // 2, tb * P:(tb + 1) * P], QKT[p0:p0 + 64, 8, 0:P * (tb + 1)],
                                     start=True, stop=True)
                last.then_inc(idx_s.sem, 1)

            for i, (n0, n1) in enumerate(IN_CHUNKS):
                b = 2 * (i % 2)
                if i:
                    chunk_cols(n1 - n0, [b, b + 1], ("dve", "act"))
                if i == 3:
                    pe.wait_ge(d2pe.sem, d2pe.next("pe"))
                    qk_transposes(range(5))
                if i == 4:
                    all_evacuated()
                if i >= 4:
                    index_dots(i - 4)
            pe.wait_ge(d2pe.sem, d2pe.next("pe"))
            qk_transposes(range(5, 8))
            banks_free(range(4))
            up = c("upper1")
            pe.matmul(G[:, 0, 0:4], up[:, 0:P], LF[:, 0, :], start=True, stop=True)
            pe.matmul(G[:, 0, 4:8], up[:, P:2 * P], LF[:, 0, :], start=True, stop=False)
            pe.matmul(G[:, 0, 4:8], up[:, 0:P], LF[:, 1, :], start=False, stop=True)
            gb = G[:, 2:4, :].rearrange("p b (m s) -> p (b m) s", m=2)
            for h in range(4):
                pe.matmul(gb[:, h, :], LF[:, 0, h:h + 1].to_broadcast([P, P]), up, start=True, stop=False)
                last = pe.matmul(gb[:, h, P:2 * P], LF[:, 1, h:h + 1].to_broadcast([P, P]), up[:, 0:P], start=False, stop=True)
            last.then_inc(pe2d.sem, 1)
            pe.wait_ge(p2pe.sem, p2pe.next("pe"))
            qk_transposes(range(8, 11))
            all_evacuated()
            pe.wait_ge(d2pe.sem, d2pe.next("pe"))
            pe.wait_ge(idx_taken.sem, len(DOTS) * (l + 1))
            units(UNITS, QKT, PT, lambda kb, vcol: PROJ[:, kb, vcol:vcol + 64], None)
            def o_block(tb):
                pe.wait_ge(o_ready.sem, o_ready.seen["pe"] - 1 + tb)

            product_tokens(XN, o_block, ("dve",))
            def hidden(ch):
                pe.wait_ge(hb_ready.sem, hb_ready.next("pe"))
                for j in range(2):
                    transposes(j, [(T[j][:, k * 256 + tb * P:k * 256 + tb * P + P],
                                    HB[:, ch % 2, tb, (2 * j + k) * P:(2 * j + k + 1) * P]) for k in range(2) for tb in range(NTB)], parts=True)

            for ch in range(8):
                b = 2 * (ch % 2)
                if ch:
                    chunk_cols(512, [b, b + 1], ("act",))
                else:
                    first_cols(XN, xn_block, 512, [0, 1], ("act",))
                if ch:
                    hidden(ch - 1)
            hidden(7)
            pe.wait_ge(misc_loaded.sem, 16 * (l + 1))
            transposes(0, [(T[0][:, k * 256 + tb * P:k * 256 + tb * P + P], PLE[:, tb, k * P:(k + 1) * P])
                           for k in range(2) for tb in range(NTB)], parts=True)
            all_evacuated()
            product_rows(hTh, hTl, 16, ("dve",))
            embed = weights()
            rows_tile(embed, 2, PLETh, PLETl, 0, 2, 0, Sp).then_inc(pe2a.sem, 1)

            def embed_second():
                pe.wait_ge(a2pe.sem, a2pe.next("pe"))
                last = rows_tile(embed, 2, PLETh, PLETl, 0, 2, 1, Sp)
                last.then_inc(w_used.sem, 1)

            def x_block(tb):
                pe.wait_ge(d2pe.sem, d2pe.next("pe"))

            product_tokens(X, x_block, ("act",), embed_second, NTB)

        for l in range(DEPTH):
            first_cols(X, x_block, IN2_CHUNKS[0][1] - IN2_CHUNKS[0][0], [0, 1], ("act",))
            ones = c("upper1")[:, P:2 * P]
            for q, i in enumerate(SEQ2):
                n0, n1 = IN2_CHUNKS[i]
                b = 2 * (q % 2)
                if 1 <= i <= 3:
                    banks_free([b, b + 1])
                    out = G[:, b:b + 2, :].rearrange("p b (m s) -> p (b m) s", m=2)
                    for j in range(2):
                        sh, sl = weights()
                        wh, wl = slot_cols_of(ring_hi, sh, 512), slot_cols_of(ring_lo, sl, 512)
                        for m in range(4):
                            ms_ = slice(m * P, (m + 1) * P)
                            for k in range(4):
                                first = j == 0 and k == 0
                                last = product(out[:, m, :], wh[:, k, ms_], wl[:, k, ms_], xTh[:, 4 * j + k, :], xTl[:, 4 * j + k, :],
                                               first and m % 2 == 0, j == 1 and k == 3, skip_group_check=True)
                        last.then_inc(w_used.sem, 1)
                    chunk_made([b, b + 1], ("dve", "act"))
                elif q:
                    chunk_cols(n1 - n0, [b, b + 1], ("act",) if i == 4 else ("dve", "act"))
                if i == 1:
                    pe.wait_ge(misc_loaded.sem, 16 * (DEPTH + l + 1))
                    transposes(0, [(T[0][:, g * P:(g + 1) * P], WSA[:, g, :]) for g in range(4)])
                if i == 2:
                    bank_free_t(0)
                    for g in range(4):
                        last = pe.matmul(Sp[:, 0, g * P:(g + 1) * P], WST[:, g, :], P2[:, :, A2 + 256 + g * 64:A2 + 256 + (g + 1) * 64],
                                         start=True, stop=True)
                    last.then_inc(pe2d.sem, 1)
                if i in (3, 5):
                    if i == 3:
                        pe.wait_ge(d2pe.sem, d2pe.next("pe"))
                    pe.wait_ge(a2pe.sem, a2pe.next("pe"))
                    for b in range(2):
                        o_ = (b + (2 if i == 5 else 0)) * 512
                        last = pe.matmul(Sp[:, b, :], ones, SQ[:, o_:o_ + 512], start=True, stop=True)
                    last.then_inc(pe2a.sem, 1)
                if i == 6:
                    pe.wait_ge(d2pe.sem, d2pe.next("pe"))
                    bank_free_t(0)
                    for tb in range(NTB):
                        pe.matmul(T[0][:, tb * 4:tb * 4 + 4], c("chunk_upper"), GL[:, tb, :], start=True, stop=True)
                    for tb in range(NTB):
                        last = pe.matmul(T[0][:, 8 + tb * 4:12 + tb * 4], c("chunk_ones"), GL[:, tb, :], start=True, stop=True)
                    n_t[0] += 1
                    t_free[0] = (t_taken[0], n_t[0])
                    last.then_inc(t_full[0].sem, 1)
                    for tb in range(NTB):
                        for h in range(H2):
                            last = pe.matmul(Sp[:, tb, h * P:(h + 1) * P], GL[:, tb, h:h + 1].to_broadcast([P, P]), c("chunk_upper"),
                                             start=True, stop=True)
                    last.then_inc(pe2d.sem, 1)
                    for tb in (1, 0):
                        bank_free_t(tb)
                        for h in range(H2):
                            last = pe.matmul(T[tb][:, h * P:(h + 1) * P], BETA[:, tb, h:h + 1].to_broadcast([P, P]), ident,
                                             start=True, stop=True)
                        t_free[tb] = (beta_taken, l + 1)
                    last.then_inc(pe2d.sem, 1)
            banks_free([2, 3])
            for i in range(8):
                tb, h = i // 4, i % 4
                kT_ = CV[:, 4 + h, tb * P:(tb + 1) * P]
                last = pe.matmul(G[:, 2 + tb, h * P:(h + 1) * P], kT_, kT_, start=True, stop=True)
            last.then_inc(pe2d.sem, 1)
            banks_free([0, 1])
            for i in range(8):
                tb, h = i // 4, i % 4
                last = pe.matmul(G[:, tb, h * P:(h + 1) * P], CV[:, 4 + h, tb * P:(tb + 1) * P], CV[:, h, tb * P:(tb + 1) * P], start=True, stop=True)
            last.then_inc(pe2a.sem, 1)
            for tb in range(NTB):
                if tb == 0:
                    pe.wait_ge(d2pe.sem, d2pe.next("pe"))
                else:
                    pe.wait_ge(lv_done.sem, lv_done.next("pe"))
                transposes(tb, [(T[tb][:, h * P:(h + 1) * P], TT[:, tb * 4 + h, :]) for h in range(H2)])
            lv_done.next("pe", LEVELS - 3)
            all_evacuated()
            pe.wait_ge(a2pe.sem, a2pe.next("pe"))
            for lv in range(1, LEVELS):
                pe.wait_ge(p2pe.sem, p2pe.next("pe"))
                for tb in range(NTB):
                    if lv > 1:
                        pe.wait_ge(d2pe.sem, d2pe.next("pe", 1 + tb))
                    for h in range(H2):
                        last = pe.matmul(G[:, tb, h * P:(h + 1) * P], MLV[lv % 2][:, 4 * tb + h, :], TN[:, 4 * tb + h, :], start=True, stop=True)
                    last.then_inc(pe2a.sem, 1)
                for tb in range(NTB):
                    pe.wait_ge(a2pe.sem, a2pe.next("pe"))
                    if lv > 1 and tb == 1:
                        pe.wait_ge(d2pe.sem, d2pe.next("pe"))
                    for h in range(H2):
                        i, cs = 4 * tb + h, slice(h * P, (h + 1) * P)
                        if lv < LEVELS - 1:
                            pe.matmul(G[:, 2 + tb, cs], TT[:, i, :], WB[:, i, :], start=True, stop=True)
                        last = pe.matmul(Sp[:, tb, cs], WB[:, i, :], TT[:, i, :], start=True, stop=True)
                    last.then_inc(pe2d.sem, 1)
                if lv <= NTB:
                    tb = lv - 1
                    transposes(0, [(T[0][:, h * P:(h + 1) * P], CV[:, 4 + h, tb * P:(tb + 1) * P]) for h in range(H2)])
                    transposes(1, [(T[1][:, h * P:(h + 1) * P], CV[:, 8 + h, tb * P:(tb + 1) * P]) for h in range(H2)])
            pe.wait_ge(d2pe.sem, d2pe.next("pe", 2))
            all_evacuated()
            for i in range(8):
                cs = slice((i % 4) * P, (i % 4 + 1) * P)
                last = pe.matmul(G[:, i // 4, cs], TT[:, i, :], VB[:, i, :], start=True, stop=True)
            last.then_inc(pe2d.sem, 1)
            for i in range(8):
                cs = slice((i % 4) * P, (i % 4 + 1) * P)
                last = pe.matmul(G[:, 2 + i // 4, cs], KBE[:, i, :], TT[:, i, :], start=True, stop=True)
            last.then_inc(pe2a.sem, 1)
            pe.wait_ge(d2pe.sem, d2pe.next("pe"))
            pe.wait_ge(a2pe.sem, a2pe.next("pe"))
            for tb in range(NTB):
                for half in range(2):
                    rows = slice(half * CHUNK, (half + 1) * CHUNK)
                    toks = slice(tb * P + half * CHUNK, tb * P + (half + 1) * CHUNK)
                    for h in range(H2):
                        last = pe.matmul(G[:, 0, h * P:(h + 1) * P], WTs[:, tb * 4 + h, :], ST[:, h, :], start=True, stop=True)
                    last.then_inc(pe2d.sem, 1)
                    for h in range(H2):
                        pe.matmul(Sp[rows, tb, h * P:(h + 1) * P], CV[:, h, toks], ST[:, h, :],
                                  start=(h == 0), stop=False, skip_group_check=True)
                    pe.wait_ge(d2pe.sem, d2pe.next("pe"))
                    if not (tb == 1 and half == 1):
                        for h in range(H2):
                            last = pe.matmul(G[:, 1, h * P:(h + 1) * P], KD[rows, tb * 4 + h, :], DT[rows, tb * 4 + h, :],
                                             start=True, stop=True)
                        last.then_inc(pe2d.sem, 1)
                    if half == 1:
                        for h in range(H2):
                            last = pe.matmul(Sp[:, tb, h * P:(h + 1) * P], AT_[:, tb * 4 + h, :], DT[:, tb * 4 + h, :],
                                             start=False, stop=True, skip_group_check=True)
                        last.then_inc(pe2a.sem, 1)
                    if not (tb == 1 and half == 1):
                        pe.wait_ge(d2pe.sem, d2pe.next("pe"))
            for b in range(2):
                transposes(b, [(T[b][:, k * 256 + tb * P:k * 256 + tb * P + P], P2[:, tb, C2 + (2 * b + k) * P:C2 + (2 * b + k + 1) * P])
                               for k in range(2) for tb in range(NTB)])
            all_evacuated()
            units(UNITS2, QKT2, PT2, lambda kb, vcol: P2[:, kb, vcol:vcol + 64], None)
            product_tokens(XN, o_block, ("dve",))
            if l == 0:
                def hidden2(ch):
                    pe.wait_ge(hb_ready.sem, hb_ready.next("pe"))
                    i = ch % 2
                    transposes(i, [(T[i][:, k * 256 + tb * P:k * 256 + tb * P + P], HB2[:, i, tb, k * P:(k + 1) * P])
                                   for k in range(2) for tb in range(NTB)], parts=True)

                for ch in range(NCH2):
                    b = 2 * (ch % 2)
                    if ch:
                        chunk_cols(512, [b, b + 1], ())
                    else:
                        first_cols(X, x_block, 512, [0, 1], ())
                    if ch:
                        hidden2(ch - 1)
                hidden2(NCH2 - 1)
                all_evacuated()
                product_rows(hT2h, hT2l, FT2 // 2, ("dve",))

        for tb in range(NTB):
            x_block(tb)
            token_transposes(X, tb)
            all_evacuated()
            for k in range(KT):
                toks = slice(tb * P, (tb + 1) * P)
                last = product(Sp[:, 0, tb * 8:tb * 8 + 8], xTh[:, k, toks], xTl[:, k, toks], RWh[:, k, :], RWl[:, k, :], k == 0, k == KT - 1)
        last.then_inc(pe2d.sem, 1)
        pe.wait_ge(d2pe.sem, d2pe.next("pe"))
        ones = c("upper1")[:, P:2 * P]
        pe.matmul(Sp[:, 1, 0:8], c("before"), ANY[:, 0, :], start=True, stop=True)
        pe.matmul(Sp[:, 1, 8:16], ones, ANY[:, 0, :], start=True, stop=False)
        pe.matmul(Sp[:, 1, 8:16], c("before"), ANY[:, 1, :], start=False, stop=True)
        pe.matmul(Sp[:, 1, 16:24], ones, ANY[:, 0, :], start=True, stop=False)
        last = pe.matmul(Sp[:, 1, 16:24], ones, ANY[:, 1, :], start=False, stop=True)
        last.then_inc(pe2d.sem, 1)

        def gather():
            g8 = Sp[:, :, :].rearrange("p b (k j) -> p (b k) j", k=4)
            for k in range(KT):
                for tb in range(NTB):
                    last = pe.matmul(g8[:, k, :], X[:, tb, k * P:(k + 1) * P], Pm[:, tb, :], start=(tb == 0), stop=(tb == 1))
            last.then_inc(m_g.sem, 1)

        def scatter(tb):
            for h in range(2):
                cs = slice(h * 512, (h + 1) * 512)
                pe.matmul(Sp[:, h, :], PmT[:, tb, :], YBh[:, cs], start=True, stop=False)
                last = pe.matmul(Sp[:, h, :], PmT[:, tb, :], YBl[:, cs], start=False, stop=True)
            last.then_inc(m_sc.sem, 1)

        banks_free(range(4))
        pe.wait_ge(m_p.sem, 1)
        gather()
        assert n_use["pe"] == U0

        def expert_pe(i):
            def w_slots(j):
                pe.wait_ge(w_lo.sem, i * USES_E + (U0 + j + 1))
                pe.wait_ge(w_lo_pool.sem, i * USES_E + (U0 + j + 1))
                return (U0 + j) % H, (U0 + j) % R

            def hidden_e(ch):
                pe.wait_ge(m_hb.sem, i * NCH2 + (ch + 1))
                k = ch % 2
                if ch >= 2:
                    pe.wait_ge(m_tt[k].sem, 6 * i + (ch // 2))
                for q in range(2):
                    last = pe.transpose(T[k][:, q * P:(q + 1) * P], HB2[:, k, 0, q * P:(q + 1) * P], ident)
                last.then_inc(m_tf[k].sem, 1)

            pe.wait_ge(m_gd.sem, i + 1)
            for ch in range(NCH2):
                if ch >= 2:
                    pe.wait_ge(m_hb.sem, i * NCH2 + (ch - 1))
                for j in range(2):
                    sh, sl = w_slots(2 * ch + j)
                    bh, bl = slot_cols_of(ring_hi, sh, 512), slot_cols_of(ring_lo, sl, 512)
                    for k in range(4):
                        last = product(G[:, ch % 2, :], xgTh[:, 4 * j + k, :], xgTl[:, 4 * j + k, :], bh[:, k, :], bl[:, k, :],
                                       j == 0 and k == 0, j == 1 and k == 3)
                    last.then_inc(w_used.sem, 1)
                if ch:
                    hidden_e(ch - 1)
                if ch == 1:
                    pe.wait_ge(m_y.sem, i + 1)
                    scatter(0)
                if ch == 4:
                    pe.wait_ge(m_acc.sem, 2 * i + 2)
                    scatter(1)
            k0 = 0
            for q, m in enumerate(DOWN2):
                if q == len(DOWN2) - 1:
                    pe.wait_ge(m_tt[0].sem, 6 * i + 6)
                sh, sl = w_slots(2 * NCH2 + q)
                bh, bl = slot_rows_of(ring_hi, sh, m), slot_rows_of(ring_lo, sl, m)
                for k in range(m):
                    for h in range(2):
                        cs = slice(h * 512, (h + 1) * 512)
                        last = product(G[:, 2 + h, :], hEh[:, k0 + k, :], hEl[:, k0 + k, :], bh[:, k, cs], bl[:, k, cs],
                                       k0 + k == 0, k0 + k == FT2 - 1)
                last.then_inc(w_used.sem, 1)
                k0 += m
                if q == 0:
                    hidden_e(NCH2 - 1)
                    pe.wait_ge(m_tt[1].sem, 6 * i + 5)
                    for tb in range(NTB):
                        last = pe.transpose(T[1][:, tb * P:(tb + 1) * P], Pm[:, tb, :], ident)
                    last.then_inc(m_tf[1].sem, 1)
                if q == GATHER_AT:
                    pe.wait_ge(m_acc.sem, 2 * i + 3)
                    pe.wait_ge(m_p.sem, i + 2)
                    gather()
            pe.wait_ge(m_tt[1].sem, 6 * i + 6)

        with pe.Fori(0, NE) as i:
            expert_pe(i)
        pe.wait_ge(m_flag.sem, 1)
        over = pe.value_load(FLAG[0:1, 0:1], min_val=0, max_val=1)
        with pe.If(over > 0):
            with pe.Fori(NE, 2 * NE) as i:
                expert_pe(i)
        n_all = pe.value_load(FLAG[0:1, 1:2], min_val=NE, max_val=2 * NE)
        for tb in range(NTB):
            if tb == 0:
                pe.wait_ge(m_y.sem, n_all + 1)
                pe.wait_ge(m_gd.sem, n_all + 1)
                pe.wait_ge(m_tt[1].sem, n_all * 6)
            pe.wait_ge(m_acc.sem, n_all * 2 + (1 + tb))
            scatter(tb)

    @block.scalar
    def _(act):
        n_t, n_x = [0], [0, 0]
        slot_count = [0] * R
        n_hi = [0]

        def high_parts(upto):
            while n_hi[0] < min(upto, U0):
                n = n_hi[0]
                n_hi[0] += 1
                m = floats_of(TILES[n])
                slot_count[n % R] += 16 * len(TILES[n])
                act.wait_ge(w_in_slot[n % R].sem, slot_count[n % R])
                if n >= H:
                    act.wait_ge(w_used.sem, n - H + 1)
                nc.scalar.activation(ring_hi[:, n % H, 0:m], ring[:, n % R, 0:m], ACT.Copy).then_inc(w_hi.sem, 1)

        def met(n, ahead=H - 1):
            n_use["act"] += n
            high_parts(n_use["act"] + ahead)

        def full(n, ahead=H - 1):
            met(n, ahead)
            act.wait_ge(w_used.sem, n_use["act"])

        def evac(dst):
            n_t[0] += 1
            act.wait_ge(t_full[1].sem, n_t[0])
            n = dst.free_size()
            nc.scalar.activation(dst, T[1][:, 0:n].rearrange("p (k s) -> p k s", k=dst.shape[1]), ACT.Copy).then_inc(t_taken[1].sem, 1)

        def high_evac(i, dst):
            n_x[i] += 1
            act.wait_ge(x_full[i].sem, n_x[i])
            nc.scalar.activation(dst, T[i][:, :].rearrange("p (k s) -> p k s", k=dst.shape[1]), ACT.Copy).then_inc(x_hi[i].sem, 1)

        def block_evac(tb):
            for i in range(2):
                high_evac(i, xTh[:, 4 * i:4 * i + 4, tb * P:(tb + 1) * P])

        def token_evac():
            for tb in range(NTB):
                block_evac(tb)

        def mean_square(src, tb):
            nc.scalar.activation(XN[:, tb, :], src, ACT.Square, scale=D ** -0.5, accum_out=ssq[:, tb:tb + 1]).then_inc(s_ssq.sem, 1)

        def mean_squares_of_product(n):
            met(n)
            for tb in range(NTB):
                if tb == 0:
                    act.wait_ge(g_half.sem, g_half.next("act"))
                else:
                    act.wait_ge(w_used.sem, n_use["act"])
                mean_square(G[:, 2 * tb:2 * tb + 2, :].rearrange("p b n -> p (b n)"), tb)

        def mean_squares_of_x():
            for tb in range(NTB):
                act.wait_ge(d2a.sem, d2a.next("act"))
                mean_square(X[:, tb, :], tb)

        def units(us, lbuf, pt):
            def exps(u):
                kind, j, tb = us[u]
                nk = P * (tb + 1)
                act.wait_ge(maxed.sem, maxed.next("act"))
                if kind == "d":
                    nc.scalar.activation(esk[:, u % 2, :], esk[:, u % 2, :], ACT.Exp)
                for m in range(4):
                    last = nc.scalar.activation(lbuf[:, u % 2, m, 0:nk], lbuf[:, u % 2, m, 0:nk], ACT.Exp,
                                                bias=nmx[:, u % 2, m:m + 1], accum_out=rsum[:, u % 2, m:m + 1])
                last.then_inc(probs.sem, 1)

            exps(0)
            exps(1)
            for u in range(len(us)):
                if us[u][2] == 1:
                    evac(pt[:, 1, 0:2 if us[u][0] == "c" else 4, :])
                if u + 2 < len(us):
                    exps(u + 2)
                if us is UNITS and u == 6:
                    met(0)

        act.dma_start(X[:, :, :], w["x"][0].rearrange("(t p) d -> p t d", p=P)).then_inc(x_loaded.sem, 16)

        def load(dst, src):
            act.dma_start(dst, src, allow_slow_non_contiguous=True).then_inc(loaded.sem, 16)

        load(POS[:, :], w["positions"][0].rearrange("(t p) -> p t", p=P))
        for q, name in enumerate(("lambda_q1", "lambda_k1", "lambda_q2", "lambda_k2")):
            load(p_lam[:, q], w[name].partition_broadcast(P))
        load(p_sink, w["sinks"].rearrange("l h -> (l h)").partition_broadcast(P))
        load(p_sub, w["diff_subln"].partition_broadcast(P))
        load(p_bf, w["b_forget"].rearrange("l h -> (l h)").partition_broadcast(P))
        load(p_alog, w["b_a_log_2"].rearrange("l h -> (l h)").partition_broadcast(P))
        load(p_dt, w["b_dt_bias_2"].rearrange("l h -> (l h)").partition_broadcast(P))
        load(p_bn, w["b_norm_g_2"].partition_broadcast(P))
        load(ALN[:, 0], w["a_ln_g_2"].partition_broadcast(P))
        load(ALN[:, 1], w["a_ln_b_2"].partition_broadcast(P))
        load(RW[:, :, :], w["moe_router_2"][0].rearrange("(k p) e -> p k e", p=P))
        act.dma_start(TAPS, w["conv_w_2"].rearrange("l j (b p) -> (l j b) p", p=P)).then_inc(rows_loaded.sem, 16)
        act.dma_start(ABS, w["a_bs_2"].rearrange("l g t -> (l g) t")).then_inc(rows_loaded.sem, 16)
        for l in range(DEPTH):
            if l:
                mean_squares_of_x()
            else:
                act.wait_ge(x_loaded.sem, 16)
                for tb in range(NTB):
                    mean_square(X[:, tb, :], tb)
                high_parts(H - 1)
            token_evac()
            if l == 0:
                act.wait_ge(d2a.sem, d2a.next("act"))
                nc.scalar.activation(RWh[:, :, :], RW[:, :, :], ACT.Copy)
                nc.scalar.activation(lamt, lamt, ACT.Exp)
                nc.scalar.activation(SN[:, :, :], KK_[:, :, :], ACT.Sin)
                nc.scalar.activation(SH[:, :, :], KK_[:, :, :], ACT.Sin, scale=0.5).then_inc(a2d.sem, 1)
            for i, (n0, n1) in enumerate(IN_CHUNKS):
                full(2, H - 1 if i < IN_N - 1 else 0)
                nc.scalar.activation(PROJ[:, 1, n0:n1], G[:, 2 * (i % 2) + 1, 0:n1 - n0], ACT.Copy).then_inc(g_act.sem, 1)
                if i == 3:
                    for b in (1, 3):
                        evac(QKT[:, 2 * b:2 * b + 2, :])
                if i == 5:
                    act.wait_ge(d2a.sem, d2a.next("act"))
                    step(act, nc.scalar.activation(GL[:, :, :], GL[:, :, :], ACT.Abs), astep)
                    step(act, nc.scalar.activation(GL[:, :, :], GL[:, :, :], ACT.Exp, scale=-1.0), astep)
                    nc.scalar.activation(GL[:, :, :], GL[:, :, :], ACT.Ln, bias=c("one")).then_inc(a2d.sem, 1)
                if i >= 4:
                    act.wait_ge(idx_s.sem, idx_s.next("act"))
                    if i > 4:
                        act.wait_ge(d2a.sem, d2a.next("act"))
                    nc.scalar.activation(DOT_R, Sp[:, :, :].rearrange("p b n -> p (b n)"), ACT.Relu).then_inc(idx_taken.sem, 1)
            for b in (5, 7, 9):
                evac(QKT[:, 2 * b:2 * b + 2, :])
            units(UNITS, L, PT)
            token_evac()
            mean_squares_of_product(4)
            mean_squares_of_x()
            token_evac()
            for ch in range(9):
                if ch < 8:
                    full(2)
                    b = 2 * (ch % 2)
                    nc.scalar.activation(HB[:, ch % 2, :, :], G[:, b:b + 2, :], ACT.Relu).then_inc(g_act.sem, 1)
                if ch:
                    for j in range(2):
                        high_evac(j, hTh[:, 4 * ch - 4 + 2 * j:4 * ch - 2 + 2 * j, :])
            high_evac(0, PLETh[:, :, :])
            mean_squares_of_product(16)
            met(1)
            for tb in range(NTB):
                if tb == 0:
                    act.wait_ge(pe2a.sem, pe2a.next("act"))
                else:
                    act.wait_ge(w_used.sem, n_use["act"])
                nc.scalar.activation(PLR[:, tb, :], Sp[:, :, :].rearrange("p b n -> p (b n)"), ACT.Copy).then_inc((a2d if tb else a2pe).sem, 1)
                block_evac(tb)
            met(4)
            for tb in range(NTB):
                if tb == 0:
                    act.wait_ge(g_half.sem, g_half.next("act"))
                else:
                    act.wait_ge(w_used.sem, n_use["act"])
                nc.scalar.activation(XN[:, tb, :], G[:, 2 * tb:2 * tb + 2, :].rearrange("p b n -> p (b n)"), ACT.Sigmoid).then_inc(g_act.sem, 1)

        for l in range(DEPTH):
            token_evac()
            def norms(o_):
                act.wait_ge(pe2a.sem, pe2a.next("act"))
                sq = SQ[:, o_:o_ + 1024]
                step(act, nc.scalar.activation(sq, Sp[:, :, :].rearrange("p b n -> p (b n)"), ACT.Ln, bias=c("eps")), astep)
                nc.scalar.activation(sq, sq, ACT.Exp, scale=-0.5).then_inc(a2d.sem, 1)

            def conv_silu(g):
                act.wait_ge(d2a.sem, d2a.next("act"))
                cv = CV[:, 4 * g:4 * g + 4, :]
                step(act, nc.scalar.activation(cv, cv, ACT.Silu), astep)
                if g < 2:
                    nc.scalar.activation(SQ[:, 1024 * g:1024 * (g + 1)], cv.rearrange("p b s -> p (b s)"), ACT.Square).then_inc(a2pe.sem, 1)

            for q, i in enumerate(SEQ2):
                n0, n1 = IN2_CHUNKS[i]
                b = 2 * (q % 2)
                full(2, H - 1 if q < len(SEQ2) - 1 else 0)
                if i in (0, 4):
                    for tb in range(NTB):
                        o_ = A2 if i == 0 else Z2
                        last = nc.scalar.activation(P2[:, tb, o_:o_ + 512], G[:, b + tb, :], ACT.Gelu_apprx_tanh if i == 0 else ACT.Silu)
                    last.then_inc(g_act.sem, 1)
                elif i <= 3:
                    nc.scalar.activation(PAD[:, 4 * (i - 1) + 2:4 * i, 3:], G[:, b + 1, :].rearrange("p (m s) -> p m s", m=2), ACT.Copy).then_inc(g_act.sem, 1)
                else:
                    o_ = BA2 + (n0 - 2560)
                    nc.scalar.activation(P2[:, 1, o_:o_ + n1 - n0], G[:, b + 1, 0:n1 - n0], ACT.Copy).then_inc(g_act.sem, 1)
                if i == 2:
                    conv_silu(0)
                if i == 3:
                    norms(0)
                    conv_silu(1)
                if i == 5:
                    norms(1024)
                    act.wait_ge(d2a.sem, d2a.next("act"))
                    nc.scalar.activation(BETA[:, :, :], P2[:, :, BA2:BA2 + 4], ACT.Sigmoid)
                    step(act, nc.scalar.activation(GL[:, :, :], GL[:, :, :], ACT.Abs), astep)
                    step(act, nc.scalar.activation(GL[:, :, :], GL[:, :, :], ACT.Exp, scale=-1.0), astep)
                    nc.scalar.activation(ea4, p_alog[:, 4 * l:4 * l + 4], ACT.Exp)
                    nc.scalar.activation(GL[:, :, :], GL[:, :, :], ACT.Ln, bias=c("one")).then_inc(a2d.sem, 1)
                if i == 6:
                    conv_silu(2)
                    act.wait_ge(d2a.sem, d2a.next("act"))
                    nc.scalar.activation(kds8, ms8, ACT.Exp)
                    nc.scalar.activation(eg8, gc16[:, 0:8], ACT.Exp)
                    for half in range(2):
                        nc.scalar.activation(EGL[:, :, :, half], Sp[:, :, :].rearrange("p t (h s) -> p t h s", h=4)[:, :, :, half * CHUNK + CHUNK - 1], ACT.Exp)
                    nc.scalar.activation(EGB[:, :, :], Sp[:, :, :], ACT.Exp)
                    nc.scalar.activation(DT, DT, ACT.Exp).then_inc(a2d.sem, 1)
            act.wait_ge(pe2a.sem, pe2a.next("act"))
            nc.scalar.activation(AT_[:, :, :], G[:, 0:2, :].rearrange("p b (i t) -> p (b i) t", i=4), ACT.Copy).then_inc(a2pe.sem, 1)
            evac(TN[:, 4:8, :])
            for lv in range(1, LEVELS):
                for tb in range(NTB):
                    act.wait_ge(pe2a.sem, pe2a.next("act"))
                    nc.scalar.activation(WB[:, 4 * tb:4 * tb + 4, :], G[:, tb, :].rearrange("p (i t) -> p i t", i=4), ACT.Copy).then_inc(a2pe.sem, 1)
                if lv <= NTB:
                    tb = lv - 1
                    n_t[0] += 1
                    act.wait_ge(t_full[1].sem, n_t[0])
                    for h in range(H2):
                        last = nc.scalar.activation(VB[:, tb * 4 + h, :], T[1][:, h * P:(h + 1) * P], ACT.Copy, scale=BETA[:, tb, h:h + 1])
                    last.then_inc(t_taken[1].sem, 1)
                elif lv == NTB + 1:
                    met(0)
            act.wait_ge(pe2a.sem, pe2a.next("act"))
            nc.scalar.activation(WTs[:, :, :], G[:, 2:4, :].rearrange("p b (i t) -> p (b i) t", i=4), ACT.Copy).then_inc(a2pe.sem, 1)
            for tb in range(NTB):
                act.wait_ge(pe2a.sem, pe2a.next("act"))
                nc.scalar.activation(SQ[:, tb * 512:(tb + 1) * 512], Sp[:, tb, :], ACT.Square).then_inc(a2d.sem, 1)
            evac(QKT2[:, 2:4, :])
            units(UNITS2, L2, PT2)
            token_evac()
            met(4)
            if l == 0:
                token_evac()
                for ch in range(NCH2 + 1):
                    if ch < NCH2:
                        full(2)
                        if ch >= 2:
                            act.wait_ge(hb_ready.sem, 8 * DEPTH + ch - 1)
                        b = 2 * (ch % 2)
                        nc.scalar.activation(HS[:, ch % 2, :, :], G[:, b:b + 2, 0:CH2], ACT.Silu).then_inc(silu_ready.sem, 1)
                    if ch:
                        high_evac((ch - 1) % 2, hT2h[:, 2 * ch - 2:2 * ch, :])
                met(FT2 // 2)

        token_evac()
        act.wait_ge(d2a.sem, d2a.next("act"))
        nc.scalar.activation(PR[:, :, 0:1], PR[:, :, 0:1], ACT.Exp).then_inc(a2d.sem, 1)

        def gather_act(i):
            act.wait_ge(m_g.sem, i + 1)
            nc.scalar.activation(xgTh[:, :, :], Sp[:, :, :].rearrange("p b (k j) -> p (b k) j", k=4), ACT.Copy).then_inc(m_ga.sem, 1)

        def result(n):
            act.wait_ge(w_used.sem, n * USES_E + U0)
            nc.scalar.activation(YBh[:, :], G[:, 2:4, :].rearrange("p b n -> p (b n)"), ACT.Copy).then_inc(m_yh.sem, 1)

        def expert_act(i):
            n_met = [0] * R

            def high_part(j):
                q, m = (U0 + j) % R, e_floats(j)
                n_met[q] += 32 if j < 2 * NCH2 else 16
                act.wait_ge(w_in_slot[q].sem, i * slot_turn[q] + (slot_before[q] + n_met[q]))
                act.wait_ge(w_used.sem, i * USES_E + (U0 + j - H + 1))
                nc.scalar.activation(ring_hi[:, (U0 + j) % H, 0:m], ring[:, q, 0:m], ACT.Copy).then_inc(w_hi.sem, 1)

            def hidden_e(ch):
                k = ch % 2
                act.wait_ge(m_tf[k].sem, 6 * i + (ch // 2 + 1))
                nc.scalar.activation(hEh[:, 2 * ch:2 * ch + 2, :], T[k][:, 0:2 * P].rearrange("p (k j) -> p k j", k=2), ACT.Copy).then_inc(m_th[k].sem, 1)

            for j in range(H - 1):
                high_part(j)
            result(i)
            for ch in range(NCH2):
                for j in range(2):
                    high_part(2 * ch + H - 1 + j)
                act.wait_ge(w_used.sem, i * USES_E + (U0 + 2 * ch + 2))
                if ch >= 2:
                    act.wait_ge(m_hb.sem, i * NCH2 + (ch - 1))
                nc.scalar.activation(HS[:, ch % 2, 0, :], G[:, ch % 2, 0:CH2], ACT.Silu).then_inc(m_silu.sem, 1)
                if ch:
                    hidden_e(ch - 1)
            hidden_e(NCH2 - 1)
            act.wait_ge(m_tf[1].sem, 6 * i + 6)
            nc.scalar.activation(PmT[:, :, :], T[1][:, 0:2 * P].rearrange("p (t j) -> p t j", t=2), ACT.Copy).then_inc(m_tt[1].sem, 1)
            for q in range(H - 1, len(DOWN2)):
                high_part(2 * NCH2 + q)
                if q == GATHER_AT + H - 1:
                    gather_act(i + 1)

        with act.Fori(0, NE) as i:
            expert_act(i)
        act.wait_ge(m_flag.sem, 1)
        over = act.value_load(FLAG[0:1, 0:1], min_val=0, max_val=1)
        with act.If(over > 0):
            with act.Fori(NE, 2 * NE) as i:
                expert_act(i)
        n_all = act.value_load(FLAG[0:1, 1:2], min_val=NE, max_val=2 * NE)
        result(n_all)

    TWO_PI = 2 * math.pi
    PI_A = float(np.float32(6.28125))
    PI_B = float(np.float32(TWO_PI - PI_A))
    PI_C = float(np.float32(TWO_PI - PI_A - np.float64(np.float32(TWO_PI - PI_A))))
    PI_MAX = 3.1415925
    ROUND = 12582912.0

    @block.vector
    def _(dve):
        v = nc.vector
        n_t, n_x = [0], [0, 0]
        n_lo = [0]

        def do(ins, s=None):
            step(dve, ins, s or dstep)

        def low_parts(upto):
            while n_lo[0] < min(upto, U0):
                n = n_lo[0]
                n_lo[0] += 1
                m = floats_of(TILES[n])
                dve.wait_ge(w_hi.sem, n + 1)
                cs = slice(0, of_dve(m))
                v.tensor_tensor(ring_lo[:, n % R, cs], ring[:, n % R, cs], ring_hi[:, n % H, cs].bitcast(F32), ALU.subtract).then_inc(w_lo.sem, 1)

        def met(n, ahead=H - 1):
            n_use["dve"] += n
            low_parts(n_use["dve"] + ahead)

        def full(n, ahead=H - 1):
            met(n, ahead)
            dve.wait_ge(w_used.sem, n_use["dve"])

        def low_evac(i, dst, high):
            n_x[i] += 1
            dve.wait_ge(x_hi[i].sem, n_x[i])
            v.tensor_tensor(dst, T[i][:, :].rearrange("p (k s) -> p k s", k=dst.shape[1]), high.bitcast(F32), ALU.subtract).then_inc(x_taken[i].sem, 1)

        def block_sum(tb):
            if tb == 0:
                dve.wait_ge(g_half.sem, g_half.next("dve"))
            else:
                dve.wait_ge(w_used.sem, n_use["dve"])

        def t0():
            n_t[0] += 1
            dve.wait_ge(t_full[0].sem, n_t[0])

        def evac(dst):
            t0()
            n = dst.free_size()
            do(v.tensor_copy(dst, T[0][:, 0:n].rearrange("p (k s) -> p k s", k=dst.shape[1])), t_taken[0])

        def token_evac():
            for tb in range(NTB):
                for i in range(2):
                    ks, toks = slice(4 * i, 4 * i + 4), slice(tb * P, (tb + 1) * P)
                    low_evac(i, xTl[:, ks, toks], xTh[:, ks, toks])

        def rope(x, cos, sin, heads, width, ra, rb):
            xv = x.rearrange("p (h d) -> p h d", h=heads)
            n = heads * width
            a, b = ra[:, 0:n].rearrange("p (h d) -> p h d", h=heads), rb[:, 0:n].rearrange("p (h d) -> p h d", h=heads)
            hw = width // 2
            do(v.tensor_tensor(a, xv, cos.unsqueeze(1).to_broadcast([P, heads, width]), ALU.mult))
            do(v.tensor_tensor(b[:, :, 0:hw], xv[:, :, hw:], sin[:, 0:hw].unsqueeze(1).to_broadcast([P, heads, hw]), ALU.mult))
            do(v.tensor_tensor(b[:, :, hw:], xv[:, :, 0:hw], sin[:, hw:].unsqueeze(1).to_broadcast([P, heads, hw]), ALU.mult))
            return v.tensor_tensor(xv, a, b, ALU.add)

        def g_tokens(tb):
            return G[:, 2 * tb:2 * tb + 2, :].rearrange("p b n -> p (b n)")

        def normed_to_x(n, gain, s):
            met(n)
            g_half.next("dve")
            for tb in range(NTB):
                dve.wait_ge(s_rstd.sem, s_rstd.next("dve"))
                do(v.scalar_tensor_tensor(XN[:, tb, :], g_tokens(tb), rstd[:, tb:tb + 1], gain, ALU.mult, ALU.mult), g_dve if tb else None)
                do(v.tensor_tensor(X[:, tb, :], X[:, tb, :], XN[:, tb, :], ALU.add), s)

        def pre_norm(gain):
            for tb in range(NTB):
                dve.wait_ge(s_rstd.sem, s_rstd.next("dve"))
                do(v.scalar_tensor_tensor(XN[:, tb, :], X[:, tb, :], rstd[:, tb:tb + 1], gain, ALU.mult, ALU.mult), xn_ready)

        def units(us, lbuf, pt, nm_of, scale_of, nlam, between=None):
            def masked(u):
                kind, j, tb = us[u]
                nk = P * (tb + 1)
                li = u % 2
                dve.wait_ge(scores.sem, scores.next("dve"))
                do(v.scalar_tensor_tensor(lbuf[:, li, :, 0:nk], g_map(u, nk), scale_of(kind), nm_of(kind, tb), ALU.mult, ALU.subtract), taken)
                if kind == "d":
                    do(v.tensor_reduce(nmx[:, li, :], lbuf[:, li, :, 0:nk], AX_X, ALU.max, negate=True))
                    do(v.tensor_tensor(nmx[:, li, :], nmx[:, li, :], nsink, ALU.min))
                    do(v.tensor_tensor(esk[:, li, :], nmx[:, li, :], nsink, ALU.subtract), maxed)
                else:
                    do(v.tensor_reduce(nmx[:, li, :], lbuf[:, li, :, 0:nk], AX_X, ALU.max, negate=True), maxed)

            def weigh(u):
                kind, j, tb = us[u]
                nk = P * (tb + 1)
                li = u % 2
                dve.wait_ge(probs.sem, probs.next("dve"))
                if kind == "d":
                    do(v.tensor_tensor(rsum[:, li, :], rsum[:, li, :], esk[:, li, :], ALU.add))
                do(v.reciprocal(rinv[:, li, :] if kind == "c" else rinv[:, li, :].rearrange("p (j i) -> p i j", i=2),
                                rsum[:, li, :] if kind == "c" else rsum[:, li, :].rearrange("p (i j) -> p i j", i=2)))
                if kind == "c":
                    for q in range(2):
                        do(v.tensor_scalar(lbuf[:, li, 2 + q, 0:nk], lbuf[:, li, 2 + q, 0:nk], rinv[:, li, 2 + q:3 + q], nlam, ALU.mult, ALU.mult))
                        do(v.scalar_tensor_tensor(lbuf[:, li, q, 0:nk], lbuf[:, li, q, 0:nk], rinv[:, li, q:q + 1],
                                                  lbuf[:, li, 2 + q, 0:nk], ALU.mult, ALU.add), comb if q else None)

            def out(u):
                kind, j, tb = us[u]
                li = u % 2
                n = 2 if kind == "c" else 4
                dve.wait_ge(pv_done.sem, pv_done.next("dve"))
                o0 = O_COL[kind] + 128 * j
                dst = XN[:, tb, o0:o0 + 64 * n].rearrange("p (m d) -> p m d", m=n)
                src = Sp[:, u % 2, 0:64 * n].rearrange("p (m d) -> p m d", m=n)
                if kind == "c":
                    do(v.tensor_copy(dst, src), o_ready)
                else:
                    do(v.tensor_tensor(dst, src, rinv[:, li, :].unsqueeze(2).to_broadcast([P, 4, 64]), ALU.mult), o_ready)

            masked(0)
            masked(1)
            weigh(0)
            for u in range(len(us)):
                evac(pt[:, 0, 0:2 if us[u][0] == "c" else 4, :])
                if u + 2 < len(us):
                    masked(u + 2)
                if u + 1 < len(us):
                    weigh(u + 1)
                if between:
                    between(u)
                out(u)

        dve.wait_ge(c_loaded.sem, 16)

        def first_tables():
            dve.wait_ge(loaded.sem, N_LOADED)
            do(v.tensor_copy(posf, POS[:, :]))
            for tb in range(NTB):
                do(v.tensor_scalar(ANG[:, tb, :], c("inv_freq"), posf[:, tb:tb + 1], None, ALU.mult))
            do(v.tensor_scalar(KK_, ANG, 1.0 / TWO_PI, ROUND, ALU.mult, ALU.add))
            do(v.tensor_scalar(KK_, KK_, ROUND, None, ALU.subtract))
            do(v.scalar_tensor_tensor(ANG, KK_, -PI_A, ANG, ALU.mult, ALU.add))
            do(v.scalar_tensor_tensor(ANG, KK_, -PI_B, ANG, ALU.mult, ALU.add))
            do(v.scalar_tensor_tensor(ANG, KK_, -PI_C, ANG, ALU.mult, ALU.add))
            do(v.tensor_scalar(KK_, ANG, PI_MAX, -PI_MAX, ALU.min, ALU.max))
            for q in range(2):
                do(v.tensor_tensor(p_lam[:, 2 * q], p_lam[:, 2 * q], p_lam[:, 2 * q + 1], ALU.mult))
            do(v.tensor_reduce(lamt[:, 0:2], p_lam[:, 0], AX_X, ALU.add))
            do(v.tensor_reduce(lamt[:, 2:4], p_lam[:, 2], AX_X, ALU.add), d2a)
            dve.wait_ge(a2d.sem, a2d.next("dve"))
            do(v.tensor_tensor(RWl[:, :, :], RW[:, :, :], RWh[:, :, :].bitcast(F32), ALU.subtract))
            do(v.tensor_tensor(SH, SH, SH, ALU.mult))
            do(v.tensor_scalar(SH, SH, -2.0, 1.0, ALU.mult, ALU.add))
            for k in range(2):
                do(v.tensor_copy(RCOS[:, :, 32 * k:32 * k + 32], SH[:, :, 0:32]))
                do(v.tensor_copy(RCOS32[:, :, 16 * k:16 * k + 16], SH[:, :, 32:48]))
                do(v.tensor_scalar(RSIN[:, :, 32 * k:32 * k + 32], SN[:, :, 0:32], 1.0 if k else -1.0, None, ALU.mult))
                do(v.tensor_scalar(RSIN32[:, :, 16 * k:16 * k + 16], SN[:, :, 32:48], 1.0 if k else -1.0, None, ALU.mult))
            do(v.tensor_tensor(lamt[:, 0:2], lamt[:, 2:4], lamt[:, 0:2], ALU.subtract))
            for l in range(DEPTH):
                lam0 = 0.8 - 0.6 * math.exp(-0.3 * l)
                do(v.tensor_scalar(lamt[:, l:l + 1], lamt[:, l:l + 1], lam0, None, ALU.subtract))
                do(v.tensor_scalar(p_sub[:, l, :], p_sub[:, l, :], 1.0 - lam0, None, ALU.mult))
            do(v.tensor_scalar(p_sink, p_sink, -1.0, None, ALU.mult))

        for l in range(DEPTH):
            lsl = slice(4 * l, 4 * l + 4)
            pre_norm(VEC[:, 1, :])
            if l == 0:
                low_parts(H - 1)
            token_evac()
            if l == 0:
                first_tables()
            def rotate(col, heads, width):
                cos, sin = (RCOS32, RSIN32) if width == 32 else (RCOS, RSIN)
                for tb in range(NTB):
                    do(rope(PROJ[:, tb, col:col + heads * width], cos[:, tb, :], sin[:, tb, :], heads, width, ROPE_A, ROPE_B))

            def add_dots(r, s=None):
                tb, h0, n = DOTS[r]
                sc = NMA[:, tb, 0:P * (tb + 1)]
                dve.wait_ge(idx_taken.sem, len(DOTS) * l + r + 1)
                for h in range(h0, h0 + n):
                    d = dot_map(DOT_R, tb, h)
                    if h == 0:
                        do(v.tensor_scalar(sc, d, iws[:, tb, 0:1], None, ALU.mult))
                    else:
                        do(v.scalar_tensor_tensor(sc, d, iws[:, tb, h:h + 1], sc, ALU.mult, ALU.add), s if h == h0 + n - 1 else None)

            for i, (n0, n1) in enumerate(IN_CHUNKS):
                full(2, H - 1 if i < IN_N - 1 else 0)
                do(v.tensor_copy(PROJ[:, 0, n0:n1], G[:, 2 * (i % 2), 0:n1 - n0]), g_dve)
                dve.wait_ge(g_act.sem, l * G_ACT + i + 1)
                if i == 0:
                    rotate(A_Q, 8, 64)
                    if l == 0:
                        t0()
                        do(v.tensor_copy(COLS[:, :], T[0][:, 0:N_TAPS + 8]), t_taken[0])
                if i == 2:
                    rotate(A_IQ, 9, 64)
                    do(v.tensor_scalar(iws, PROJ[:, :, A_IW:A_IW + 8], IDX_HEADS ** -0.5 * HD ** -0.5, None, ALU.mult))
                    for tb in range(NTB):
                        do(v.tensor_copy(IKD[:, 0, tb, :].rearrange("p (r d) -> p r d", r=2),
                                         PROJ[:, tb, A_IK:A_IK + 64].unsqueeze(1).to_broadcast([P, 2, 64])), d2pe if tb else None)
                if i == 3:
                    for b in (0, 2, 4):
                        evac(QKT[:, 2 * b:2 * b + 2, :])
                if i == 4:
                    do(v.tensor_tensor(LF[:, :, :], PROJ[:, :, B_F:B_F + 4], p_bf[:, lsl].unsqueeze(1).to_broadcast([P, NTB, 4]), ALU.add))
                    do(v.tensor_copy(GL[:, :, :], LF[:, :, :]), d2a)
                if i == 5:
                    rotate(C_Q, 16, 32)
                    add_dots(0, d2a)
            g_dve_in.append(g_dve.made)
            dve.wait_ge(a2d.sem, a2d.next("dve"))
            do(v.scalar_tensor_tensor(LF[:, :, :], LF[:, :, :], 0.0, GL[:, :, :], ALU.min, ALU.subtract), d2pe)
            add_dots(1, d2a)
            evac(QKT[:, 12:14, :])
            dve.wait_ge(pe2d.sem, pe2d.next("dve"))
            do(v.tensor_copy(cums.rearrange("p t h -> p (t h)"), G[:, 0, 0:8]))
            gb = G[:, 2:4, :].rearrange("p b (m s) -> p (b m) s", m=2)
            for h in range(4):
                do(v.scalar_tensor_tensor(NMB0[:, ORDER[h], :], gb[:, h, 0:P], cums[:, 0, h:h + 1], c("nm")[:, P:2 * P], ALU.subtract, ALU.add))
                do(v.scalar_tensor_tensor(NMB1[:, ORDER[h], :], gb[:, h, :], cums[:, 1, h:h + 1], c("nm"), ALU.subtract, ALU.add), d2pe if h == 3 else None)
            for b in (8, 10):
                evac(QKT[:, 2 * b:min(2 * b + 2, 21), :])
            add_dots(2)
            do(v.tensor_copy(nsink.rearrange("p (i j) -> p i j", i=2), p_sink[:, lsl].rearrange("p (j i) -> p i j", i=2)))

            def choose(tb, first, last):
                nk = P * (tb + 1)
                sc = NMA[:, tb, 0:nk]
                nm = c("nm")[:, 2 * P - nk:2 * P]
                n = TOPK // 8
                if first == 0:
                    do(v.tensor_tensor(sc, sc, nm, ALU.subtract))
                for _ in range(first, last):
                    do(v.max(top8, sc))
                    do(v.match_replace(sc, top8, sc, TAKEN))
                if last == n:
                    do(v.tensor_scalar(sc, sc, TAKEN, BIG, ALU.not_equal, ALU.mult))
                    do(v.tensor_tensor(sc, sc, nm, ALU.add))

            def between(u):
                n = TOPK // 8
                if u < 2:
                    choose(0, u * n // 2, (u + 1) * n // 2)
                elif u < 6:
                    choose(1, (u - 2) * n // 4, (u - 1) * n // 4)
                elif u == 6:
                    sq = AT_[:, 0:4, :].rearrange("p (t i) n -> p t (i n)", t=2)
                    oc = XN[:, :, 512:768]
                    do(v.tensor_tensor(sq, oc, oc, ALU.mult))
                    do(v.tensor_reduce(ms8, AT_[:, 0:4, :].rearrange("p i (j n) -> p (i j) n", j=2), AX_X, ALU.add))
                    do(v.tensor_scalar(ms8, ms8, 1.0 / HD, EPS, ALU.mult, ALU.add), d2p)
                elif u == 7:
                    met(0)
                elif u == 8:
                    dve.wait_ge(p2d.sem, p2d.next("dve"))
                    for tb in range(NTB):
                        oh = XN[:, tb, 512:768].rearrange("p (h d) -> p h d", h=4)
                        do(v.tensor_tensor(oh, oh, r8[:, 4 * tb:4 * tb + 4].unsqueeze(2).to_broadcast([P, 4, 64]), ALU.mult))
                        do(v.tensor_tensor(oh, oh, p_sub[:, l, :].unsqueeze(1).to_broadcast([P, 4, 64]), ALU.mult))

            def nm_of(kind, tb):
                nk = P * (tb + 1)
                if kind == "b":
                    return (NMB0 if tb == 0 else NMB1)
                m = NMA[:, tb, 0:nk] if kind == "a" else c("nm_slide" if kind == "d" else "nm")[:, 2 * P - nk:2 * P]
                return m.unsqueeze(1).to_broadcast([P, 4, nk])

            units(UNITS, L, PT, nm_of, lambda kind: 32 ** -0.5 if kind == "c" else HD ** -0.5, lamt[:, l:l + 1], between)
            token_evac()
            normed_to_x(4, VEC[:, 0, :], d2a)
            pre_norm(VEC[:, 1, :])
            token_evac()
            for ch in range(9):
                if ch < 8:
                    met(2)
                    dve.wait_ge(g_act.sem, l * G_ACT + IN_N + ch + 1)
                    do(v.tensor_tensor(HB[:, ch % 2, :, :], HB[:, ch % 2, :, :], HB[:, ch % 2, :, :], ALU.mult), hb_ready)
                if ch:
                    for j in range(2):
                        ks = slice(4 * ch - 4 + 2 * j, 4 * ch - 2 + 2 * j)
                        low_evac(j, hTl[:, ks, :], hTh[:, ks, :])
            low_evac(0, PLETl[:, :, :], PLETh[:, :, :])
            normed_to_x(16, VEC[:, 0, :], d2pe)
            met(1)
            token_evac()
            met(4)
            g_half.next("dve")
            dve.wait_ge(a2d.sem, a2d.next("dve"))
            for tb in range(NTB):
                dve.wait_ge(g_act.sem, l * G_ACT + IN_N + 8 + 1 + tb)
                do(v.tensor_tensor(XN[:, tb, :], XN[:, tb, :], PLR[:, tb, :], ALU.mult))
                do(v.tensor_tensor(X[:, tb, :], X[:, tb, :], XN[:, tb, :], ALU.add), d2pe if l == DEPTH - 1 else d2a)

        def moments(src, tb, width, s_out):
            n = max(1, width // 512)
            wd_ = width // n
            for q in range(n):
                do(v.bn_stats(bst[:, tb, 6 * q:6 * q + 6], src[:, tb, q * wd_:(q + 1) * wd_]))
            do(v.bn_aggr(mv[:, tb, :], bst[:, tb, 0:6 * n]), s_out)

        def standardized(src, tb, s_back):
            dve.wait_ge(s_back.sem, s_back.next("dve"))
            do(v.tensor_scalar(src[:, tb, :], src[:, tb, :], mv[:, tb, 0:1], rstd[:, tb:tb + 1], ALU.subtract, ALU.mult))

        def post_norm(f_of, ready, dst, s, s_out=d2p, s_back=p2d):
            def residual(tb):
                ready(tb)
                do(v.scalar_tensor_tensor(XN[:, tb, :], X[:, tb, :], ALPHA, f_of(tb), ALU.mult, ALU.add), g_dve if (tb and s is d2pe) else None)

            def scaled(tb):
                standardized(XN, tb, s_back)
                do(v.tensor_tensor(XN[:, tb, :], XN[:, tb, :], VEC[:, 0, :], ALU.mult))
                do(v.tensor_tensor(dst[:, tb, :], XN[:, tb, :], VEC[:, 1, :], ALU.add), s)

            residual(0)
            moments(XN, 0, D, s_out)
            residual(1)
            scaled(0)
            moments(XN, 1, D, s_out)
            scaled(1)

        for l in range(DEPTH):
            lsl = slice(4 * l, 4 * l + 4)
            token_evac()
            do(v.memset(PAD[:, :, 0:3], 0.0))
            av = P2[:, :, A2 + 256:A2 + 512]
            g2 = G[:, :, :].rearrange("p b (i t) -> p (b i) t", i=4)

            def conv(blocks, s):
                for b in blocks:
                    for j in range(4):
                        tap = COLS[:, (l * 4 + j) * 12 + b:(l * 4 + j) * 12 + b + 1]
                        if j == 0:
                            do(v.tensor_scalar(CV[:, b, :], PAD[:, b, 0:S], tap, None, ALU.mult))
                        else:
                            do(v.scalar_tensor_tensor(CV[:, b, :], PAD[:, b, j:j + S], tap, CV[:, b, :], ALU.mult, ALU.add),
                               s if (b == blocks[-1] and j == 3) else None)

            for q, i in enumerate(SEQ2):
                n0, n1 = IN2_CHUNKS[i]
                b = 2 * (q % 2)
                if i == 4:
                    met(2, 0)
                    continue
                full(2)
                if 1 <= i <= 3:
                    do(v.tensor_copy(PAD[:, 4 * (i - 1):4 * (i - 1) + 2, 3:], G[:, b, :].rearrange("p (m s) -> p m s", m=2)), g_dve)
                elif i >= 5:
                    o_ = BA2 + (n0 - 2560)
                    do(v.tensor_copy(P2[:, 0, o_:o_ + n1 - n0], G[:, b, 0:n1 - n0]), g_dve)
                dve.wait_ge(g_act.sem, DEPTH * G_ACT + l * len(IN2_CHUNKS) + q + 1)
                if i == 0:
                    for tb in range(NTB):
                        moments(av, tb, 256, d2p)
                    for tb in range(NTB):
                        standardized(av, tb, p2d)
                    do(v.tensor_tensor(av, av, ALN[:, 0, l, :].unsqueeze(1).to_broadcast([P, NTB, 256]), ALU.mult))
                    do(v.tensor_tensor(av, av, ALN[:, 1, l, :].unsqueeze(1).to_broadcast([P, NTB, 256]), ALU.add))
                if i == 1:
                    t0()
                    do(v.tensor_tensor(WST, T[0][:, :].rearrange("p (g t) -> p g t", g=4), c("upper1")[:, 0:P].unsqueeze(1).to_broadcast([P, 4, P]), ALU.mult),
                       t_taken[0])
                    conv(range(0, 4), d2a)
                if i == 2:
                    conv(range(4, 8), d2a)
                    dve.wait_ge(pe2d.sem, pe2d.next("dve"))
                    for g in range(4):
                        do(v.scalar_tensor_tensor(XN[:, :, g * 64:(g + 1) * 64], Sp[:, 0, g * P:(g + 1) * P].rearrange("p (t d) -> p t d", t=2),
                                                  COLS[:, N_TAPS + 4 * l + g:N_TAPS + 4 * l + g + 1], P2[:, :, A2 + g * 64:A2 + (g + 1) * 64], ALU.add, ALU.mult),
                           d2pe if g == 3 else None)
                if i == 3:
                    conv(range(8, 10), None)
                if i == 5:
                    do(v.tensor_tensor(LF[:, :, :], P2[:, :, BA2 + 4:BA2 + 8], p_dt[:, lsl].unsqueeze(1).to_broadcast([P, NTB, 4]), ALU.add))
                    do(v.tensor_copy(GL[:, :, :], LF[:, :, :]), d2a)
                    conv(range(10, 12), d2a)
                    dve.wait_ge(a2d.sem, a2d.next("dve"))
                    do(v.scalar_tensor_tensor(CV[:, 0:4, :].rearrange("p b s -> p (b s)"), CV[:, 0:4, :].rearrange("p b s -> p (b s)"), DK ** -0.5,
                                              SQ[:, 0:1024], ALU.mult, ALU.mult))
                    dve.wait_ge(a2d.sem, a2d.next("dve"))
                    do(v.tensor_tensor(CV[:, 4:8, :].rearrange("p b s -> p (b s)"), CV[:, 4:8, :].rearrange("p b s -> p (b s)"), SQ[:, 1024:2048], ALU.mult))
                    dve.wait_ge(a2d.sem, a2d.next("dve"))
                    do(v.scalar_tensor_tensor(GL[:, :, :], LF[:, :, :], 0.0, GL[:, :, :], ALU.max, ALU.add))
                    do(v.scalar_tensor_tensor(GL[:, :, :], GL[:, :, :], -1.0, ea4.unsqueeze(1).to_broadcast([P, NTB, 4]), ALU.mult, ALU.mult), d2pe)
                if i == 6:
                    t0()
                    do(v.tensor_copy(gc16, T[0][:, 0:16]), t_taken[0])
                    do(v.tensor_tensor(ms8, gc16[:, 8:16], gc16[:, 0:8], ALU.subtract))
                    dve.wait_ge(pe2d.sem, pe2d.next("dve"))
                    for k in range(8):
                        do(v.scalar_tensor_tensor(DT[:, k, :], Sp[:, k // 4, (k % 4) * P:(k % 4 + 1) * P], gc16[:, k:k + 1], c("nm_chunk"), ALU.subtract, ALU.subtract),
                           d2a if k == 7 else None)
                    for tb in range(NTB):
                        cos2 = c("cos2").rearrange("p (t n) -> p t n", t=2)[:, tb, :]
                        sin2 = c("sin2").rearrange("p (t n) -> p t n", t=2)[:, tb, :]
                        do(rope(P2[:, tb, C2:C2 + 512], cos2, sin2, 8, 64, R2A, R2B))
            dve.wait_ge(a2d.sem, a2d.next("dve"))
            dve.wait_ge(pe2d.sem, pe2d.next("dve"))
            for tb in range(NTB):
                do(v.tensor_tensor(MT[:, 4 * tb:4 * tb + 4, :], DT[:, 4 * tb:4 * tb + 4, :], T[tb][:, :].rearrange("p (i t) -> p i t", i=4), ALU.mult),
                   beta_taken if tb else None)
            dve.wait_ge(pe2d.sem, pe2d.next("dve"))
            do(v.tensor_tensor(MT, MT, g2[:, 8:16, :], ALU.mult), d2p)
            do(v.tensor_tensor(MLV[0], MT, c("level0").unsqueeze(1).to_broadcast([P, 8, P]), ALU.mult))
            for tb in range(NTB):
                do(v.tensor_tensor(TT[:, 4 * tb:4 * tb + 4, :], ident.unsqueeze(1).to_broadcast([P, 4, P]), MLV[0][:, 4 * tb:4 * tb + 4, :], ALU.subtract),
                   lv_done if tb else d2pe)
            evac(TN[:, 0:4, :])
            for lv in range(1, LEVELS):
                for tb in range(NTB):
                    cs = slice(4 * tb, 4 * tb + 4)
                    dve.wait_ge(pe2d.sem, pe2d.next("dve"))
                    if lv < LEVELS - 1:
                        do(v.tensor_tensor(TN[:, cs, :], TN[:, cs, :], g2[:, 8 + 4 * tb:12 + 4 * tb, :], ALU.subtract), d2pe)
                    do(v.tensor_tensor(TT[:, cs, :], TT[:, cs, :], Sp[:, tb, :].rearrange("p (i t) -> p i t", i=4), ALU.subtract), d2pe)
                if lv == 1:
                    do(v.tensor_tensor(AT_[:, :, :], AT_[:, :, :], DT, ALU.mult), lv_done)
                    do(v.tensor_tensor(bek8, BETA[:, :, :].rearrange("p t h -> p (t h)"), eg8, ALU.mult))
                    for tb in range(NTB):
                        q_ = CV[:, 0:4, tb * P:(tb + 1) * P]
                        do(v.tensor_tensor(q_, q_, EGB[:, tb, :].rearrange("p (h t) -> p h t", h=4), ALU.mult))
                if lv <= NTB:
                    t0()
                    src = T[0][:, :].rearrange("p (h d) -> p h d", h=4)
                    cs = slice(4 * (lv - 1), 4 * lv)
                    do(v.tensor_tensor(KBE[:, cs, :], src, bek8[:, cs].unsqueeze(2).to_broadcast([P, 4, P]), ALU.mult), lv_done if lv == 2 else None)
                    do(v.tensor_tensor(KD[:, cs, :], src, kds8[:, cs].unsqueeze(2).to_broadcast([P, 4, P]), ALU.mult), t_taken[0])
                if lv == 3:
                    do(v.memset(ST, 0.0), lv_done)
                if lv == 4:
                    met(0)
            dve.wait_ge(pe2d.sem, pe2d.next("dve"))
            do(v.tensor_copy(VB, g2[:, 0:8, :]), d2pe)
            for tb in range(NTB):
                for half in range(2):
                    rows = slice(half * CHUNK, (half + 1) * CHUNK)
                    cs = slice(4 * tb, 4 * tb + 4)
                    dve.wait_ge(pe2d.sem, pe2d.next("dve"))
                    do(v.tensor_tensor(DT[rows, cs, :], VB[rows, cs, :], G[rows, 0, :].rearrange("p (h e) -> p h e", h=4), ALU.subtract), d2pe)
                    if not (tb == 1 and half == 1):
                        dve.wait_ge(pe2d.sem, pe2d.next("dve"))
                        for h in range(H2):
                            do(v.scalar_tensor_tensor(ST[:, h, :], ST[:, h, :], EGL[:, tb, h, half:half + 1], G[:, 1, h * P:(h + 1) * P], ALU.mult, ALU.add),
                               d2pe if h == 3 else None)
            for tb in range(NTB):
                dve.wait_ge(a2d.sem, a2d.next("dve"))
                do(v.tensor_reduce(ms8[:, 4 * tb:4 * tb + 4], SQ[:, tb * 512:(tb + 1) * 512].rearrange("p (h e) -> p h e", h=4), AX_X, ALU.add))
            do(v.tensor_scalar(ms8, ms8, 1.0 / DK, 1e-6, ALU.mult, ALU.add), d2p)
            dve.wait_ge(p2d.sem, p2d.next("dve"))
            for tb in range(NTB):
                oh = XN[:, tb, 256:768].rearrange("p (h e) -> p h e", h=4)
                do(v.tensor_tensor(oh, Sp[:, tb, :].rearrange("p (h e) -> p h e", h=4), r8[:, 4 * tb:4 * tb + 4].unsqueeze(2).to_broadcast([P, 4, P]), ALU.mult))
                do(v.tensor_tensor(oh, oh, p_bn[:, l, :].unsqueeze(1).to_broadcast([P, 4, P]), ALU.mult))
                do(v.tensor_tensor(XN[:, tb, 256:768], XN[:, tb, 256:768], P2[:, tb, Z2:Z2 + 512], ALU.mult))
            evac(QKT2[:, 0:2, :])
            units(UNITS2, L2, PT2, lambda kind, tb: c(f"nm_dil{tb}").unsqueeze(1).to_broadcast([P, 4, P * (tb + 1)]),
                  lambda kind: HD ** -0.5, None)
            token_evac()
            met(4)
            post_norm(g_tokens, block_sum, X, d2pe)
            vec_free.append(d2pe.made)
            if l == 0:
                token_evac()
                for ch in range(NCH2 + 1):
                    if ch < NCH2:
                        met(2)
                        dve.wait_ge(silu_ready.sem, silu_ready.next("dve"))
                        b = 2 * (ch % 2)
                        do(v.tensor_tensor(HB2[:, ch % 2, :, :], HS[:, ch % 2, :, :], G[:, b:b + 2, CH2:2 * CH2], ALU.mult), hb_ready)
                    if ch:
                        ks = slice(2 * ch - 2, 2 * ch)
                        low_evac((ch - 1) % 2, hT2l[:, ks, :], hT2h[:, ks, :])
                met(FT2 // 2)
                post_norm(g_tokens, block_sum, X, d2pe)
                vec_free.append(d2pe.made)

        token_evac()
        do(v.memset(RK, 1e6))
        do(v.memset(CW, 0.0))
        do(v.tensor_scalar(PmT[:, :, :], c("iota").unsqueeze(1).to_broadcast([P, NTB, P]), -1.0, None, ALU.is_equal))
        do(v.memset(ACC, 0.0), m_acc)
        dve.wait_ge(pe2d.sem, pe2d.next("dve"))
        do(v.tensor_copy(LG, Sp[:, 0, 0:16].rearrange("p (t e) -> p t e", t=2)))
        for tb in range(NTB):
            do(v.max(TOPV[:, tb, :], LG[:, tb, :]))
            do(v.max_index(IDX[:, tb, :], TOPV[:, tb, :], LG[:, tb, :]))
        do(v.tensor_copy(IDXF, IDX[:, :, :]))
        for tb in range(NTB):
            do(v.tensor_scalar(SEL[:, tb, :], c("iota")[:, 0:8], IDXF[:, tb, 0:1], None, ALU.is_equal))
            do(v.tensor_scalar(OH[:, tb, :], c("iota")[:, 0:8], IDXF[:, tb, 1:2], None, ALU.is_equal))
        do(v.tensor_tensor(ANY, SEL, OH, ALU.add), d2pe)
        do(v.tensor_tensor(PR[:, :, 0:1], TOPV[:, :, 1:2], TOPV[:, :, 0:1], ALU.subtract), d2a)
        do(v.tensor_scalar(LG, ANY, -1e6, 1e6, ALU.mult, ALU.add))
        dve.wait_ge(pe2d.sem, pe2d.next("dve"))
        do(v.tensor_tensor(RK[:, :, 0:8], LG, Sp[:, 1, 0:16].rearrange("p (t e) -> p t e", t=2), ALU.add))
        do(v.tensor_scalar(RK[:, :, 8:16], RK[:, :, 0:8], float(P), None, ALU.subtract))
        do(v.tensor_reduce(CNT[:, 0:1], Sp[:, 1, 16:24], AX_X, ALU.max))

        def slots(i):
            for tb in range(NTB):
                last = v.tensor_scalar(Pm[:, tb, :], c("iota"), RK[:, tb, bass.ds(i, 1)], None, ALU.is_equal)
            last.then_inc(m_p.sem, 1)

        def tokens_low():
            v.tensor_tensor(xgTl[:, :, :], Sp[:, :, :].rearrange("p b (k j) -> p (b k) j", k=4), xgTh[:, :, :].bitcast(F32), ALU.subtract).then_inc(m_gd.sem, 1)

        def add_back(i, tb):
            dve.wait_ge(m_sc.sem, i * 2 + (tb + 1))
            dve.wait_ge(m_acc.sem, i * 2 + (tb + 1))
            v.scalar_tensor_tensor(ACC[:, tb, :], Sp[:, :, :].rearrange("p b n -> p (b n)"), CW[:, tb, bass.ds(i, 1)], ACC[:, tb, :],
                                   ALU.mult, ALU.add).then_inc(m_acc.sem, 1)

        slots(0)
        do(v.tensor_scalar(CNT[:, 1:2], CNT[:, 0:1], float(P), None, ALU.is_gt))
        do(v.tensor_scalar(CNT[:, 2:3], CNT[:, 1:2], float(NE), float(NE), ALU.mult, ALU.add))
        do(v.tensor_copy(FLAG[:, :], CNT[:, 1:3]), m_flag)
        dve.wait_ge(a2d.sem, a2d.next("dve"))
        do(v.tensor_scalar(PR[:, :, 1:2], PR[:, :, 0:1], 1.0, None, ALU.add))
        do(v.reciprocal(PR[:, :, 2:3], PR[:, :, 1:2]))
        do(v.tensor_tensor(PR[:, :, 3:4], PR[:, :, 0:1], PR[:, :, 2:3], ALU.mult))
        for tb in range(NTB):
            do(v.tensor_scalar(CW[:, tb, 1:9], SEL[:, tb, :], PR[:, tb, 2:3], None, ALU.mult))
            do(v.scalar_tensor_tensor(CW[:, tb, 1:9], OH[:, tb, :], PR[:, tb, 3:4], CW[:, tb, 1:9], ALU.mult, ALU.add))
        do(v.tensor_copy(CW[:, :, 9:17], CW[:, :, 1:9]))
        dve.wait_ge(m_g.sem, 1)
        do(v.tensor_copy(xgTh[:, :, :], Sp[:, :, :].rearrange("p b (k j) -> p (b k) j", k=4)))
        tokens_low()

        def result_low():
            v.tensor_tensor(YBl[:, :], G[:, 2:4, :].rearrange("p b n -> p (b n)"), YBh[:, :].bitcast(F32), ALU.subtract).then_inc(m_y.sem, 1)

        def expert_dve(i):
            def low_part(j):
                q, m = (U0 + j) % R, of_dve(e_floats(j))
                dve.wait_ge(w_hi.sem, i * USES_E + (U0 + j + 1))
                v.tensor_tensor(ring_lo[:, q, 0:m], ring[:, q, 0:m], ring_hi[:, (U0 + j) % H, 0:m].bitcast(F32), ALU.subtract).then_inc(w_lo.sem, 1)

            def hidden_e(ch):
                k = ch % 2
                dve.wait_ge(m_th[k].sem, i * ((NCH2 + 1 - k) // 2) + (ch // 2 + 1))
                v.tensor_tensor(hEl[:, 2 * ch:2 * ch + 2, :], T[k][:, 0:2 * P].rearrange("p (k j) -> p k j", k=2),
                                hEh[:, 2 * ch:2 * ch + 2, :].bitcast(F32), ALU.subtract).then_inc(m_tt[k].sem, 1)

            for j in range(H - 1):
                low_part(j)
            dve.wait_ge(m_yh.sem, i + 1)
            result_low()
            for ch in range(NCH2):
                for j in range(2):
                    low_part(2 * ch + H - 1 + j)
                dve.wait_ge(m_silu.sem, i * NCH2 + (ch + 1))
                v.tensor_tensor(HB2[:, ch % 2, 0, :], HS[:, ch % 2, 0, :], G[:, ch % 2, CH2:2 * CH2], ALU.mult).then_inc(m_hb.sem, 1)
                if ch:
                    hidden_e(ch - 1)
                if ch == 2:
                    add_back(i, 0)
                if ch == 5:
                    add_back(i, 1)
            hidden_e(NCH2 - 1)
            dve.wait_ge(m_tf[1].sem, 6 * i + 6)
            slots(i + 1)
            for q in range(H - 1, len(DOWN2)):
                low_part(2 * NCH2 + q)
                if q == GATHER_AT + H - 1:
                    dve.wait_ge(m_ga.sem, i + 1)
                    tokens_low()

        with dve.Fori(0, NE) as i:
            expert_dve(i)
        over = dve.value_load(FLAG[0:1, 0:1], min_val=0, max_val=1)
        with dve.If(over > 0):
            with dve.Fori(NE, 2 * NE) as i:
                expert_dve(i)
        n_all = dve.value_load(FLAG[0:1, 1:2], min_val=NE, max_val=2 * NE)
        dve.wait_ge(m_yh.sem, n_all + 1)
        result_low()
        for tb in range(NTB):
            add_back(n_all, tb)
        dve.wait_ge(m_acc.sem, n_all * 2 + 3)
        post_norm(lambda tb: ACC[:, tb, :], lambda tb: None, XN, f_out, f_r, f_p)

    @block.gpsimd
    def _(pool):
        g = nc.gpsimd

        def load(dst, src, s=loaded):
            pool.dma_start(dst, src, allow_slow_non_contiguous=True).then_inc(s.sem, 16)

        def power(dst, src, n, s):
            g.tensor_tensor(dst, src, c("mhalf")[:, 0:n], ALU.pow).then_inc(s.sem, 1)

        def root(tb, src, eps, s):
            step(pool, g.tensor_scalar(ms[:, tb:tb + 1], src, eps, None, ALU.add), pstep)
            power(rstd[:, tb:tb + 1], ms[:, tb:tb + 1], 1, s)

        def rms():
            for tb in range(NTB):
                pool.wait_ge(s_ssq.sem, s_ssq.next("pool"))
                root(tb, ssq[:, tb:tb + 1], EPS, s_rstd)

        def layer_norm(s_in=d2p, s_out=p2d):
            for tb in range(NTB):
                pool.wait_ge(s_in.sem, s_in.next("pool"))
                root(tb, mv[:, tb, 1:2], 1e-5, s_out)

        def asked(dst, src, n, s_in=d2p, s_out=p2d):
            pool.wait_ge(s_in.sem, s_in.next("pool"))
            power(dst, src, n, s_out)

        n_lo = [0, 0]

        def met(n, ahead=H - 1):
            n_lo[1] += n
            while n_lo[0] < min(n_lo[1] + ahead, U0):
                t = n_lo[0]
                n_lo[0] += 1
                m = floats_of(TILES[t])
                cs = slice(of_dve(m), m)
                pool.wait_ge(w_hi.sem, t + 1)
                g.tensor_tensor(ring_lo[:, t % R, cs], ring[:, t % R, cs], ring_hi[:, t % H, cs].bitcast(F32), ALU.subtract).then_inc(w_lo_pool.sem, 1)

        def rope(x, cos, sin, heads, width, a, b):
            xv = x.rearrange("p (h d) -> p h d", h=heads)
            a, b = a.rearrange("p (h d) -> p h d", h=heads), b.rearrange("p (h d) -> p h d", h=heads)
            hw = width // 2
            step(pool, g.tensor_tensor(a, xv, cos.unsqueeze(1).to_broadcast([P, heads, width]), ALU.mult), pstep)
            step(pool, g.tensor_tensor(b[:, :, 0:hw], xv[:, :, hw:], sin[:, 0:hw].unsqueeze(1).to_broadcast([P, heads, hw]), ALU.mult), pstep)
            step(pool, g.tensor_tensor(b[:, :, hw:], xv[:, :, 0:hw], sin[:, hw:].unsqueeze(1).to_broadcast([P, heads, hw]), ALU.mult), pstep)
            step(pool, g.tensor_tensor(xv, a, b, ALU.add), pstep)

        def gains(q, name, l):
            vec_loaded[q].made += 16
            pool.dma_start(VEC[:, q, :], w[name][l].partition_broadcast(P)).then_inc(vec_loaded[q].sem, 16)

        def gains_loaded(q):
            pool.wait_ge(vec_loaded[q].sem, vec_loaded[q].made)

        gains(1, "norm_pre_mix", 0)
        pool.wait_ge(c_loaded.sem, 16)
        gains_loaded(1)
        rms()
        met(1)
        gains(0, "norm_post_mix", 0)
        for l in range(DEPTH):
            if l:
                gains_loaded(1)
                rms()
                gains(0, "norm_post_mix", l)
                met(1)
            met(2 * IN_N - 1, 0)
            pool.wait_ge(g_dve.sem, g_dve_in[l])
            pool.wait_ge(g_act.sem, l * G_ACT + IN_N)
            for tb in range(NTB):
                rope(PROJ[:, tb, D_Q:D_Q + 384], RCOS[:, tb, :], RSIN[:, tb, :], 6, 64, XN[:, 0, 512:896], XN[:, 1, 512:896])
            for q, col in enumerate((D_K, D_K + 64)):
                for tb in range(NTB):
                    last = g.tensor_copy(IKD[:, 1 + q, tb, :].rearrange("p (r d) -> p r d", r=2),
                                         PROJ[:, tb, col:col + 64].unsqueeze(1).to_broadcast([P, 2, 64]))
            last.then_inc(p2pe.sem, 1)
            gains(1, "norm_pre_mlp", l)
            asked(r8, ms8, 8)
            met(0)
            for q in range(2):
                gains_loaded(q)
            met(4)
            rms()
            rms()
            gains(0, "norm_post_mlp", l)
            load(PLE, w["p"][l, 0].rearrange("(t p) d -> p t d", p=P), misc_loaded)
            gains_loaded(0)
            met(32)
            rms()
            gains(1, *(("norm_pre_mix", l + 1) if l + 1 < DEPTH else ("ln1_b_2", 0)))
            if l == DEPTH - 1:
                load(WSA, w["a_ws_2"][0].rearrange("g t s -> t g s"), misc_loaded)
            met(5)
        for l in range(DEPTH):
            if l:
                pool.wait_ge(d2pe.sem, vec_free[2 * l - 1])
                gains(0, "ln1_g_2", l)
                gains(1, "ln1_b_2", l)
            met(2)
            layer_norm()
            if l == 0:
                gains(0, "ln1_g_2", 0)
            met(2 * len(IN2_CHUNKS) - 2, 0)
            pool.wait_ge(d2p.sem, d2p.next("pool"))
            for lv in range(1, LEVELS):
                if lv >= 2:
                    pool.wait_ge(lv_done.sem, lv_done.next("pool"))
                m = c(f"level{lv}").unsqueeze(1).to_broadcast([P, 8, P])
                g.tensor_tensor(MLV[lv % 2], MT, m, ALU.mult).then_inc(p2pe.sem, 1)
            met(0)
            asked(r8, ms8, 8)
            for q in range(2):
                gains_loaded(q)
            met(4)
            layer_norm()
            if l + 1 < DEPTH:
                load(WSA, w["a_ws_2"][l + 1].rearrange("g t s -> t g s"), misc_loaded)
            pool.wait_ge(d2pe.sem, vec_free[2 * l])
            gains(0, "ln2_g_2", l)
            gains(1, "ln2_b_2", l)
            for q in range(2):
                gains_loaded(q)
            if l == 0:
                met(2 * NCH2 + FT2 // 2)
                layer_norm()

        def expert_pool(i):
            for j in range(USES_E):
                q, m = (U0 + j) % R, e_floats(j)
                pool.wait_ge(w_hi.sem, i * USES_E + (U0 + j + 1))
                cs = slice(of_dve(m), m)
                g.tensor_tensor(ring_lo[:, q, cs], ring[:, q, cs], ring_hi[:, (U0 + j) % H, cs].bitcast(F32), ALU.subtract).then_inc(w_lo_pool.sem, 1)

        with pool.Fori(0, NE) as i:
            expert_pool(i)
        pool.wait_ge(m_flag.sem, 1)
        over = pool.value_load(FLAG[0:1, 0:1], min_val=0, max_val=1)
        with pool.If(over > 0):
            with pool.Fori(NE, 2 * NE) as i:
                expert_pool(i)
        layer_norm(f_r, f_p)

    ctx.close()


_INS = ["x", "p", "positions", "w_in", "b_forget", "lambda_q1", "lambda_k1", "lambda_q2", "lambda_k2", "diff_subln",
        "sinks", "w_out", "norm_pre_mix", "norm_post_mix", "norm_pre_mlp", "norm_post_mlp", "w_mlp_up", "w_mlp_down",
        "w_ple_proj", "w_ple_gate", "w_in_2", "conv_w_2", "a_ln_g_2", "a_ln_b_2", "a_ws_2", "a_bs_2", "b_a_log_2",
        "b_dt_bias_2", "b_norm_g_2", "w_out_2", "ln1_g_2", "ln1_b_2", "ln2_g_2", "ln2_b_2", "ffn_w_gate_2", "ffn_w_up_2",
        "ffn_w_down_2", "moe_router_2", "moe_w_gate_2", "moe_w_up_2", "moe_w_down_2"]


def kernel(**inputs):
    import concourse.bacc as _bacc
    from concourse.bass_utils import run_bass_kernel_spmd as _run

    nc = _bacc.Bacc("TRN2", target_bir_lowering=False, num_devices=1)
    table, at = consts()
    arrays, w = {}, {}
    for name in _INS:
        a = np.ascontiguousarray(inputs[name])
        arrays[f"in_{name}"] = a
        w[name] = nc.dram_tensor(f"in_{name}", a.shape, mybir.dt.from_np(a.dtype), kind="ExternalInput").ap()
    arrays["shape_tables"] = table
    const_d = nc.dram_tensor("shape_tables", table.shape, F32, kind="ExternalInput").ap()
    out_d = nc.dram_tensor("out", (1, S, D), F32, kind="ExternalOutput").ap()
    build(nc, at, table.shape[1], const_d, w, out_d)
    r = _run(nc, [arrays], core_ids=[0])
    return r.results[0]["out"]
```

```python
import math
from contextlib import ExitStack

import numpy as np

import concourse.bass as bass
from concourse import mybir

F32 = mybir.dt.float32
F32R = mybir.dt.float32r
I32 = mybir.dt.int32
U32 = mybir.dt.uint32
ALU = mybir.AluOpType
ACT = mybir.ActivationFunctionType
AX_X = mybir.AxisListType.X

P = 128
D = 1024
S = 256
NTB = S // P
KT = D // P
DEPTH = 2
EPS = 1e-6
BIG = 1e30
TAKEN = -3e38
HD = 64
TOPK = min(256, S // 4)
D_FF = 4 * D
D_PLE = 256
A_Q, A_K, A_V, A_IQ, A_IK, A_IW = 0, 256, 512, 768, 1280, 1344
B_Q, B_K, B_V, B_F = 1352, 1608, 1864, 2120
C_Q, C_K, C_V = 2124, 2380, 2636
D_Q, D_K, D_V, D_IN = 2892, 3148, 3276, 3404
IDX_HEADS = 8
D_IN2 = 3336
H2 = 4
DK = 128
CHUNK = 64
LEVELS = 6
FF2 = 2816
FT2 = FF2 // P
CH2 = 256
NCH2 = FF2 // CH2
NE = 8
N_TAPS = DEPTH * 4 * 12
ALPHA = (2.0 * DEPTH) ** 0.25

R = 6
H = 3
SLOT = 2048
DOWN2 = [1] * 6 + [2] * 8
USES_E = 2 * NCH2 + len(DOWN2)
assert sum(DOWN2) == FT2 and USES_E % R == 0 and USES_E % H == 0
CT_N = 2 * NE + 2
GATHER_AT = 8


def consts():
    i = np.arange(P)
    s_, t_ = i[:, None], i[None, :]
    cols, at = [], {}

    def put(name, a):
        a = np.asarray(a, np.float32).reshape(P, -1)
        at[name] = (sum(c.shape[1] for c in cols), a.shape[1])
        cols.append(a)

    half = HD // 2
    inv = (np.float32(10000.0) ** (-np.arange(half, dtype=np.float32) / np.float32(half))).astype(np.float32)
    inv32 = (np.float32(10000.0) ** (-np.arange(16, dtype=np.float32) / np.float32(16))).astype(np.float32)
    put("ident", np.eye(P))
    put("inv_freq", np.broadcast_to(np.concatenate([inv, inv32])[None], (P, 48)))
    put("one", np.ones((P, 1)))
    put("eps", np.full((P, 1), EPS))
    put("mhalf", np.full((P, 16), -0.5))
    causal = np.where(i[None, :] <= i[:, None], 0.0, BIG)
    put("nm", np.concatenate([np.zeros((P, P)), causal], 1))
    slide = np.where(i[None, :] > i[:, None], 0.0, BIG)
    put("nm_slide", np.concatenate([slide, causal], 1))
    for tb in range(NTB):
        t = tb * P + i[:, None]
        s = np.arange((tb + 1) * P)[None, :]
        n = np.zeros((P, (tb + 1) * P))
        for window, dil in ((128, 1), (512, 4), (2048, 16)):
            n += (s <= t) & ((t - s) % dil == 0) & (t - s <= window)
        put(f"nm_dil{tb}", np.where(n > 0, -np.log(np.maximum(n, 1)), BIG))
    put("upper1", np.concatenate([s_ <= t_, np.ones((P, P))], 1))
    put("before", s_ < t_)
    same = (s_ // CHUNK) == (t_ // CHUNK)
    put("chunk_upper", same & (s_ <= t_))
    put("chunk_ones", same)
    put("nm_chunk", np.where(same & (s_ <= t_), 0.0, BIG))
    for l in range(LEVELS):
        b = 1 << l
        put(f"level{l}", (s_ // (2 * b) == t_ // (2 * b)) & ((t_ // b) % 2 == 1) & ((s_ // b) % 2 == 0))
    put("iota", np.broadcast_to(i[None, :], (P, P)))
    tok = np.arange(S, dtype=np.float32).reshape(NTB, P)
    inv2 = (np.float32(10000.0) ** (-np.arange(0, HD, 2, dtype=np.float32) / np.float32(HD))).astype(np.float32)
    ang = (tok[:, :, None] * inv2).astype(np.float32).astype(np.float64)
    put("cos2", np.concatenate([np.cos(ang), np.cos(ang)], 2).transpose(1, 0, 2))
    put("sin2", np.concatenate([-np.sin(ang), np.sin(ang)], 2).transpose(1, 0, 2))
    return np.ascontiguousarray(np.concatenate(cols, 1)), at


class Signal:

    def __init__(self, sem):
        self.sem, self.made, self.seen = sem, 0, {}

    def next(self, who, n=1):
        self.seen[who] = self.seen.get(who, 0) + n
        return self.seen[who]


def build(nc, at, n_const, const_d, w, out_d):
    ctx = ExitStack()

    def sb(name, shape, dt=F32):
        return ctx.enter_context(nc.sbuf_tensor(name, shape, dt))

    def sig(name):
        return Signal(ctx.enter_context(nc.semaphore(name)))

    def base_now():
        return (nc.sbuf_base + 31) // 32 * 32

    def parts_at(name, base, o, shape):
        return nc.alloc_sbuf_tensor_at(name, shape, F32R, offset=base + 4 * o)

    ring_base = base_now()
    ring = sb("ring", [P, R, SLOT])
    ring_lo = parts_at("ring_lo", ring_base, 0, [P, R, SLOT])
    ring_hi = sb("ring_hi", [P, H, SLOT], F32R)
    X = sb("X", [P, NTB, D])
    XN = sb("XN", [P, NTB, D])
    xTh_base = base_now()
    xTh = sb("xTh", [P, KT, S], F32R)
    xTl_base = base_now()
    xTl = sb("xTl", [P, KT, S], F32R)
    RW = sb("RW", [P, KT, NE])
    RWh, RWl = sb("RWh", [P, KT, NE], F32R), sb("RWl", [P, KT, NE], F32R)
    C = sb("C", [P, n_const])
    VEC = sb("VEC", [P, 2, D])
    COLS = sb("COLS", [P, N_TAPS + 8])
    SM = sb("SM", [P, 900])
    POS = sb("POS", [P, NTB], I32)
    IDX = sb("IDX", [P, NTB, 8], U32)
    FLAG = sb("FLAG", [P, 2], I32)
    ARENA_N = 17472
    arena_base = base_now()
    ARENA = sb("ARENA", [P, ARENA_N])

    G = ctx.enter_context(nc.psum_tensor("G", [P, 4, 512], F32))
    T = [ctx.enter_context(nc.psum_tensor(f"T{i}", [P, 512], F32)) for i in range(2)]
    Sp = ctx.enter_context(nc.psum_tensor("Sp", [P, 2, 512], F32))

    def c(name):
        o, n = at[name]
        return C[:, o:o + n]

    ident = c("ident")
    small_at = [0]

    def small(n):
        o = small_at[0]
        small_at[0] += n
        assert small_at[0] <= 900
        return SM[:, o:o + n]

    p_bf, p_sink = small(8), small(8)
    p_lam = small(256).rearrange("p (v l d) -> p v l d", v=4, l=2)
    p_sub = small(128).rearrange("p (l d) -> p l d", l=2)
    p_alog, p_dt = small(8), small(8)
    p_bn = small(256).rearrange("p (l d) -> p l d", l=2)
    ssq, ms, rstd = small(2), small(2), small(2)
    posf = small(2)
    nmx = small(8).rearrange("p (b m) -> p b m", b=2)
    rsum = small(8).rearrange("p (b m) -> p b m", b=2)
    esk = small(8).rearrange("p (b m) -> p b m", b=2)
    rinv = small(8).rearrange("p (b m) -> p b m", b=2)
    nsink = small(4)
    lamt = small(4)
    top8 = small(8)
    gc16, kds8, eg8, bek8 = small(16), small(8), small(8), small(8)
    EGL = small(16).rearrange("p (t h c) -> p t h c", t=2, h=4)
    iws, cums = small(16).rearrange("p (t h) -> p t h", t=2), small(8).rearrange("p (t h) -> p t h", t=2)
    ea4 = small(4)
    ms8, r8 = small(8), small(8)
    bst = small(24).rearrange("p (t n) -> p t n", t=2)
    mv = small(4).rearrange("p (t n) -> p t n", t=2)

    def ar(o, n):
        assert o + n <= ARENA_N, (o, n)
        return ARENA[:, o:o + n]

    PROJ = ar(0, NTB * D_IN).rearrange("p (t n) -> p t n", t=NTB)
    o = NTB * D_IN
    QKT = ar(o, 21 * S).rearrange("p (b s) -> p b s", b=21)
    o += 21 * S
    L = ar(o, 2 * 4 * S).rearrange("p (b m s) -> p b m s", b=2, m=4)
    ROPE_A = ar(o, 1024)
    ROPE_B = ar(o + 1024, 1024)
    o += 2 * 4 * S
    PT = ar(o, 1024).rearrange("p (k m t) -> p k m t", k=2, m=4)
    o += 1024
    NMB = ar(o, 1536)
    NMB0 = ar(o, 512).rearrange("p (h s) -> p h s", h=4)
    NMB1 = ar(o + 512, 1024).rearrange("p (h s) -> p h s", h=4)
    o += 1536
    NMA = ar(o, 512).rearrange("p (t s) -> p t s", t=2)
    o += 512
    AT_ = sb("AT_", [P, 8, P])
    TAPS = AT_[0:N_TAPS, 6, :]
    ABS = AT_[0:8, 7, :]
    PLE = AT_[:, 0:4, :].rearrange("p (t k) n -> p t (k n)", t=NTB)
    IKD = AT_[:, 0:6, :].rearrange("p (q t) n -> p q t n", q=3)
    LF = sb("LF", [P, NTB, 4])
    GL = sb("GL", [P, NTB, 4])
    BETA = sb("BETA", [P, NTB, 4])
    ROT = sb("ROT", [P, 384])
    RCOS = ROT[:, 0:128].rearrange("p (t n) -> p t n", t=2)
    RSIN = ROT[:, 128:256].rearrange("p (t n) -> p t n", t=2)
    RCOS32 = ROT[:, 256:320].rearrange("p (t n) -> p t n", t=2)
    RSIN32 = ROT[:, 320:384].rearrange("p (t n) -> p t n", t=2)
    ANG = ar(0, 96).rearrange("p (t n) -> p t n", t=2)
    KK_ = ar(96, 96).rearrange("p (t n) -> p t n", t=2)
    SN = ar(192, 96).rearrange("p (t n) -> p t n", t=2)
    SH = ar(288, 96).rearrange("p (t n) -> p t n", t=2)
    hTh = parts_at("hTh", arena_base, 0, [P, 32, S])
    hTl = parts_at("hTl", arena_base, 32 * S, [P, 32, S])
    HB = XN[:, :, :].rearrange("p b (t n) -> p b t n", t=NTB)
    PLETh = parts_at("PLETh", arena_base, 64 * S, [P, 2, S])
    PLETl = parts_at("PLETl", arena_base, 66 * S, [P, 2, S])
    PLR = ar(0, NTB * D).rearrange("p (t n) -> p t n", t=NTB)
    P2 = ar(0, NTB * 1800).rearrange("p (t n) -> p t n", t=NTB)
    A2, Z2, BA2, C2 = 0, 512, 1024, 1032
    o2 = 3600
    PAD = ar(o2, 12 * (S + 3)).rearrange("p (b s) -> p b s", b=12)
    TN = ar(o2, 512).rearrange("p (i t) -> p i t", i=8)
    WN = ar(o2 + 512, 512).rearrange("p (i t) -> p i t", i=8)
    TT = ar(o2 + 1024, 1024).rearrange("p (i t) -> p i t", i=8)
    WB = ar(o2 + 2048, 1024).rearrange("p (i t) -> p i t", i=8)
    o2 += 12 * (S + 3)
    CV = ar(o2, 12 * S).rearrange("p (b s) -> p b s", b=12)
    o2 += 12 * S
    SQ = ar(o2, 2048)
    MLV = [ar(o2 + 1024 * i, 1024).rearrange("p (i t) -> p i t", i=8) for i in range(2)]
    o2 += 2048
    VB = ar(o2, 1024).rearrange("p (i e) -> p i e", i=8)
    KBE = ar(o2 + 1024, 1024).rearrange("p (i e) -> p i e", i=8)
    KD = ar(o2 + 2048, 1024).rearrange("p (i e) -> p i e", i=8)
    MT = ar(o2 + 3072, 1024).rearrange("p (i t) -> p i t", i=8)
    WSA = ar(o2 + 3072, 512).rearrange("p (g s) -> p g s", g=4)
    WST = ar(o2 + 3584, 512).rearrange("p (g t) -> p g t", g=4)
    o2 += 4096
    EGB = ar(o2 - 4096 + 2048, 1024).rearrange("p (t n) -> p t n", t=2)
    DT = ar(o2, 1024).rearrange("p (i t) -> p i t", i=8)
    o2 += 1024
    WTs = MT
    STATE = [a.rearrange("p (h e) -> p h e", h=4) for a in (ar(o2, 512), SQ[:, 1024:1536])]
    o2 += 512
    QKT2 = nc.alloc_sbuf_tensor_at("QKT2", [P, 4, S], F32, offset=xTh_base)
    PT2 = nc.alloc_sbuf_tensor_at("PT2", [P, 2, 4, P], F32, offset=xTh_base + 4 * 4 * S)
    L2 = nc.alloc_sbuf_tensor_at("L2", [P, 2, 4, S], F32, offset=xTl_base)
    R2A, R2B = XN[:, 0, 256:768], XN[:, 1, 256:768]
    ALN = sb("ALN", [P, 2, 2, 256])
    hT2h = parts_at("hT2h", arena_base, 0, [P, FT2, S])
    hT2l = parts_at("hT2l", arena_base, FT2 * S, [P, FT2, S])
    HS = ar(2 * FT2 * S, 2 * NTB * CH2).rearrange("p (b t n) -> p b t n", b=2, t=NTB)
    HB2 = ar(2 * FT2 * S + 1024, 2 * NTB * CH2).rearrange("p (b t n) -> p b t n", b=2, t=NTB)
    hEh = parts_at("hEh", arena_base, 0, [P, FT2, P])
    hEl = parts_at("hEl", arena_base, FT2 * P, [P, FT2, P])
    om = 2 * FT2 * P
    Pm = ar(om, NTB * P).rearrange("p (t j) -> p t j", t=NTB)
    PmT = parts_at("PmT", arena_base, om + 256, [P, NTB, P])
    ACC = ar(om + 512, NTB * D).rearrange("p (t n) -> p t n", t=NTB)
    YBh = parts_at("YBh", arena_base, om + 2560, [P, D])
    YBl = parts_at("YBl", arena_base, 2 * FT2 * S + 3072, [P, D])
    xgTh = parts_at("xgTh", arena_base, om + 3584, [P, KT, P])
    xgTl = parts_at("xgTl", arena_base, 2 * FT2 * S + 2048, [P, KT, P])
    RK = ar(om + 4608, NTB * CT_N).rearrange("p (t e) -> p t e", t=NTB)
    CW = ar(om + 4608 + 64, NTB * CT_N).rearrange("p (t e) -> p t e", t=NTB)
    LG = ar(om + 4608 + 192, NTB * NE).rearrange("p (t e) -> p t e", t=NTB)
    SEL = ar(om + 4608 + 208, NTB * NE).rearrange("p (t e) -> p t e", t=NTB)
    OH = ar(om + 4608 + 224, NTB * NE).rearrange("p (t e) -> p t e", t=NTB)
    TOPV = ar(om + 4608 + 240, NTB * 8).rearrange("p (t e) -> p t e", t=NTB)
    IDXF = ar(om + 4608 + 256, NTB * 8).rearrange("p (t e) -> p t e", t=NTB)
    PR = ar(om + 4608 + 272, NTB * 4).rearrange("p (t e) -> p t e", t=NTB)
    CNT = ar(om + 4608 + 280, 16)
    ANY = ar(om + 4608 + 296, NTB * NE).rearrange("p (t e) -> p t e", t=NTB)

    x_loaded = [sig("x_loaded0"), sig("x_loaded1")]
    c_loaded = [sig("first_tables_loaded"), sig("tables_loaded")]
    pos_loaded = sig("positions_loaded")
    rows_loaded = sig("rows_loaded")
    loaded = sig("params_loaded")
    vec_loaded = [sig("vec_loaded0"), sig("vec_loaded1")]
    misc_loaded = sig("misc_loaded")
    misc_used = sig("misc_used")
    w_in_slot = [Signal(ctx.enter_context(nc.semaphore(f"w_in_slot{i}"))) for i in range(R)]
    w_hi, w_lo, w_lo_pool = sig("w_high_part"), sig("w_low_part"), sig("w_low_part_pool")
    w_used = sig("w_used")
    g_half = sig("g_first_half")
    x_full = [sig("x_full0"), sig("x_full1")]
    x_hi = [sig("x_high0"), sig("x_high1")]
    x_taken = [sig("x_taken0"), sig("x_taken1")]
    g_dve, g_act = sig("g_taken_dve"), sig("g_taken_act")
    t_full = [sig("t_full0"), sig("t_full1")]
    t_taken = [sig("t_taken0"), sig("t_taken1")]
    s_ssq, s_rstd, xn_ready = sig("ssq_ready"), sig("rstd_ready"), sig("xn_ready")
    s_ms = sig("ms_ready")
    beta_taken = sig("beta_rows_taken")
    lv_done, pe_own = sig("level_done"), sig("pe_own")
    dstep, astep, pstep = sig("dve_step"), sig("act_step"), sig("pool_step")
    a2d, d2a = sig("act_to_dve"), sig("dve_to_act")
    d2p, p2d = sig("dve_to_pool"), sig("pool_to_dve")
    d2pe = sig("dve_to_pe")
    a2pe = sig("act_to_pe")
    pe2d, pe2a = sig("pe_to_dve"), sig("pe_to_act")
    p2pe = sig("pool_to_pe")
    scores, taken = sig("scores_ready"), sig("scores_taken")
    maxed, probs = sig("max_ready"), sig("probs_ready")
    pv_done, o_ready = sig("pv_ready"), sig("o_ready")
    o_full = sig("state_outputs")
    o_ms, o_root = sig("output_mean_squares"), sig("output_roots")
    z_ready = sig("output_gates")
    p_full, p_taken = sig("probs_transposed"), sig("probs_taken")
    c_rotated = sig("differential_heads_rotated")
    f_taken = sig("gate_sums_taken")
    idx_s, idx_taken = sig("index_dots"), sig("index_dots_taken")
    silu_ready, hb_ready = sig("silu_ready"), sig("hidden_ready")
    out_done = sig("out_written")
    m_flag, f_out, f_r, f_p = sig("overflow_flag"), sig("result_ready"), sig("final_dve"), sig("final_pool")
    m_chunk, m_silu, m_hb = sig("e_chunk"), sig("e_silu"), sig("e_hidden")
    m_tf, m_tt = [sig("e_t_full0"), sig("e_t_full1")], [sig("e_t_taken0"), sig("e_t_taken1")]
    m_th = [sig("e_t_high0"), sig("e_t_high1")]
    m_p, m_g, m_gd, m_ga = sig("e_slots"), sig("e_gathered"), sig("e_gather_taken_dve"), sig("e_gather_taken_act")
    m_yh, m_y = sig("e_y_high_part"), sig("e_y_taken")
    m_sc, m_acc = sig("e_scattered"), sig("e_added")


    n_use = {"pe": 0, "dve": 0, "act": 0}
    g_dve_in = [[], []]
    vec_free = []
    block = ctx.enter_context(nc.Block())

    def step(eng, ins, s):
        ins.then_inc(s.sem, 1)
        s.made += 1
        eng.wait_ge(s.sem, s.made)

    def uses_cols(W, n0, n1):
        v = W[:, n0:n1].rearrange("(j k p) n -> j p k n", j=2, p=P)
        return [[(v[j], 0, n1 - n0)] for j in range(2)]

    def uses_rows(W, per=2):
        v = W.rearrange("(k p) n -> p k n", p=P)
        n = v.shape[1]
        return [[(v[:, k:k + per], None, per)] for k in range(0, n, per)]

    def uses_pair(Wg, Wu, ch):
        g = Wg[:, ch * CH2:(ch + 1) * CH2].rearrange("(j k p) n -> j p k n", j=2, p=P)
        u = Wu[:, ch * CH2:(ch + 1) * CH2].rearrange("(j k p) n -> j p k n", j=2, p=P)
        return [[(g[j], 0, CH2), (u[j], CH2, CH2)] for j in range(2)]

    def uses_down(Wd):
        v = Wd.rearrange("(k p) n -> p k n", p=P)
        got, k = [], 0
        for m in DOWN2:
            got.append([(v[:, k:k + m], None, m)])
            k += m
        return got

    IN_CHUNKS = [(n, min(n + 512, D_IN)) for n in range(0, D_IN, 512)]
    IN2_CHUNKS = [(0, 512), (512, 1024), (1024, 1536), (1536, 2048), (2048, 2560), (2560, 3072), (3072, D_IN2)]
    SEQ2 = [0, 1, 2, 3, 5, 6, 4]

    TILES = []
    for l in range(DEPTH):
        for n0, n1 in IN_CHUNKS:
            TILES += uses_cols(w["w_in"][l], n0, n1)
        TILES += uses_rows(w["w_out"][l])
        for n0 in range(0, D_FF, 512):
            TILES += uses_cols(w["w_mlp_up"][l], n0, n0 + 512)
        TILES += uses_rows(w["w_mlp_down"][l]) + uses_rows(w["w_ple_proj"][l]) + uses_rows(w["w_ple_gate"][l])
    for l in range(DEPTH):
        for i in SEQ2:
            TILES += uses_cols(w["w_in_2"][l], *IN2_CHUNKS[i])
        TILES += uses_rows(w["w_out_2"][l])
        if l == 0:
            for ch in range(NCH2):
                TILES += uses_pair(w["ffn_w_gate_2"][0], w["ffn_w_up_2"][0], ch)
            TILES += uses_rows(w["ffn_w_down_2"][0])
    U0 = len(TILES)

    def floats_of(use):
        return sum(m * D if c0 is None else 4 * m for _, c0, m in use)

    def e_floats(j):
        return SLOT if j < 2 * NCH2 else DOWN2[j - 2 * NCH2] * D

    def of_dve(m):
        return m * 11 // 32 * 2

    def slot_cols_of(buf, slot, width):
        return buf[:, slot, 0:4 * width].rearrange("p (k n) -> p k n", k=4)

    def slot_rows_of(buf, slot, n):
        return buf[:, slot, 0:n * D].rearrange("p (k n) -> p k n", k=n)

    slot_before = [16 * sum(len(TILES[n]) for n in range(U0) if n % R == q) for q in range(R)]
    slot_turn = [sum((32 if j < 2 * NCH2 else 16) for j in range(USES_E) if (U0 + j) % R == q) for q in range(R)]

    @block.sync
    def _(sp):
        def small_parameters():
            def load(dst, src):
                sp.dma_start(dst, src, allow_slow_non_contiguous=True).then_inc(loaded.sem, 16)

            for q, name in enumerate(("lambda_q1", "lambda_k1", "lambda_q2", "lambda_k2")):
                load(p_lam[:, q], w[name].partition_broadcast(P))
            load(p_sink, w["sinks"].rearrange("l h -> (l h)").partition_broadcast(P))
            load(p_sub, w["diff_subln"].partition_broadcast(P))
            load(p_bf, w["b_forget"].rearrange("l h -> (l h)").partition_broadcast(P))
            load(p_alog, w["b_a_log_2"].rearrange("l h -> (l h)").partition_broadcast(P))
            load(p_dt, w["b_dt_bias_2"].rearrange("l h -> (l h)").partition_broadcast(P))
            load(p_bn, w["b_norm_g_2"].partition_broadcast(P))
            load(ALN[:, 0], w["a_ln_g_2"].partition_broadcast(P))
            load(ALN[:, 1], w["a_ln_b_2"].partition_broadcast(P))
            load(RW[:, :, :], w["moe_router_2"][0].rearrange("(k p) e -> p k e", p=P))
            sp.dma_start(TAPS, w["conv_w_2"].rearrange("l j (b p) -> (l j b) p", p=P)).then_inc(rows_loaded.sem, 16)
            sp.dma_start(ABS, w["a_bs_2"].rearrange("l g t -> (l g) t")).then_inc(rows_loaded.sem, 16)

        c1 = at["nm"][0]
        sp.dma_start(C[:, 0:c1], const_d[:, 0:c1]).then_inc(c_loaded[0].sem, 16)
        sp.dma_start(POS[:, :], w["positions"][0].rearrange("(t p) -> p t", p=P), allow_slow_non_contiguous=True).then_inc(pos_loaded.sem, 16)
        for tb in range(NTB):
            sp.dma_start(X[:, tb, :], w["x"][0, tb * P:(tb + 1) * P, :]).then_inc(x_loaded[tb].sem, 16)
        for n, use in enumerate(TILES):
            if n == R:
                small_parameters()
                sp.dma_start(C[:, c1:], const_d[:, c1:]).then_inc(c_loaded[1].sem, 16)
            if n >= R:
                sp.wait_ge(w_used.sem, n - R + 1)
            width = sum(x[2] for x in use)
            for src, c0, m in use:
                dst = slot_rows_of(ring, n % R, m) if c0 is None else slot_cols_of(ring, n % R, width)[:, :, c0:c0 + m]
                sp.dma_start(dst, src).then_inc(w_in_slot[n % R].sem, 16)
        wg = w["moe_w_gate_2"][0]
        wu = w["moe_w_up_2"][0]
        wd = w["moe_w_down_2"][0]

        def expert(i, e):
            for j in range(USES_E):
                n = U0 + j
                sp.wait_ge(w_used.sem, i * USES_E + (n - R + 1))
                if j < 2 * NCH2:
                    ch, half = j // 2, j % 2
                    rows = slice(half * 512, half * 512 + 512)
                    for wm, c0 in ((wg, 0), (wu, CH2)):
                        src = wm[bass.ds(e, 1), rows, ch * CH2:(ch + 1) * CH2].rearrange("e (k p) n -> p (e k) n", p=P)
                        sp.dma_start(slot_cols_of(ring, n % R, 512)[:, :, c0:c0 + CH2], src).then_inc(w_in_slot[n % R].sem, 16)
                else:
                    k0 = sum(DOWN2[:j - 2 * NCH2])
                    m = DOWN2[j - 2 * NCH2]
                    src = wd[bass.ds(e, 1), k0 * P:(k0 + m) * P, :].rearrange("e (k p) n -> p (e k) n", p=P)
                    sp.dma_start(slot_rows_of(ring, n % R, m), src).then_inc(w_in_slot[n % R].sem, 16)

        with sp.Fori(0, NE) as i:
            expert(i, i)
        sp.wait_ge(m_flag.sem, 1)
        over = sp.value_load(FLAG[0:1, 0:1], min_val=0, max_val=1)
        with sp.If(over > 0):
            with sp.Fori(NE, 2 * NE) as i:
                expert(i, i - NE)
        for tb in range(NTB):
            sp.wait_ge(f_out.sem, tb + 1)
            sp.dma_start(out_d[0, tb * P:(tb + 1) * P, :], XN[:, tb, :]).then_inc(out_done.sem, 16)
        sp.wait_ge(out_done.sem, 16 * NTB)

    ORDER = [0, 2, 1, 3]

    def maps(kind, j=0):
        if kind == "a":
            return [(64 * (h % 2), h // 2, 2 + h // 2, 64, A_V + 64 * h, h) for h in ORDER]
        if kind == "b":
            return [(64 * (h % 2), 9 + h // 2, 11 + h // 2, 64, B_V + 64 * h, h) for h in ORDER]
        if kind == "c":
            return [(32 * i, 13 + j, 15 + j, 32, C_V + 64 * (2 * j + i // 2), i // 2 + 2 * (i % 2)) for i in ORDER]
        if kind == "d":
            return [(64 * (h % 2), 17 + h // 2, 19 + h // 2, 64, D_V + 64 * (h // 2), h) for h in ORDER]
        return [(64 * (h % 2), h // 2, 2 + h // 2, 64, C2 + 512 + 64 * h, h) for h in ORDER]

    UNITS = [(kind, j, tb) for kind, js in (("c", 2), ("b", 1), ("d", 1), ("a", 1)) for j in range(js) for tb in range(NTB)]
    UNITS2 = [("e", 0, tb) for tb in range(NTB)]
    DOTS = [(0, 0, 8), (1, 0, 4), (1, 4, 4)]
    DOT_R = PT.rearrange("p k m t -> p (k m t)")

    def dot_map(buf, tb, h):
        nk = P * (tb + 1)
        return buf[:, (h % 2) * 512 + (h // 2) % (4 // (tb + 1)) * nk:][:, 0:nk]

    O_COL = {"a": 0, "b": 256, "c": 512, "d": 768, "e": 768}
    QK_COLS = [A_Q, A_Q + 128, A_K, A_K + 128, A_IQ, A_IQ + 128, A_IQ + 256, A_IQ + 384, ("twice", A_IK),
               B_Q, B_Q + 128, B_K, B_K + 128, C_Q, C_Q + 128, C_K, C_K + 128, D_Q, D_Q + 128, ("twice", D_K), ("twice", D_K + 64)]

    def g_map(u, nk):
        h = G[:, 2 * (u % 2):2 * (u % 2) + 2, :].rearrange("p b (m s) -> p (b m) s", m=2)
        return h[:, :, 0:nk]

    QK_BLOCKS = [(0, 2), (2, 2), (4, 2), (6, 2), (8, 2), (10, 2), (12, 2), (14, 2), (16, 1), (17, 2), (19, 2)]
    U_D = 1
    def unit_logits(u):
        return (L, L2)[u % 4 // 2][:, u % 2]

    IN_N = len(IN_CHUNKS)
    G_ACT = IN_N + 8 + NTB
    N_LOADED = 16 * 13
    N_ROWS = 16 * 2

    @block.tensor
    def _(pe):
        n_t, n_x, n_p = [0, 0], [0, 0], [0, 0]
        t_free = [None, None]
        made = {"dve": 0, "act": 0}
        need = [(0, 0)] * 4

        def weights():
            n = n_use["pe"]
            n_use["pe"] += 1
            pe.wait_ge(w_lo.sem, n + 1)
            pe.wait_ge(w_lo_pool.sem, n + 1)
            return n % H, n % R

        def product(out, ah, al, bh, bl, start, stop, **kw):
            pe.matmul(out, ah, bh, start=start, stop=False, **kw)
            pe.matmul(out, ah, bl, start=False, stop=False, **kw)
            return pe.matmul(out, al, bh, start=False, stop=stop, **kw)

        def banks_free(banks):
            d, a = max(need[b][0] for b in banks), max(need[b][1] for b in banks)
            if d:
                pe.wait_ge(g_dve.sem, d)
            if a:
                pe.wait_ge(g_act.sem, a)

        def chunk_made(banks, by, times=1):
            for e in by:
                made[e] += times
            for b in banks:
                need[b] = (made["dve"], made["act"])

        def bank_free_t(i):
            if t_free[i]:
                pe.wait_ge(t_free[i][0].sem, t_free[i][1])

        def transposes(i, pairs, parts=False, act_takes=False):
            bank_free_t(i)
            for dst, src in pairs:
                k = src.shape[0]
                last = pe.transpose(dst, src, ident[0:k, 0:k])
            n = n_x if parts else n_p if act_takes else n_t
            n[i] += 1
            t_free[i] = (x_taken[i] if parts else p_taken if act_takes else t_taken[i], n[i])
            last.then_inc((x_full[i] if parts else p_full if act_takes else t_full[i]).sem, 1)

        def all_evacuated():
            for i in range(2):
                bank_free_t(i)

        def token_transposes(src, tb, ready):
            for i in range(2):
                ready(tb)
                transposes(i, [(T[i][:, k * P:(k + 1) * P], src[:, tb, (4 * i + k) * P:(4 * i + k + 1) * P]) for k in range(4)], parts=True)

        def cols_tile(slots, j, tb, width, bank):
            bh, bl = slot_cols_of(ring_hi, slots[0], width), slot_cols_of(ring_lo, slots[1], width)
            toks = slice(tb * P, (tb + 1) * P)
            for k in range(4):
                last = product(G[:, bank, 0:width], xTh[:, 4 * j + k, toks], xTl[:, 4 * j + k, toks], bh[:, k, :], bl[:, k, :],
                               j == 0 and k == 0, j == 1 and k == 3)
            return last

        def rows_tile(slots, m, ah, al, k0, n, tb, out):
            bh, bl = slot_rows_of(ring_hi, slots[0], m), slot_rows_of(ring_lo, slots[1], m)
            toks = slice(tb * P, (tb + 1) * P)
            for k in range(m):
                for h in range(2):
                    cs = slice(h * 512, (h + 1) * 512)
                    last = product(out[:, h, :], ah[:, k0 + k, toks], al[:, k0 + k, toks], bh[:, k, cs], bl[:, k, cs],
                                   k0 + k == 0, k0 + k == n - 1)
            return last

        def g_of(tb):
            return G[:, 2 * tb:2 * tb + 2, :]

        def transposed_in(src, ready, part, banks, between=None):
            token_transposes(src, 0, ready)
            if between:
                between()
            all_evacuated()
            banks_free(banks)
            first = weights()
            part(first, 0, 0)
            token_transposes(src, 1, ready)
            second = weights()
            part(second, 1, 0)
            all_evacuated()
            part(first, 0, 1).then_inc(w_used.sem, 1)
            part(second, 1, 1).then_inc(w_used.sem, 1)

        def first_cols(src, ready, width, banks, by):
            transposed_in(src, ready, lambda slots, j, tb: cols_tile(slots, j, tb, width, banks[tb]), banks)
            chunk_made(banks, by)

        def chunk_cols(width, banks, by):
            banks_free(banks)
            for j in range(2):
                slots = weights()
                for tb in range(NTB):
                    last = cols_tile(slots, j, tb, width, banks[tb])
                last.then_inc(w_used.sem, 1)
            chunk_made(banks, by)

        def product_rows(ah, al, n_tiles, by, first=0, times=1, behind=()):
            if not first:
                banks_free(range(4))
            for t in range(first, n_tiles - 2):
                slots = weights()
                for tb in range(NTB):
                    last = rows_tile(slots, 2, ah, al, 2 * t, 2 * n_tiles, tb, g_of(tb))
                last.then_inc(w_used.sem, 1)
                if t < len(behind):
                    behind[t]()
            all_evacuated()
            slots = []
            for tb in range(NTB):
                for j in range(2):
                    if tb == 0:
                        slots.append(weights())
                    last = rows_tile(slots[j], 2, ah, al, 2 * (n_tiles - 2 + j), 2 * n_tiles, tb, g_of(tb))
                    if tb:
                        last.then_inc(w_used.sem, 1)
                    elif j:
                        last.then_inc(g_half.sem, 1)
            chunk_made(range(4), by, times)

        def product_tokens(src, ready, by, between=None, times=1):
            transposed_in(src, ready, lambda slots, j, tb: rows_tile(slots, 2, xTh, xTl, 2 * j, KT, tb, g_of(tb)), range(4), between)
            product_rows(xTh, xTl, KT // 2, by, 2, times)

        def units(us, qkt, pt, v_of, sliding_heads):
            def logits(u):
                kind, j, tb = us[u]
                nk = P * (tb + 1)
                if u >= 2:
                    pe.wait_ge(taken.sem, taken.seen["pe0"] + u - 1)
                out = g_map(u, nk)
                mp = maps(kind, j)
                for n, m in enumerate(ORDER):
                    p0, qb, kb, kd = mp[m][:4]
                    if kind == "c" and n == 2:
                        last.then_inc(pe_own.sem, 1)
                        pe_own.made += 1
                        pe.wait_ge(pe_own.sem, pe_own.made)
                    last = pe.matmul(out[:, m, :], qkt[p0:p0 + kd, qb, tb * P:(tb + 1) * P], qkt[p0:p0 + kd, kb, 0:nk],
                                     start=True, stop=True)
                last.then_inc(scores.sem, 1)

            def prob_transposes(u):
                tb = us[u][2]
                pe.wait_ge(probs.sem, probs.next("pe"))
                for kb in range(tb + 1):
                    transposes(kb, [(T[kb][:, m * P:(m + 1) * P], unit_logits(u)[:, m, kb * P:(kb + 1) * P]) for m in range(4)], act_takes=kb == 0)

            def values(u, base):
                kind, j, tb = us[u]
                all_evacuated()
                if u >= 2:
                    pe.wait_ge(o_ready.sem, base + u - 1)
                mp = maps(kind, j)
                for m in range(4):
                    vcol, o_ = mp[m][4:]
                    for kb in range(tb + 1):
                        last = pe.matmul(Sp[:, u % 2, o_ * 64:(o_ + 1) * 64], pt[:, kb, m, :], v_of(kb, vcol),
                                         start=(kb == 0), stop=(kb == tb))
                last.then_inc(pv_done.sem, 1)

            taken.seen.setdefault("pe0", 0)
            base = o_ready.seen.get("pe", 0)
            logits(0)
            logits(1)
            for u in range(len(us)):
                if u + 2 < len(us):
                    if us[u + 2][0] == "d" and us[u + 2][2] == 0:
                        all_evacuated()
                    logits(u + 2)
                prob_transposes(u)
                values(u, base)
                if u == U_D:
                    sliding_heads()
            taken.seen["pe0"] += len(us)
            o_ready.seen["pe"] = base + len(us)

        pe.wait_ge(c_loaded[0].sem, 16)
        for l in range(DEPTH):
            def xn_block(tb):
                pe.wait_ge(xn_ready.sem, xn_ready.next("pe"))

            first_cols(XN, xn_block, IN_CHUNKS[0][1] - IN_CHUNKS[0][0], [0, 1], ("dve", "act"))
            sp2 = Sp[:, :, :].rearrange("p b n -> p (b n)")

            def qk_transposes(blocks):
                for b in blocks:
                    pairs = []
                    first, n = QK_BLOCKS[b]
                    for k in range(n):
                        col = QK_COLS[first + k]
                        for tb in range(NTB):
                            if isinstance(col, tuple):
                                src = IKD[:, {A_IK: 0, D_K: 1, D_K + 64: 2}[col[1]], tb, :]
                            else:
                                src = PROJ[:, tb, col:col + P]
                            pairs.append((T[b % 2][:, k * 256 + tb * P:k * 256 + tb * P + P], src))
                    transposes(b % 2, pairs)

            def index_dots(r):
                tb, h0, n = DOTS[r]
                if r:
                    pe.wait_ge(idx_taken.sem, len(DOTS) * l + r)
                for h in range(h0, h0 + n):
                    p0 = 64 * (h % 2)
                    last = pe.matmul(dot_map(sp2, tb, h), QKT[p0:p0 + 64, 4 + h // 2, tb * P:(tb + 1) * P], QKT[p0:p0 + 64, 8, 0:P * (tb + 1)],
                                     start=True, stop=True)
                last.then_inc(idx_s.sem, 1)

            for i, (n0, n1) in enumerate(IN_CHUNKS):
                b = 2 * (i % 2)
                if i:
                    chunk_cols(n1 - n0, [b, b + 1], ("dve", "act"))
                if i == 2 and l == 0:
                    pe.wait_ge(rows_loaded.sem, N_ROWS)
                    transposes(0, [(T[0][:, 0:N_TAPS], TAPS), (T[0][:, N_TAPS:N_TAPS + 8], ABS)])
                if i == 3:
                    pe.wait_ge(d2pe.sem, d2pe.next("pe"))
                    qk_transposes(range(5))
                if i == 4:
                    all_evacuated()
                if i == 4:
                    index_dots(0)
                if i == 5:
                    index_dots(1)
                    pe.wait_ge(d2pe.sem, d2pe.next("pe"))
                    banks_free([b, b + 1])
                    all_evacuated()
                    up = c("upper1")
                    pe.matmul(G[:, b, 0:4], up[:, 0:P], LF[:, 0, :], start=True, stop=True)
                    pe.matmul(G[:, b, 4:8], up[:, P:2 * P], LF[:, 0, :], start=True, stop=False)
                    pe.matmul(G[:, b, 4:8], up[:, 0:P], LF[:, 1, :], start=False, stop=True)
                    for h in range(4):
                        gb = T[h // 2][:, (h % 2) * S:(h % 2 + 1) * S]
                        pe.matmul(gb, LF[:, 0, h:h + 1].to_broadcast([P, P]), up, start=True, stop=False)
                        last = pe.matmul(gb[:, P:2 * P], LF[:, 1, h:h + 1].to_broadcast([P, P]), up[:, 0:P], start=False, stop=True)
                    last.then_inc(pe2d.sem, 1)
                    t_free[0] = t_free[1] = (f_taken, l + 1)
                    index_dots(2)
            pe.wait_ge(c_rotated.sem, c_rotated.next("pe"))
            qk_transposes(range(5, 9))
            all_evacuated()
            banks_free(range(4))
            pe.wait_ge(idx_taken.sem, len(DOTS) * (l + 1))

            def sliding_heads():
                pe.wait_ge(p2pe.sem, p2pe.next("pe"))
                qk_transposes(range(9, 11))

            units(UNITS, QKT, PT, lambda kb, vcol: PROJ[:, kb, vcol:vcol + 64], sliding_heads)
            def o_block(tb):
                pe.wait_ge(o_ready.sem, o_ready.seen["pe"] - 1 + tb)

            product_tokens(XN, o_block, ("dve",))
            def hidden(ch):
                pe.wait_ge(hb_ready.sem, hb_ready.next("pe"))
                for j in range(2):
                    transposes(j, [(T[j][:, k * 256 + tb * P:k * 256 + tb * P + P],
                                    HB[:, ch % 2, tb, (2 * j + k) * P:(2 * j + k + 1) * P]) for k in range(2) for tb in range(NTB)], parts=True)

            for ch in range(8):
                b = 2 * (ch % 2)
                if ch:
                    chunk_cols(512, [b, b + 1], ("act",))
                else:
                    first_cols(XN, xn_block, 512, [0, 1], ("act",))
                if ch:
                    hidden(ch - 1)

            def own_embedding():
                pe.wait_ge(misc_loaded.sem, 16 * (l + 1))
                transposes(0, [(T[0][:, k * 256 + tb * P:k * 256 + tb * P + P], PLE[:, tb, k * P:(k + 1) * P])
                               for k in range(2) for tb in range(NTB)], parts=True)

            product_rows(hTh, hTl, 16, ("dve",), behind=(lambda: hidden(7), own_embedding))
            embed = weights()
            rows_tile(embed, 2, PLETh, PLETl, 0, 2, 0, Sp).then_inc(pe2a.sem, 1)

            def embed_second():
                pe.wait_ge(a2pe.sem, a2pe.next("pe"))
                last = rows_tile(embed, 2, PLETh, PLETl, 0, 2, 1, Sp)
                last.then_inc(w_used.sem, 1)

            def x_block(tb):
                pe.wait_ge(d2pe.sem, d2pe.next("pe"))

            product_tokens(X, x_block, ("act",), embed_second, NTB)

        def dilated_logits(u):
            nk = P * (u + 1)
            mp = maps("e")
            if u == 0:
                all_evacuated()
            for m in ORDER:
                p0, qb, kb, kd = mp[m][:4]
                out = (T[m // 2] if u == 0 else G[:, 2 + m // 2, :])[:, (m % 2) * nk:(m % 2 + 1) * nk]
                last = pe.matmul(out, QKT2[p0:p0 + kd, qb, u * P:(u + 1) * P], QKT2[p0:p0 + kd, kb, 0:nk], start=True, stop=True)
            last.then_inc(scores.sem, 1)
            if u == 0:
                t_free[0] = t_free[1] = (taken, taken.seen["pe0"] + 1)
            taken.seen["pe0"] += 1

        def dilated_transposes(u, kb):
            if kb == 0:
                pe.wait_ge(probs.sem, probs.next("pe"))
            transposes(1, [(T[1][:, m * P:(m + 1) * P], L2[:, u, m, kb * P:(kb + 1) * P]) for m in range(4)])

        def dilated_values(u):
            bank_free_t(1)
            if u == 0:
                pe.wait_ge(taken.sem, taken.seen["pe0"])
            for m in range(4):
                vcol, head = maps("e")[m][4:]
                for kb in range(u + 1):
                    last = pe.matmul(G[:, 2 + u, head * 64:(head + 1) * 64], PT2[:, kb, m, :], P2[:, kb, vcol:vcol + 64],
                                     start=(kb == 0), stop=(kb == u))
            last.then_inc(pv_done.sem, 1)

        for l in range(DEPTH):
            first_cols(X, x_block, IN2_CHUNKS[0][1] - IN2_CHUNKS[0][0], [0, 1], ("act",))
            ones = c("upper1")[:, P:2 * P]
            for q, i in enumerate(SEQ2):
                n0, n1 = IN2_CHUNKS[i]
                b = 2 * (q % 2)
                if 1 <= i <= 3:
                    banks_free([b, b + 1])
                    out = G[:, b:b + 2, :].rearrange("p b (m s) -> p (b m) s", m=2)
                    for j in range(2):
                        sh, sl = weights()
                        wh, wl = slot_cols_of(ring_hi, sh, 512), slot_cols_of(ring_lo, sl, 512)
                        for m in range(4):
                            ms_ = slice(m * P, (m + 1) * P)
                            for k in range(4):
                                first = j == 0 and k == 0
                                last = product(out[:, m, :], wh[:, k, ms_], wl[:, k, ms_], xTh[:, 4 * j + k, :], xTl[:, 4 * j + k, :],
                                               first and m % 2 == 0, j == 1 and k == 3, skip_group_check=True)
                        last.then_inc(w_used.sem, 1)
                    chunk_made([b, b + 1], ("dve", "act"))
                elif q:
                    chunk_cols(n1 - n0, [b, b + 1], ("act",) if i == 4 else ("dve", "act"))
                if i == 1:
                    pe.wait_ge(misc_loaded.sem, 16 * (DEPTH + l + 1))
                    transposes(0, [(T[0][:, g * P:(g + 1) * P], WSA[:, g, :]) for g in range(4)])
                if i == 2:
                    bank_free_t(0)
                    for g in range(4):
                        last = pe.matmul(Sp[:, 0, g * P:(g + 1) * P], WST[:, g, :], P2[:, :, A2 + 256 + g * 64:A2 + 256 + (g + 1) * 64],
                                         start=True, stop=True)
                    last.then_inc(pe2d.sem, 1)
                if i in (3, 5):
                    if i == 3:
                        pe.wait_ge(d2pe.sem, d2pe.next("pe"))
                    pe.wait_ge(a2pe.sem, a2pe.next("pe"))
                    for b in range(2):
                        o_ = (b + (2 if i == 5 else 0)) * 512
                        last = pe.matmul(Sp[:, b, :], ones, SQ[:, o_:o_ + 512], start=True, stop=True)
                    last.then_inc(pe2a.sem, 1)
                if i == 6:
                    pe.wait_ge(d2pe.sem, d2pe.next("pe"))
                    bank_free_t(0)
                    for tb in range(NTB):
                        pe.matmul(T[0][:, tb * 4:tb * 4 + 4], c("chunk_upper"), GL[:, tb, :], start=True, stop=True)
                    for tb in range(NTB):
                        last = pe.matmul(T[0][:, 8 + tb * 4:12 + tb * 4], c("chunk_ones"), GL[:, tb, :], start=True, stop=True)
                    n_t[0] += 1
                    t_free[0] = (t_taken[0], n_t[0])
                    last.then_inc(t_full[0].sem, 1)
                    for tb in range(NTB):
                        for h in range(H2):
                            last = pe.matmul(Sp[:, tb, h * P:(h + 1) * P], GL[:, tb, h:h + 1].to_broadcast([P, P]), c("chunk_upper"),
                                             start=True, stop=True)
                    last.then_inc(pe2d.sem, 1)
                    for tb in (1, 0):
                        bank_free_t(tb)
                        for h in range(H2):
                            last = pe.matmul(T[tb][:, h * P:(h + 1) * P], BETA[:, tb, h:h + 1].to_broadcast([P, P]), ident,
                                             start=True, stop=True)
                        t_free[tb] = (beta_taken, l + 1)
                    last.then_inc(pe2d.sem, 1)
            banks_free([2, 3])
            for i in range(8):
                tb, h = i // 4, i % 4
                kT_ = CV[:, 4 + h, tb * P:(tb + 1) * P]
                last = pe.matmul(G[:, 2 + tb, h * P:(h + 1) * P], kT_, kT_, start=True, stop=True)
            last.then_inc(pe2d.sem, 1)
            banks_free([0, 1])
            for i in range(8):
                tb, h = i // 4, i % 4
                last = pe.matmul(G[:, tb, h * P:(h + 1) * P], CV[:, 4 + h, tb * P:(tb + 1) * P], CV[:, h, tb * P:(tb + 1) * P], start=True, stop=True)
            last.then_inc(pe2a.sem, 1)
            for tb in range(NTB):
                if tb == 0:
                    pe.wait_ge(d2pe.sem, d2pe.next("pe"))
                else:
                    pe.wait_ge(lv_done.sem, lv_done.next("pe"))
                transposes(tb, [(T[tb][:, h * P:(h + 1) * P], TT[:, tb * 4 + h, :]) for h in range(H2)])
            lv_done.next("pe", LEVELS - 3)
            all_evacuated()
            pe.wait_ge(a2pe.sem, a2pe.next("pe"))
            for lv in range(1, LEVELS):
                pe.wait_ge(p2pe.sem, p2pe.next("pe"))
                for tb in range(NTB):
                    if lv > 1:
                        pe.wait_ge(d2pe.sem, d2pe.next("pe", 1 + tb))
                    for h in range(H2):
                        last = pe.matmul(G[:, tb, h * CHUNK:(h + 1) * CHUNK], MLV[lv % 2][:, 4 * tb + h, :], TN[:, 4 * tb + h, :], start=True, stop=True)
                    last.then_inc(pe2a.sem, 1)
                if lv >= LEVELS - 2:
                    dilated_logits(lv - (LEVELS - 2))
                for tb in range(NTB):
                    if lv > 1 and tb == 1:
                        pe.wait_ge(d2pe.sem, d2pe.next("pe"))
                    if lv < LEVELS - 1:
                        pe.wait_ge(a2pe.sem, a2pe.next("pe"))
                        for h in range(H2):
                            i = 4 * tb + h
                            last = pe.matmul(G[:, 2 + tb, h * CHUNK:(h + 1) * CHUNK], TT[:, i, :], WN[:, i, :], start=True, stop=True)
                        last.then_inc(pe2d.sem, 1)
                    pe.wait_ge(a2pe.sem, a2pe.next("pe"))
                    for h in range(H2):
                        i = 4 * tb + h
                        last = pe.matmul(Sp[:, tb, h * P:(h + 1) * P], WB[:, i, :], TT[:, i, :], start=True, stop=True)
                    last.then_inc(pe2d.sem, 1)
                if lv <= NTB:
                    tb = lv - 1
                    transposes(0, [(T[0][:, h * P:(h + 1) * P], CV[:, 4 + h, tb * P:(tb + 1) * P]) for h in range(H2)])
                    transposes(1, [(T[1][:, h * P:(h + 1) * P], CV[:, 8 + h, tb * P:(tb + 1) * P]) for h in range(H2)])
                if lv == NTB + 1:
                    for b in range(2):
                        transposes(b, [(T[b][:, k * 256 + tb * P:k * 256 + tb * P + P], P2[:, tb, C2 + (2 * b + k) * P:C2 + (2 * b + k + 1) * P])
                                       for k in range(2) for tb in range(NTB)])
            pe.wait_ge(d2pe.sem, d2pe.next("pe", 2))
            for i in range(8):
                cs = slice((i % 4) * P, (i % 4 + 1) * P)
                last = pe.matmul(Sp[:, i // 4, cs], KBE[:, i, :], TT[:, i, :], start=True, stop=True)
            last.then_inc(pe2a.sem, 1)
            for i in range(8):
                cs = slice((i % 4) * P, (i % 4 + 1) * P)
                last = pe.matmul(G[:, i // 4, cs], TT[:, i, :], VB[:, i, :], start=True, stop=True)
                if i % 4 == 3:
                    last.then_inc(pe2d.sem, 1)
            def by_state(n):
                tb, half = n // 2, n % 2
                for h in range(H2):
                    pe.matmul(Sp[half * CHUNK:(half + 1) * CHUNK, tb, h * P:(h + 1) * P], CV[:, h, n * CHUNK:(n + 1) * CHUNK], STATE[n % 2][:, h, :],
                              start=(h == 0), stop=False, skip_group_check=True)

            for n in range(2 * NTB):
                tb, half = n // 2, n % 2
                rows = slice(half * CHUNK, (half + 1) * CHUNK)
                if n:
                    for h in range(H2):
                        last = pe.matmul(G[:, 0, h * P:(h + 1) * P], WTs[:, tb * 4 + h, :], STATE[n % 2][:, h, :], start=True, stop=True)
                    last.then_inc(pe2d.sem, 1)
                    by_state(n)
                if n == 1:
                    dilated_values(0)
                    dilated_transposes(1, 0)
                pe.wait_ge(d2pe.sem, d2pe.next("pe"))
                if n < 2 * NTB - 1:
                    for h in range(H2):
                        last = pe.matmul(T[0][:, h * P:(h + 1) * P], KD[rows, tb * 4 + h, :], DT[rows, tb * 4 + h, :], start=True, stop=True)
                    last.then_inc(pe2d.sem, 1)
                if half == 1:
                    for h in range(H2):
                        last = pe.matmul(Sp[:, tb, h * P:(h + 1) * P], AT_[:, tb * 4 + h, :], DT[:, tb * 4 + h, :],
                                         start=False, stop=True, skip_group_check=True)
                    last.then_inc(o_full.sem, 1)
                if n == 0:
                    dilated_transposes(0, 0)
                    pe.wait_ge(a2pe.sem, a2pe.next("pe"))
                    by_state(0)
                if n == 1:
                    dilated_transposes(1, 1)
                if n == 2:
                    dilated_values(1)
                if n < 2 * NTB - 1:
                    pe.wait_ge(d2pe.sem, d2pe.next("pe"))
            product_tokens(XN, xn_block, ("dve",))
            if l == 0:
                def hidden2(ch):
                    pe.wait_ge(hb_ready.sem, hb_ready.next("pe"))
                    i = ch % 2
                    transposes(i, [(T[i][:, k * 256 + tb * P:k * 256 + tb * P + P], HB2[:, i, tb, k * P:(k + 1) * P])
                                   for k in range(2) for tb in range(NTB)], parts=True)

                for ch in range(NCH2):
                    b = 2 * (ch % 2)
                    if ch:
                        chunk_cols(512, [b, b + 1], ())
                    else:
                        first_cols(X, x_block, 512, [0, 1], ())
                    if ch:
                        hidden2(ch - 1)
                pe.wait_ge(hb_ready.sem, hb_ready.seen["pe"] + 1)
                product_rows(hT2h, hT2l, FT2 // 2, ("dve",), behind=(lambda: hidden2(NCH2 - 1),))

        for tb in range(NTB):
            token_transposes(X, tb, x_block)
            all_evacuated()
            for k in range(KT):
                toks = slice(tb * P, (tb + 1) * P)
                last = product(Sp[:, 0, tb * 8:tb * 8 + 8], xTh[:, k, toks], xTl[:, k, toks], RWh[:, k, :], RWl[:, k, :], k == 0, k == KT - 1)
        last.then_inc(pe2d.sem, 1)
        pe.wait_ge(d2pe.sem, d2pe.next("pe"))
        ones = c("upper1")[:, P:2 * P]
        pe.matmul(Sp[:, 1, 0:8], c("before"), ANY[:, 0, :], start=True, stop=True)
        pe.matmul(Sp[:, 1, 8:16], ones, ANY[:, 0, :], start=True, stop=False)
        pe.matmul(Sp[:, 1, 8:16], c("before"), ANY[:, 1, :], start=False, stop=True)
        pe.matmul(Sp[:, 1, 16:24], ones, ANY[:, 0, :], start=True, stop=False)
        last = pe.matmul(Sp[:, 1, 16:24], ones, ANY[:, 1, :], start=False, stop=True)
        last.then_inc(pe2d.sem, 1)

        def gather():
            g8 = Sp[:, :, :].rearrange("p b (k j) -> p (b k) j", k=4)
            for k in range(KT):
                for tb in range(NTB):
                    last = pe.matmul(g8[:, k, :], X[:, tb, k * P:(k + 1) * P], Pm[:, tb, :], start=(tb == 0), stop=(tb == 1))
            last.then_inc(m_g.sem, 1)

        def scatter(tb):
            for h in range(2):
                cs = slice(h * 512, (h + 1) * 512)
                pe.matmul(Sp[:, h, :], PmT[:, tb, :], YBh[:, cs], start=True, stop=False)
                last = pe.matmul(Sp[:, h, :], PmT[:, tb, :], YBl[:, cs], start=False, stop=True)
            last.then_inc(m_sc.sem, 1)

        banks_free(range(4))
        pe.wait_ge(m_p.sem, 1)
        gather()
        assert n_use["pe"] == U0

        def expert_pe(i):
            def w_slots(j):
                pe.wait_ge(w_lo.sem, i * USES_E + (U0 + j + 1))
                pe.wait_ge(w_lo_pool.sem, i * USES_E + (U0 + j + 1))
                return (U0 + j) % H, (U0 + j) % R

            def hidden_e(ch):
                pe.wait_ge(m_hb.sem, i * NCH2 + (ch + 1))
                k = ch % 2
                if ch >= 2:
                    pe.wait_ge(m_tt[k].sem, 6 * i + (ch // 2))
                for q in range(2):
                    last = pe.transpose(T[k][:, q * P:(q + 1) * P], HB2[:, k, 0, q * P:(q + 1) * P], ident)
                last.then_inc(m_tf[k].sem, 1)

            pe.wait_ge(m_gd.sem, i + 1)
            for ch in range(NCH2):
                if ch >= 2:
                    pe.wait_ge(m_hb.sem, i * NCH2 + (ch - 1))
                for j in range(2):
                    sh, sl = w_slots(2 * ch + j)
                    bh, bl = slot_cols_of(ring_hi, sh, 512), slot_cols_of(ring_lo, sl, 512)
                    for k in range(4):
                        last = product(G[:, ch % 2, :], xgTh[:, 4 * j + k, :], xgTl[:, 4 * j + k, :], bh[:, k, :], bl[:, k, :],
                                       j == 0 and k == 0, j == 1 and k == 3)
                    last.then_inc(w_used.sem, 1)
                if ch:
                    hidden_e(ch - 1)
                if ch == 1:
                    pe.wait_ge(m_y.sem, i + 1)
                    scatter(0)
                if ch == 4:
                    pe.wait_ge(m_acc.sem, 2 * i + 2)
                    scatter(1)
            k0 = 0
            for q, m in enumerate(DOWN2):
                if q == len(DOWN2) - 1:
                    pe.wait_ge(m_tt[0].sem, 6 * i + 6)
                sh, sl = w_slots(2 * NCH2 + q)
                bh, bl = slot_rows_of(ring_hi, sh, m), slot_rows_of(ring_lo, sl, m)
                for k in range(m):
                    for h in range(2):
                        cs = slice(h * 512, (h + 1) * 512)
                        last = product(G[:, 2 + h, :], hEh[:, k0 + k, :], hEl[:, k0 + k, :], bh[:, k, cs], bl[:, k, cs],
                                       k0 + k == 0, k0 + k == FT2 - 1)
                last.then_inc(w_used.sem, 1)
                k0 += m
                if q == 0:
                    hidden_e(NCH2 - 1)
                    pe.wait_ge(m_tt[1].sem, 6 * i + 5)
                    for tb in range(NTB):
                        last = pe.transpose(T[1][:, tb * P:(tb + 1) * P], Pm[:, tb, :], ident)
                    last.then_inc(m_tf[1].sem, 1)
                if q == GATHER_AT:
                    pe.wait_ge(m_acc.sem, 2 * i + 3)
                    pe.wait_ge(m_p.sem, i + 2)
                    gather()
            pe.wait_ge(m_tt[1].sem, 6 * i + 6)

        with pe.Fori(0, NE) as i:
            expert_pe(i)
        pe.wait_ge(m_flag.sem, 1)
        over = pe.value_load(FLAG[0:1, 0:1], min_val=0, max_val=1)
        with pe.If(over > 0):
            with pe.Fori(NE, 2 * NE) as i:
                expert_pe(i)
        n_all = pe.value_load(FLAG[0:1, 1:2], min_val=NE, max_val=2 * NE)
        for tb in range(NTB):
            if tb == 0:
                pe.wait_ge(m_y.sem, n_all + 1)
                pe.wait_ge(m_gd.sem, n_all + 1)
                pe.wait_ge(m_tt[1].sem, n_all * 6)
            pe.wait_ge(m_acc.sem, n_all * 2 + (1 + tb))
            scatter(tb)

    @block.scalar
    def _(act):
        n_t, n_x = [0], [0, 0]
        slot_count = [0] * R
        n_hi = [0]

        def high_parts(upto):
            while n_hi[0] < min(upto, U0):
                n = n_hi[0]
                n_hi[0] += 1
                m = floats_of(TILES[n])
                slot_count[n % R] += 16 * len(TILES[n])
                act.wait_ge(w_in_slot[n % R].sem, slot_count[n % R])
                if n >= H:
                    act.wait_ge(w_used.sem, n - H + 1)
                nc.scalar.activation(ring_hi[:, n % H, 0:m], ring[:, n % R, 0:m], ACT.Copy).then_inc(w_hi.sem, 1)

        def met(n, ahead=H - 1):
            n_use["act"] += n
            high_parts(n_use["act"] + ahead)

        def full(n, ahead=H - 1):
            met(n, ahead)
            act.wait_ge(w_used.sem, n_use["act"])

        def t1():
            n_t[0] += 1
            act.wait_ge(t_full[1].sem, n_t[0])

        def evac(dst):
            t1()
            n = dst.free_size()
            nc.scalar.activation(dst, T[1][:, 0:n].rearrange("p (k s) -> p k s", k=dst.shape[1]), ACT.Copy).then_inc(t_taken[1].sem, 1)

        def high_evac(i, dst):
            n_x[i] += 1
            act.wait_ge(x_full[i].sem, n_x[i])
            nc.scalar.activation(dst, T[i][:, :].rearrange("p (k s) -> p k s", k=dst.shape[1]), ACT.Copy).then_inc(x_hi[i].sem, 1)

        def block_evac(tb):
            for i in range(2):
                high_evac(i, xTh[:, 4 * i:4 * i + 4, tb * P:(tb + 1) * P])

        def token_evac():
            for tb in range(NTB):
                block_evac(tb)

        def mean_square(src, tb):
            nc.scalar.activation(XN[:, tb, :], src, ACT.Square, scale=D ** -0.5, accum_out=ssq[:, tb:tb + 1]).then_inc(s_ssq.sem, 1)

        def block_sum(tb):
            if tb == 0:
                act.wait_ge(g_half.sem, g_half.next("act"))
            else:
                act.wait_ge(w_used.sem, n_use["act"])

        def mean_square_of_product(tb):
            block_sum(tb)
            mean_square(G[:, 2 * tb:2 * tb + 2, :].rearrange("p b n -> p (b n)"), tb)

        def mean_square_of_x(tb):
            act.wait_ge(d2a.sem, d2a.next("act"))
            mean_square(X[:, tb, :], tb)

        def normed_in(n, of_product):
            met(n, 1)
            for tb in range(NTB):
                of_product(tb)
                if tb:
                    block_evac(0)
                mean_square_of_x(tb)
            met(0)
            block_evac(1)

        def units(us, pt):
            def exps(u):
                kind, j, tb = us[u]
                nk = P * (tb + 1)
                act.wait_ge(maxed.sem, maxed.next("act"))
                if kind == "d":
                    nc.scalar.activation(esk[:, u % 2, :], esk[:, u % 2, :], ACT.Exp)
                for m in range(4):
                    last = nc.scalar.activation(unit_logits(u)[:, m, 0:nk], unit_logits(u)[:, m, 0:nk], ACT.Exp,
                                                bias=nmx[:, u % 2, m:m + 1], accum_out=rsum[:, u % 2, m:m + 1])
                last.then_inc(probs.sem, 1)

            exps(0)
            exps(1)
            for u in range(len(us)):
                act.wait_ge(p_full.sem, p_full.next("act"))
                nc.scalar.activation(pt[:, 0, :, :], T[0][:, :].rearrange("p (m t) -> p m t", m=4), ACT.Copy).then_inc(p_taken.sem, 1)
                if us[u][2] == 1:
                    evac(pt[:, 1, :, :])
                if u + 2 < len(us):
                    exps(u + 2)
                if u == U_D:
                    evac(QKT[:, 17:19, :])
                if u >= len(us) - H:
                    met(0, min(u - (len(us) - H) + 1, H - 1))

        for l in range(DEPTH):
            if l == 0:
                for tb in range(NTB):
                    act.wait_ge(x_loaded[tb].sem, 16)
                    mean_square(X[:, tb, :], tb)
                for tb in range(NTB):
                    high_parts(tb + 1)
                    if tb:
                        act.wait_ge(d2a.sem, d2a.next("act"))
                        nc.scalar.activation(SN[:, :, :], KK_[:, :, :], ACT.Sin)
                        nc.scalar.activation(SH[:, :, :], KK_[:, :, :], ACT.Sin, scale=0.5).then_inc(a2d.sem, 1)
                    block_evac(tb)
                high_parts(H)
            for i, (n0, n1) in enumerate(IN_CHUNKS):
                full(2, H - 1 if i < IN_N - 1 else 0)
                nc.scalar.activation(PROJ[:, 1, n0:n1], G[:, 2 * (i % 2) + 1, 0:n1 - n0], ACT.Copy).then_inc(g_act.sem, 1)
                if i == 2 and l == 0:
                    act.wait_ge(d2a.sem, d2a.next("act"))
                    nc.scalar.activation(RWh[:, :, :], RW[:, :, :], ACT.Copy)
                    nc.scalar.activation(lamt, lamt, ACT.Exp).then_inc(a2d.sem, 1)
                if i == 3:
                    for b in (1, 3):
                        evac(QKT[:, 2 * b:2 * b + 2, :])
                for r in {4: (0,), 5: (1, 2)}.get(i, ()):
                    act.wait_ge(idx_s.sem, idx_s.next("act"))
                    if r:
                        act.wait_ge(d2a.sem, d2a.next("act"))
                    nc.scalar.activation(DOT_R, Sp[:, :, :].rearrange("p b n -> p (b n)"), ACT.Relu).then_inc(idx_taken.sem, 1)
                if i == 4:
                    act.wait_ge(d2a.sem, d2a.next("act"))
                    step(act, nc.scalar.activation(GL[:, :, :], GL[:, :, :], ACT.Abs), astep)
                    step(act, nc.scalar.activation(GL[:, :, :], GL[:, :, :], ACT.Exp, scale=-1.0), astep)
                    nc.scalar.activation(GL[:, :, :], GL[:, :, :], ACT.Ln, bias=c("one")).then_inc(a2d.sem, 1)
            for b in (10, 14):
                evac(QKT[:, b:b + 2, :])
            units(UNITS, PT)
            token_evac()
            normed_in(4, mean_square_of_product)
            for ch in range(9):
                if ch < 8:
                    full(2)
                    b = 2 * (ch % 2)
                    nc.scalar.activation(HB[:, ch % 2, :, :], G[:, b:b + 2, :], ACT.Relu).then_inc(g_act.sem, 1)
                if ch:
                    for j in range(2):
                        high_evac(j, hTh[:, 4 * ch - 4 + 2 * j:4 * ch - 2 + 2 * j, :])
            met(1)
            high_evac(0, PLETh[:, :, :])
            met(15, 1)
            for tb in range(NTB):
                mean_square_of_product(tb)
            met(0)
            met(1)
            for tb in range(NTB):
                if tb == 0:
                    act.wait_ge(pe2a.sem, pe2a.next("act"))
                else:
                    act.wait_ge(w_used.sem, n_use["act"])
                nc.scalar.activation(PLR[:, tb, :], Sp[:, :, :].rearrange("p b n -> p (b n)"), ACT.Copy).then_inc((a2d if tb else a2pe).sem, 1)
                block_evac(tb)
            def gate(tb):
                block_sum(tb)
                nc.scalar.activation(XN[:, tb, :], G[:, 2 * tb:2 * tb + 2, :].rearrange("p b n -> p (b n)"), ACT.Sigmoid).then_inc(g_act.sem, 1)

            if l + 1 < DEPTH:
                normed_in(4, gate)
            else:
                met(4, 1)
                for tb in range(NTB):
                    gate(tb)
                block_evac(0)
                met(0)

        for l in range(DEPTH):
            if l:
                token_evac()
            else:
                block_evac(1)

            def norms(o_, between=None):
                act.wait_ge(pe2a.sem, pe2a.next("act"))
                sq = SQ[:, o_:o_ + 1024]
                step(act, nc.scalar.activation(sq, Sp[:, :, :].rearrange("p b n -> p (b n)"), ACT.Ln, bias=c("eps")), astep)
                if between:
                    between()
                nc.scalar.activation(sq, sq, ACT.Exp, scale=-0.5).then_inc(a2d.sem, 1)

            def conv_silu(g):
                act.wait_ge(d2a.sem, d2a.next("act"))
                cv = CV[:, 4 * g:4 * g + 4, :]
                step(act, nc.scalar.activation(cv, cv, ACT.Silu), astep)
                if g < 2:
                    nc.scalar.activation(SQ[:, 1024 * g:1024 * (g + 1)], cv.rearrange("p b s -> p (b s)"), ACT.Square).then_inc(a2pe.sem, 1)

            def dilated_exps(u):
                act.wait_ge(maxed.sem, maxed.next("act"))
                nk = P * (u + 1)
                for m in range(4):
                    last = nc.scalar.activation(L2[:, u, m, 0:nk], L2[:, u, m, 0:nk], ACT.Exp,
                                                bias=nmx[:, u, m:m + 1], accum_out=rsum[:, u, m:m + 1])
                last.then_inc(probs.sem, 1)

            for q, i in enumerate(SEQ2):
                n0, n1 = IN2_CHUNKS[i]
                b = 2 * (q % 2)
                full(2, H - 1 if q < len(SEQ2) - 1 else 0)
                if i in (0, 4):
                    for tb in range(NTB):
                        o_ = A2 if i == 0 else Z2
                        last = nc.scalar.activation(P2[:, tb, o_:o_ + 512], G[:, b + tb, :], ACT.Gelu_apprx_tanh if i == 0 else ACT.Silu)
                    last.then_inc(g_act.sem, 1)
                elif i <= 3:
                    nc.scalar.activation(PAD[:, 4 * (i - 1) + 2:4 * i, 3:], G[:, b + 1, :].rearrange("p (m s) -> p m s", m=2), ACT.Copy).then_inc(g_act.sem, 1)
                else:
                    o_ = BA2 + (n0 - 2560)
                    nc.scalar.activation(P2[:, 1, o_:o_ + n1 - n0], G[:, b + 1, 0:n1 - n0], ACT.Copy).then_inc(g_act.sem, 1)
                if i == 2:
                    conv_silu(0)
                if i == 3:
                    norms(0)
                    conv_silu(1)
                if i == 5:
                    def decay_input():
                        act.wait_ge(d2a.sem, d2a.next("act"))
                        step(act, nc.scalar.activation(GL[:, :, :], GL[:, :, :], ACT.Abs), astep)

                    norms(1024, decay_input)
                    nc.scalar.activation(BETA[:, :, :], P2[:, :, BA2:BA2 + 4], ACT.Exp, scale=-1.0)
                    step(act, nc.scalar.activation(GL[:, :, :], GL[:, :, :], ACT.Exp, scale=-1.0), astep)
                    nc.scalar.activation(ea4, p_alog[:, 4 * l:4 * l + 4], ACT.Exp)
                    nc.scalar.activation(GL[:, :, :], GL[:, :, :], ACT.Ln, bias=c("one")).then_inc(a2d.sem, 1)
                if i == 6:
                    conv_silu(2)
                    act.wait_ge(d2a.sem, d2a.next("act"))
                    nc.scalar.activation(kds8, ms8, ACT.Exp)
                    nc.scalar.activation(eg8, gc16[:, 0:8], ACT.Exp)
                    for half in range(2):
                        nc.scalar.activation(EGL[:, :, :, half], Sp[:, :, :].rearrange("p t (h s) -> p t h s", h=4)[:, :, :, half * CHUNK + CHUNK - 1], ACT.Exp)
                    nc.scalar.activation(EGB[:, :, :], Sp[:, :, :], ACT.Exp)
                    nc.scalar.activation(DT, DT, ACT.Exp).then_inc(a2d.sem, 1)
            act.wait_ge(pe2a.sem, pe2a.next("act"))
            nc.scalar.activation(AT_[:, :, :], G[:, 0:2, :].rearrange("p b (i t) -> p (b i) t", i=4), ACT.Copy).then_inc(a2pe.sem, 1)
            t1()
            for half in range(2):
                rows = slice(half * CHUNK, (half + 1) * CHUNK)
                last = nc.scalar.activation(TN[rows, 4:8, :], T[1][rows, :].rearrange("p (i t) -> p i t", i=4)[:, :, rows], ACT.Copy)
            last.then_inc(t_taken[1].sem, 1)
            for lv in range(1, LEVELS):
                for tb in range(NTB):
                    act.wait_ge(pe2a.sem, pe2a.next("act"))
                    joined = G[:, tb, 0:4 * CHUNK].rearrange("p (i t) -> p i t", i=4)
                    if lv < LEVELS - 1:
                        nc.scalar.activation(WN[:, 4 * tb:4 * tb + 4, :], joined, ACT.Copy).then_inc(a2pe.sem, 1)
                    for half in range(2):
                        rows = slice(half * CHUNK, (half + 1) * CHUNK)
                        last = nc.scalar.activation(WB[rows, 4 * tb:4 * tb + 4, rows], joined[rows], ACT.Copy)
                    last.then_inc(a2pe.sem, 1)
                if lv <= NTB:
                    tb = lv - 1
                    t1()
                    for h in range(H2):
                        last = nc.scalar.activation(VB[:, tb * 4 + h, :], T[1][:, h * P:(h + 1) * P], ACT.Copy, scale=BETA[:, tb, h:h + 1])
                    last.then_inc(t_taken[1].sem, 1)
                elif lv == NTB + 1:
                    evac(QKT2[:, 2:4, :])
            dilated_exps(0)
            act.wait_ge(pe2a.sem, pe2a.next("act"))
            nc.scalar.activation(WTs[:, :, :], Sp[:, :, :].rearrange("p b (i t) -> p (b i) t", i=4), ACT.Copy).then_inc(a2pe.sem, 1)
            evac(PT2[:, 0, :, :])
            dilated_exps(1)
            evac(PT2[:, 0, :, :])
            for tb in range(NTB):
                act.wait_ge(o_full.sem, o_full.next("act"))
                for h in range(H2):
                    last = nc.scalar.activation(SQ[:, (4 * tb + h) * P:(4 * tb + h + 1) * P], Sp[:, tb, h * P:(h + 1) * P], ACT.Square,
                                                scale=DK ** -0.5, accum_out=ms8[:, 4 * tb + h:4 * tb + h + 1])
                last.then_inc(o_ms.sem, 1)
                if tb == 0:
                    evac(PT2[:, 1, :, :])
                    met(0)
            token_evac()
            met(4)
            if l == 0:
                token_evac()
                for ch in range(NCH2 + 1):
                    if ch < NCH2:
                        full(2)
                        if ch >= 2:
                            act.wait_ge(hb_ready.sem, 8 * DEPTH + ch - 1)
                        b = 2 * (ch % 2)
                        nc.scalar.activation(HS[:, ch % 2, :, :], G[:, b:b + 2, 0:CH2], ACT.Silu).then_inc(silu_ready.sem, 1)
                    if ch:
                        high_evac((ch - 1) % 2, hT2h[:, 2 * ch - 2:2 * ch, :])
                met(FT2 // 2)

        token_evac()
        act.wait_ge(d2a.sem, d2a.next("act"))
        nc.scalar.activation(PR[:, :, 0:1], PR[:, :, 0:1], ACT.Exp).then_inc(a2d.sem, 1)

        def gather_act(i):
            act.wait_ge(m_g.sem, i + 1)
            nc.scalar.activation(xgTh[:, :, :], Sp[:, :, :].rearrange("p b (k j) -> p (b k) j", k=4), ACT.Copy).then_inc(m_ga.sem, 1)

        def result(n):
            act.wait_ge(w_used.sem, n * USES_E + U0)
            nc.scalar.activation(YBh[:, :], G[:, 2:4, :].rearrange("p b n -> p (b n)"), ACT.Copy).then_inc(m_yh.sem, 1)

        def expert_act(i):
            n_met = [0] * R

            def high_part(j):
                q, m = (U0 + j) % R, e_floats(j)
                n_met[q] += 32 if j < 2 * NCH2 else 16
                act.wait_ge(w_in_slot[q].sem, i * slot_turn[q] + (slot_before[q] + n_met[q]))
                act.wait_ge(w_used.sem, i * USES_E + (U0 + j - H + 1))
                nc.scalar.activation(ring_hi[:, (U0 + j) % H, 0:m], ring[:, q, 0:m], ACT.Copy).then_inc(w_hi.sem, 1)

            def hidden_e(ch):
                k = ch % 2
                act.wait_ge(m_tf[k].sem, 6 * i + (ch // 2 + 1))
                nc.scalar.activation(hEh[:, 2 * ch:2 * ch + 2, :], T[k][:, 0:2 * P].rearrange("p (k j) -> p k j", k=2), ACT.Copy).then_inc(m_th[k].sem, 1)

            for j in range(H - 1):
                high_part(j)
            result(i)
            for ch in range(NCH2):
                for j in range(2):
                    high_part(2 * ch + H - 1 + j)
                act.wait_ge(w_used.sem, i * USES_E + (U0 + 2 * ch + 2))
                if ch >= 2:
                    act.wait_ge(m_hb.sem, i * NCH2 + (ch - 1))
                nc.scalar.activation(HS[:, ch % 2, 0, :], G[:, ch % 2, 0:CH2], ACT.Silu).then_inc(m_silu.sem, 1)
                if ch:
                    hidden_e(ch - 1)
            hidden_e(NCH2 - 1)
            act.wait_ge(m_tf[1].sem, 6 * i + 6)
            nc.scalar.activation(PmT[:, :, :], T[1][:, 0:2 * P].rearrange("p (t j) -> p t j", t=2), ACT.Copy).then_inc(m_tt[1].sem, 1)
            for q in range(H - 1, len(DOWN2)):
                high_part(2 * NCH2 + q)
                if q == GATHER_AT + H - 1:
                    gather_act(i + 1)

        with act.Fori(0, NE) as i:
            expert_act(i)
        act.wait_ge(m_flag.sem, 1)
        over = act.value_load(FLAG[0:1, 0:1], min_val=0, max_val=1)
        with act.If(over > 0):
            with act.Fori(NE, 2 * NE) as i:
                expert_act(i)
        n_all = act.value_load(FLAG[0:1, 1:2], min_val=NE, max_val=2 * NE)
        result(n_all)

    TWO_PI = 2 * math.pi
    PI_A = float(np.float32(6.28125))
    PI_B = float(np.float32(TWO_PI - PI_A))
    PI_C = float(np.float32(TWO_PI - PI_A - np.float64(np.float32(TWO_PI - PI_A))))
    PI_MAX = 3.1415925
    ROUND = 12582912.0

    @block.vector
    def _(dve):
        v = nc.vector
        n_t, n_x = [0], [0, 0]
        n_lo = [0]

        def do(ins, s=None):
            step(dve, ins, s or dstep)

        def low_parts(upto):
            while n_lo[0] < min(upto, U0):
                n = n_lo[0]
                n_lo[0] += 1
                m = floats_of(TILES[n])
                dve.wait_ge(w_hi.sem, n + 1)
                cs = slice(0, of_dve(m))
                v.tensor_tensor(ring_lo[:, n % R, cs], ring[:, n % R, cs], ring_hi[:, n % H, cs].bitcast(F32), ALU.subtract).then_inc(w_lo.sem, 1)

        def met(n, ahead=H - 1):
            n_use["dve"] += n
            low_parts(n_use["dve"] + ahead)

        def full(n, ahead=H - 1):
            met(n, ahead)
            dve.wait_ge(w_used.sem, n_use["dve"])

        def low_evac(i, dst, high):
            n_x[i] += 1
            dve.wait_ge(x_hi[i].sem, n_x[i])
            v.tensor_tensor(dst, T[i][:, :].rearrange("p (k s) -> p k s", k=dst.shape[1]), high.bitcast(F32), ALU.subtract).then_inc(x_taken[i].sem, 1)

        def block_sum(tb):
            if tb == 0:
                dve.wait_ge(g_half.sem, g_half.next("dve"))
            else:
                dve.wait_ge(w_used.sem, n_use["dve"])

        def t0():
            n_t[0] += 1
            dve.wait_ge(t_full[0].sem, n_t[0])

        def evac(dst):
            t0()
            n = dst.free_size()
            do(v.tensor_copy(dst, T[0][:, 0:n].rearrange("p (k s) -> p k s", k=dst.shape[1])), t_taken[0])

        def block_evac(tb):
            for i in range(2):
                ks, toks = slice(4 * i, 4 * i + 4), slice(tb * P, (tb + 1) * P)
                low_evac(i, xTl[:, ks, toks], xTh[:, ks, toks])

        def token_evac():
            for tb in range(NTB):
                block_evac(tb)

        def rope(x, cos, sin, heads, width, ra, rb):
            xv = x.rearrange("p (h d) -> p h d", h=heads)
            n = heads * width
            a, b = ra[:, 0:n].rearrange("p (h d) -> p h d", h=heads), rb[:, 0:n].rearrange("p (h d) -> p h d", h=heads)
            hw = width // 2
            do(v.tensor_tensor(a, xv, cos.unsqueeze(1).to_broadcast([P, heads, width]), ALU.mult))
            do(v.tensor_tensor(b[:, :, 0:hw], xv[:, :, hw:], sin[:, 0:hw].unsqueeze(1).to_broadcast([P, heads, hw]), ALU.mult))
            do(v.tensor_tensor(b[:, :, hw:], xv[:, :, 0:hw], sin[:, hw:].unsqueeze(1).to_broadcast([P, heads, hw]), ALU.mult))
            return v.tensor_tensor(xv, a, b, ALU.add)

        def by_halves(op, s):
            for i in range(2):
                do(op(slice(512 * i, 512 * i + 512)), s)

        def g_tokens(tb):
            return G[:, 2 * tb:2 * tb + 2, :].rearrange("p b n -> p (b n)")

        def normed_product(tb, gain):
            dve.wait_ge(s_rstd.sem, s_rstd.next("dve"))
            do(v.scalar_tensor_tensor(XN[:, tb, :], g_tokens(tb), rstd[:, tb:tb + 1], gain, ALU.mult, ALU.mult), g_dve if tb else None)

        def added_to_x(tb, s):
            if s is d2pe:
                by_halves(lambda cs: v.tensor_tensor(X[:, tb, cs], X[:, tb, cs], XN[:, tb, cs], ALU.add), s)
            else:
                do(v.tensor_tensor(X[:, tb, :], X[:, tb, :], XN[:, tb, :], ALU.add), s)

        def pre_norm(tb, gain):
            dve.wait_ge(s_rstd.sem, s_rstd.next("dve"))
            by_halves(lambda cs: v.scalar_tensor_tensor(XN[:, tb, cs], X[:, tb, cs], rstd[:, tb:tb + 1], gain[:, cs], ALU.mult, ALU.mult), xn_ready)

        def normed_in(n, addend, gain):
            met(n, 1)
            g_half.next("dve")
            for tb in range(NTB):
                addend(tb)
                if tb:
                    block_evac(0)
                added_to_x(tb, d2a)
                pre_norm(tb, gain)
            met(0)
            block_evac(1)

        def units(us, nm_of, scale_of, nlam, between=None):
            def masked(u):
                kind, j, tb = us[u]
                nk = P * (tb + 1)
                li = u % 2
                dve.wait_ge(scores.sem, scores.next("dve"))
                lbuf = unit_logits(u)
                do(v.scalar_tensor_tensor(lbuf[:, :, 0:nk], g_map(u, nk), scale_of(kind), nm_of(kind, tb), ALU.mult, ALU.subtract), taken)
                if kind == "d":
                    do(v.tensor_reduce(nmx[:, li, :], lbuf[:, :, 0:nk], AX_X, ALU.max, negate=True))
                    do(v.tensor_tensor(nmx[:, li, :], nmx[:, li, :], nsink, ALU.min))
                    do(v.tensor_tensor(esk[:, li, :], nmx[:, li, :], nsink, ALU.subtract), maxed)
                else:
                    do(v.tensor_reduce(nmx[:, li, :], lbuf[:, :, 0:nk], AX_X, ALU.max, negate=True), maxed)

            def weigh(u):
                kind, j, tb = us[u]
                nk = P * (tb + 1)
                li = u % 2
                dve.wait_ge(probs.sem, probs.next("dve"))
                if kind == "d":
                    do(v.tensor_tensor(rsum[:, li, :], rsum[:, li, :], esk[:, li, :], ALU.add))
                do(v.reciprocal(rinv[:, li, :] if kind == "c" else rinv[:, li, :].rearrange("p (j i) -> p i j", i=2),
                                rsum[:, li, :] if kind == "c" else rsum[:, li, :].rearrange("p (i j) -> p i j", i=2)))
                if kind == "c":
                    do(v.tensor_scalar(rinv[:, li, 2:4], rinv[:, li, 2:4], nlam, None, ALU.mult))

            def out(u):
                kind, j, tb = us[u]
                li = u % 2
                n = 2 if kind == "c" else 4
                dve.wait_ge(pv_done.sem, pv_done.next("dve"))
                o0 = O_COL[kind] + 128 * j
                dst = XN[:, tb, o0:o0 + 64 * n].rearrange("p (m d) -> p m d", m=n)
                src = Sp[:, u % 2, 0:64 * n].rearrange("p (m d) -> p m d", m=n)
                if kind == "c":
                    both = AT_[:, 6:8, :].rearrange("p b (m d) -> p (b m) d", m=2)
                    do(v.tensor_tensor(both, Sp[:, u % 2, 0:256].rearrange("p (m d) -> p m d", m=4), rinv[:, li, :].unsqueeze(2).to_broadcast([P, 4, 64]), ALU.mult))
                    do(v.tensor_tensor(dst, both[:, 0:2, :], both[:, 2:4, :], ALU.add), o_ready)
                else:
                    do(v.tensor_tensor(dst, src, rinv[:, li, :].unsqueeze(2).to_broadcast([P, 4, 64]), ALU.mult), o_ready)

            masked(0)
            masked(1)
            weigh(0)
            for u in range(len(us)):
                if u + 2 < len(us):
                    masked(u + 2)
                if u + 1 < len(us):
                    weigh(u + 1)
                if between:
                    between(u)
                out(u)

        dve.wait_ge(c_loaded[0].sem, 16)

        def angles():
            dve.wait_ge(pos_loaded.sem, 16)
            do(v.tensor_copy(posf, POS[:, :]))
            for tb in range(NTB):
                do(v.tensor_scalar(ANG[:, tb, :], c("inv_freq"), posf[:, tb:tb + 1], None, ALU.mult))
            do(v.tensor_scalar(KK_, ANG, 1.0 / TWO_PI, ROUND, ALU.mult, ALU.add))
            do(v.tensor_scalar(KK_, KK_, ROUND, None, ALU.subtract))
            do(v.scalar_tensor_tensor(ANG, KK_, -PI_A, ANG, ALU.mult, ALU.add))
            do(v.scalar_tensor_tensor(ANG, KK_, -PI_B, ANG, ALU.mult, ALU.add))
            do(v.scalar_tensor_tensor(ANG, KK_, -PI_C, ANG, ALU.mult, ALU.add))
            do(v.tensor_scalar(KK_, ANG, PI_MAX, -PI_MAX, ALU.min, ALU.max), d2a)

        def rotations():
            dve.wait_ge(a2d.sem, a2d.next("dve"))
            do(v.tensor_tensor(SH, SH, SH, ALU.mult))
            do(v.tensor_scalar(SH, SH, -2.0, 1.0, ALU.mult, ALU.add))
            for k in range(2):
                do(v.tensor_copy(RCOS[:, :, 32 * k:32 * k + 32], SH[:, :, 0:32]))
                do(v.tensor_copy(RCOS32[:, :, 16 * k:16 * k + 16], SH[:, :, 32:48]))
                do(v.tensor_scalar(RSIN[:, :, 32 * k:32 * k + 32], SN[:, :, 0:32], 1.0 if k else -1.0, None, ALU.mult))
                do(v.tensor_scalar(RSIN32[:, :, 16 * k:16 * k + 16], SN[:, :, 32:48], 1.0 if k else -1.0, None, ALU.mult))

        def lambda_sums():
            dve.wait_ge(loaded.sem, N_LOADED)
            for q in range(2):
                do(v.tensor_tensor(p_lam[:, 2 * q], p_lam[:, 2 * q], p_lam[:, 2 * q + 1], ALU.mult))
            do(v.tensor_reduce(lamt[:, 0:2], p_lam[:, 0], AX_X, ALU.add))
            do(v.tensor_reduce(lamt[:, 2:4], p_lam[:, 2], AX_X, ALU.add), d2a)

        def parameters():
            dve.wait_ge(a2d.sem, a2d.next("dve"))
            do(v.tensor_tensor(RWl[:, :, :], RW[:, :, :], RWh[:, :, :].bitcast(F32), ALU.subtract))
            do(v.tensor_tensor(lamt[:, 0:2], lamt[:, 2:4], lamt[:, 0:2], ALU.subtract))
            for l in range(DEPTH):
                lam0 = 0.8 - 0.6 * math.exp(-0.3 * l)
                do(v.tensor_scalar(lamt[:, l:l + 1], lamt[:, l:l + 1], lam0, None, ALU.subtract))
                do(v.tensor_scalar(p_sub[:, l, :], p_sub[:, l, :], 1.0 - lam0, None, ALU.mult))
            do(v.tensor_scalar(p_sink, p_sink, -1.0, None, ALU.mult))

        for l in range(DEPTH):
            lsl = slice(4 * l, 4 * l + 4)
            if l == 0:
                angles()
                for tb in range(NTB):
                    pre_norm(tb, VEC[:, 1, :])
                for tb in range(NTB):
                    low_parts(tb + 1)
                    if tb:
                        rotations()
                    block_evac(tb)
                low_parts(H)

            def rotate(col, heads, width):
                cos, sin = (RCOS32, RSIN32) if width == 32 else (RCOS, RSIN)
                for tb in range(NTB):
                    do(rope(PROJ[:, tb, col:col + heads * width], cos[:, tb, :], sin[:, tb, :], heads, width, ROPE_A, ROPE_B))

            def add_dots(r, s=None):
                tb, h0, n = DOTS[r]
                sc = NMA[:, tb, 0:P * (tb + 1)]
                dve.wait_ge(idx_taken.sem, len(DOTS) * l + r + 1)
                for h in range(h0, h0 + n):
                    d = dot_map(DOT_R, tb, h)
                    if h == 0:
                        do(v.tensor_scalar(sc, d, iws[:, tb, 0:1], None, ALU.mult))
                    else:
                        do(v.scalar_tensor_tensor(sc, d, iws[:, tb, h:h + 1], sc, ALU.mult, ALU.add), s if h == h0 + n - 1 else None)

            for i, (n0, n1) in enumerate(IN_CHUNKS):
                full(2, H - 1 if i < IN_N - 1 else 0)
                do(v.tensor_copy(PROJ[:, 0, n0:n1], G[:, 2 * (i % 2), 0:n1 - n0]), g_dve)
                g_dve_in[l].append(g_dve.made)
                dve.wait_ge(g_act.sem, l * G_ACT + i + 1)
                if i == 0:
                    rotate(A_Q, 8, 64)
                if i == 1 and l == 0:
                    lambda_sums()
                if i == 2 and l == 0:
                    t0()
                    do(v.tensor_copy(COLS[:, :], T[0][:, 0:N_TAPS + 8]), t_taken[0])
                if i == 3 and l == 0:
                    parameters()
                    dve.wait_ge(c_loaded[1].sem, 16)
                if i == 2:
                    rotate(A_IQ, 9, 64)
                    do(v.tensor_scalar(iws, PROJ[:, :, A_IW:A_IW + 8], IDX_HEADS ** -0.5 * HD ** -0.5, None, ALU.mult))
                    for tb in range(NTB):
                        do(v.tensor_copy(IKD[:, 0, tb, :].rearrange("p (r d) -> p r d", r=2),
                                         PROJ[:, tb, A_IK:A_IK + 64].unsqueeze(1).to_broadcast([P, 2, 64])), d2pe if tb else None)
                if i == 3:
                    for b in (0, 2, 4):
                        evac(QKT[:, 2 * b:2 * b + 2, :])
                if i == 4:
                    do(v.tensor_tensor(LF[:, :, :], PROJ[:, :, B_F:B_F + 4], p_bf[:, lsl].unsqueeze(1).to_broadcast([P, NTB, 4]), ALU.add))
                    do(v.tensor_copy(GL[:, :, :], LF[:, :, :]), d2a)
                    add_dots(0, d2a)
                if i == 5:
                    dve.wait_ge(a2d.sem, a2d.next("dve"))
                    do(v.scalar_tensor_tensor(LF[:, :, :], LF[:, :, :], 0.0, GL[:, :, :], ALU.min, ALU.subtract), d2pe)
                    add_dots(1, d2a)
                    dve.wait_ge(pe2d.sem, pe2d.next("dve"))
                    do(v.tensor_copy(cums.rearrange("p t h -> p (t h)"), G[:, 2 * (i % 2), 0:8]))
                    for h in range(4):
                        gb = T[h // 2][:, (h % 2) * S:(h % 2 + 1) * S]
                        do(v.scalar_tensor_tensor(NMB0[:, ORDER[h], :], gb[:, 0:P], cums[:, 0, h:h + 1], c("nm")[:, P:2 * P], ALU.subtract, ALU.add))
                        do(v.scalar_tensor_tensor(NMB1[:, ORDER[h], :], gb, cums[:, 1, h:h + 1], c("nm"), ALU.subtract, ALU.add), f_taken if h == 3 else None)
                    add_dots(2)
            evac(QKT[:, 12:14, :])
            evac(QKT[:, 16:17, :])
            do(v.tensor_copy(nsink.rearrange("p (i j) -> p i j", i=2), p_sink[:, lsl].rearrange("p (j i) -> p i j", i=2)))

            def choose(tb, first, last):
                nk = P * (tb + 1)
                sc = NMA[:, tb, 0:nk]
                nm = c("nm")[:, 2 * P - nk:2 * P]
                n = TOPK // 8
                if first == 0:
                    do(v.tensor_tensor(sc, sc, nm, ALU.subtract))
                for _ in range(first, last):
                    do(v.max(top8, sc))
                    do(v.match_replace(sc, top8, sc, TAKEN))
                if last == n:
                    do(v.tensor_scalar(sc, sc, TAKEN, BIG, ALU.not_equal, ALU.mult))
                    do(v.tensor_tensor(sc, sc, nm, ALU.add))

            def between(u):
                n = TOPK // 8
                if u < 2:
                    choose(0, u * n // 2, (u + 1) * n // 2)
                elif u < 6:
                    choose(1, (u - 2) * n // 4, (u - 1) * n // 4)
                elif u == 6:
                    sq = AT_[:, 0:4, :].rearrange("p (t i) n -> p t (i n)", t=2)
                    oc = XN[:, :, 512:768]
                    do(v.tensor_tensor(sq, oc, oc, ALU.mult))
                    do(v.tensor_reduce(ms8, AT_[:, 0:4, :].rearrange("p i (j n) -> p (i j) n", j=2), AX_X, ALU.add))
                    do(v.tensor_scalar(ms8, ms8, 1.0 / HD, EPS, ALU.mult, ALU.add), d2p)
                if u >= len(UNITS) - H + 1:
                    met(0, u - (len(UNITS) - H))
                if u == U_D:
                    evac(QKT[:, 19:21, :])
                elif u == 8:
                    dve.wait_ge(p2d.sem, p2d.next("dve"))
                    for tb in range(NTB):
                        oh = XN[:, tb, 512:768].rearrange("p (h d) -> p h d", h=4)
                        do(v.tensor_tensor(oh, oh, r8[:, 4 * tb:4 * tb + 4].unsqueeze(2).to_broadcast([P, 4, 64]), ALU.mult))
                        do(v.tensor_tensor(oh, oh, p_sub[:, l, :].unsqueeze(1).to_broadcast([P, 4, 64]), ALU.mult))

            def nm_of(kind, tb):
                nk = P * (tb + 1)
                if kind == "b":
                    return (NMB0 if tb == 0 else NMB1)
                m = NMA[:, tb, 0:nk] if kind == "a" else c("nm_slide" if kind == "d" else "nm")[:, 2 * P - nk:2 * P]
                return m.unsqueeze(1).to_broadcast([P, 4, nk])

            units(UNITS, nm_of, lambda kind: 32 ** -0.5 if kind == "c" else HD ** -0.5, lamt[:, l:l + 1], between)
            token_evac()
            normed_in(4, lambda tb: normed_product(tb, VEC[:, 0, :]), VEC[:, 1, :])
            for ch in range(9):
                if ch < 8:
                    met(2)
                    dve.wait_ge(g_act.sem, l * G_ACT + IN_N + ch + 1)
                    do(v.tensor_tensor(HB[:, ch % 2, :, :], HB[:, ch % 2, :, :], HB[:, ch % 2, :, :], ALU.mult), hb_ready)
                if ch:
                    for j in range(2):
                        ks = slice(4 * ch - 4 + 2 * j, 4 * ch - 2 + 2 * j)
                        low_evac(j, hTl[:, ks, :], hTh[:, ks, :])
            met(1)
            low_evac(0, PLETl[:, :, :], PLETh[:, :, :])
            met(15, 1)
            g_half.next("dve")
            for tb in range(NTB):
                normed_product(tb, VEC[:, 0, :])
                added_to_x(tb, d2pe)
            met(1)
            token_evac()
            def gated_embedding(tb):
                if tb == 0:
                    dve.wait_ge(a2d.sem, a2d.next("dve"))
                dve.wait_ge(g_act.sem, l * G_ACT + IN_N + 8 + 1 + tb)
                do(v.tensor_tensor(XN[:, tb, :], XN[:, tb, :], PLR[:, tb, :], ALU.mult))

            if l + 1 < DEPTH:
                normed_in(4, gated_embedding, VEC[:, 1, :])
            else:
                met(4, 1)
                g_half.next("dve")
                for tb in range(NTB):
                    gated_embedding(tb)
                    if tb:
                        block_evac(0)
                    added_to_x(tb, d2pe)
                met(0)

        def moments(src, tb, width, s_out):
            n = max(1, width // 512)
            wd_ = width // n
            for q in range(n):
                do(v.bn_stats(bst[:, tb, 6 * q:6 * q + 6], src[:, tb, q * wd_:(q + 1) * wd_]))
            do(v.bn_aggr(mv[:, tb, :], bst[:, tb, 0:6 * n]), s_out)

        def standardized(src, tb, s_back):
            dve.wait_ge(s_back.sem, s_back.next("dve"))
            do(v.tensor_scalar(src[:, tb, :], src[:, tb, :], mv[:, tb, 0:1], rstd[:, tb:tb + 1], ALU.subtract, ALU.mult))

        def post_norm(f_of, ready, dst, s, s_out=d2p, s_back=p2d):
            def residual(tb):
                ready(tb)
                do(v.scalar_tensor_tensor(XN[:, tb, :], X[:, tb, :], ALPHA, f_of(tb), ALU.mult, ALU.add), g_dve if (tb and s is d2pe) else None)

            def scaled(tb):
                standardized(XN, tb, s_back)
                do(v.tensor_tensor(XN[:, tb, :], XN[:, tb, :], VEC[:, 0, :], ALU.mult))
                if s is d2pe:
                    by_halves(lambda cs: v.tensor_tensor(dst[:, tb, cs], XN[:, tb, cs], VEC[:, 1, cs], ALU.add), s)
                else:
                    do(v.tensor_tensor(dst[:, tb, :], XN[:, tb, :], VEC[:, 1, :], ALU.add), s)

            for tb in range(NTB):
                residual(tb)
                if tb and s is d2pe:
                    block_evac(0)
                moments(XN, tb, D, s_out)
                scaled(tb)

        for l in range(DEPTH):
            lsl = slice(4 * l, 4 * l + 4)
            block_evac(1)
            do(v.memset(PAD[:, :, 0:3], 0.0))
            av = P2[:, :, A2 + 256:A2 + 512]
            g2 = G[:, :, :].rearrange("p b (i t) -> p (b i) t", i=4)

            def dilated_masked(u):
                nk = P * (u + 1)
                nm = c(f"nm_dil{u}").unsqueeze(1)
                dve.wait_ge(scores.sem, scores.next("dve"))
                if u == 0:
                    for k in range(2):
                        do(v.scalar_tensor_tensor(L2[:, 0, 2 * k:2 * k + 2, 0:nk], T[k][:, 0:2 * nk].rearrange("p (m s) -> p m s", m=2), HD ** -0.5,
                                                  nm.to_broadcast([P, 2, nk]), ALU.mult, ALU.subtract), taken if k else None)
                else:
                    do(v.scalar_tensor_tensor(L2[:, 1, :, 0:nk], G[:, 2:4, :].rearrange("p b (m s) -> p (b m) s", m=2), HD ** -0.5,
                                              nm.to_broadcast([P, 4, nk]), ALU.mult, ALU.subtract), taken)
                do(v.tensor_reduce(nmx[:, u, :], L2[:, u, :, 0:nk], AX_X, ALU.max, negate=True), maxed)

            def dilated_sums(u):
                dve.wait_ge(probs.sem, probs.next("dve"))
                do(v.reciprocal(rinv[:, u, :].rearrange("p (j i) -> p i j", i=2), rsum[:, u, :].rearrange("p (i j) -> p i j", i=2)))

            def dilated_out(u):
                dve.wait_ge(pv_done.sem, pv_done.next("dve"))
                do(v.tensor_tensor(XN[:, u, 768:1024].rearrange("p (m d) -> p m d", m=4), G[:, 2 + u, 0:256].rearrange("p (m d) -> p m d", m=4),
                                   rinv[:, u, :].unsqueeze(2).to_broadcast([P, 4, 64]), ALU.mult))

            def gated(tb, meanwhile=None):
                oh = XN[:, tb, 256:768].rearrange("p (h e) -> p h e", h=4)
                if tb == 0:
                    dve.wait_ge(z_ready.sem, z_ready.next("dve"))
                dve.wait_ge(o_ms.sem, o_ms.next("dve"))
                do(v.tensor_tensor(XN[:, tb, 256:768], Sp[:, tb, :], P2[:, tb, Z2:Z2 + 512], ALU.mult))
                if meanwhile:
                    meanwhile()
                dve.wait_ge(o_root.sem, o_root.next("dve"))
                for i in range(2):
                    hs = slice(2 * i, 2 * i + 2)
                    do(v.tensor_tensor(oh[:, hs], oh[:, hs], r8[:, 4 * tb + 2 * i:4 * tb + 2 * i + 2].unsqueeze(2).to_broadcast([P, 2, P]), ALU.mult), xn_ready)

            def conv(blocks, s):
                for b in blocks:
                    for j in range(4):
                        tap = COLS[:, (l * 4 + j) * 12 + b:(l * 4 + j) * 12 + b + 1]
                        if j == 0:
                            do(v.tensor_scalar(CV[:, b, :], PAD[:, b, 0:S], tap, None, ALU.mult))
                        else:
                            do(v.scalar_tensor_tensor(CV[:, b, :], PAD[:, b, j:j + S], tap, CV[:, b, :], ALU.mult, ALU.add),
                               s if (b == blocks[-1] and j == 3) else None)

            for q, i in enumerate(SEQ2):
                n0, n1 = IN2_CHUNKS[i]
                b = 2 * (q % 2)
                if i == 4:
                    met(2, 0)
                    continue
                full(2)
                if 1 <= i <= 3:
                    do(v.tensor_copy(PAD[:, 4 * (i - 1):4 * (i - 1) + 2, 3:], G[:, b, :].rearrange("p (m s) -> p m s", m=2)), g_dve)
                elif i >= 5:
                    o_ = BA2 + (n0 - 2560)
                    do(v.tensor_copy(P2[:, 0, o_:o_ + n1 - n0], G[:, b, 0:n1 - n0]), g_dve)
                dve.wait_ge(g_act.sem, DEPTH * G_ACT + l * len(IN2_CHUNKS) + q + 1)
                if i == 0:
                    for tb in range(NTB):
                        moments(av, tb, 256, d2p)
                    for tb in range(NTB):
                        standardized(av, tb, p2d)
                    do(v.tensor_tensor(av, av, ALN[:, 0, l, :].unsqueeze(1).to_broadcast([P, NTB, 256]), ALU.mult))
                    do(v.tensor_tensor(av, av, ALN[:, 1, l, :].unsqueeze(1).to_broadcast([P, NTB, 256]), ALU.add))
                if i == 1:
                    t0()
                    do(v.tensor_tensor(WST, T[0][:, :].rearrange("p (g t) -> p g t", g=4), c("upper1")[:, 0:P].unsqueeze(1).to_broadcast([P, 4, P]), ALU.mult),
                       t_taken[0])
                    conv(range(0, 4), d2a)
                if i == 2:
                    conv(range(4, 8), d2a)
                    dve.wait_ge(pe2d.sem, pe2d.next("dve"))
                    for g in range(4):
                        do(v.scalar_tensor_tensor(XN[:, :, g * 64:(g + 1) * 64], Sp[:, 0, g * P:(g + 1) * P].rearrange("p (t d) -> p t d", t=2),
                                                  COLS[:, N_TAPS + 4 * l + g:N_TAPS + 4 * l + g + 1], P2[:, :, A2 + g * 64:A2 + (g + 1) * 64], ALU.add, ALU.mult),
                           d2pe if g == 3 else None)
                if i == 3:
                    conv(range(8, 10), None)
                if i == 5:
                    do(v.tensor_tensor(LF[:, :, :], P2[:, :, BA2 + 4:BA2 + 8], p_dt[:, lsl].unsqueeze(1).to_broadcast([P, NTB, 4]), ALU.add))
                    do(v.tensor_copy(GL[:, :, :], LF[:, :, :]), d2a)
                    conv(range(10, 12), d2a)
                    dve.wait_ge(a2d.sem, a2d.next("dve"))
                    do(v.scalar_tensor_tensor(CV[:, 0:4, :].rearrange("p b s -> p (b s)"), CV[:, 0:4, :].rearrange("p b s -> p (b s)"), DK ** -0.5,
                                              SQ[:, 0:1024], ALU.mult, ALU.mult))
                    dve.wait_ge(a2d.sem, a2d.next("dve"))
                    do(v.tensor_tensor(CV[:, 4:8, :].rearrange("p b s -> p (b s)"), CV[:, 4:8, :].rearrange("p b s -> p (b s)"), SQ[:, 1024:2048], ALU.mult))
                    dve.wait_ge(a2d.sem, a2d.next("dve"))
                    do(v.tensor_scalar(BETA[:, :, :], BETA[:, :, :], 1.0, None, ALU.add))
                    do(v.reciprocal(BETA[:, :, :], BETA[:, :, :]))
                    do(v.scalar_tensor_tensor(GL[:, :, :], LF[:, :, :], 0.0, GL[:, :, :], ALU.max, ALU.add))
                    do(v.scalar_tensor_tensor(GL[:, :, :], GL[:, :, :], -1.0, ea4.unsqueeze(1).to_broadcast([P, NTB, 4]), ALU.mult, ALU.mult), d2pe)
                if i == 6:
                    t0()
                    do(v.tensor_copy(gc16, T[0][:, 0:16]), t_taken[0])
                    do(v.tensor_tensor(ms8, gc16[:, 8:16], gc16[:, 0:8], ALU.subtract))
                    dve.wait_ge(pe2d.sem, pe2d.next("dve"))
                    for k in range(8):
                        do(v.scalar_tensor_tensor(DT[:, k, :], Sp[:, k // 4, (k % 4) * P:(k % 4 + 1) * P], gc16[:, k:k + 1], c("nm_chunk"), ALU.subtract, ALU.subtract),
                           d2a if k == 7 else None)
                    for tb in range(NTB):
                        cos2 = c("cos2").rearrange("p (t n) -> p t n", t=2)[:, tb, :]
                        sin2 = c("sin2").rearrange("p (t n) -> p t n", t=2)[:, tb, :]
                        do(rope(P2[:, tb, C2:C2 + 512], cos2, sin2, 8, 64, R2A, R2B))
                    do(v.memset(WB, 0.0))
            dve.wait_ge(a2d.sem, a2d.next("dve"))
            dve.wait_ge(pe2d.sem, pe2d.next("dve"))
            for tb in range(NTB):
                do(v.tensor_tensor(MT[:, 4 * tb:4 * tb + 4, :], DT[:, 4 * tb:4 * tb + 4, :], T[tb][:, :].rearrange("p (i t) -> p i t", i=4), ALU.mult),
                   beta_taken if tb else None)
            dve.wait_ge(pe2d.sem, pe2d.next("dve"))
            do(v.tensor_tensor(MT, MT, g2[:, 8:16, :], ALU.mult), d2p)
            do(v.tensor_tensor(MLV[0], MT, c("level0").unsqueeze(1).to_broadcast([P, 8, P]), ALU.mult))
            for tb in range(NTB):
                do(v.tensor_tensor(TT[:, 4 * tb:4 * tb + 4, :], ident.unsqueeze(1).to_broadcast([P, 4, P]), MLV[0][:, 4 * tb:4 * tb + 4, :], ALU.subtract),
                   lv_done if tb else d2pe)
            t0()
            for half in range(2):
                rows = slice(half * CHUNK, (half + 1) * CHUNK)
                do(v.tensor_copy(TN[rows, 0:4, :], T[0][rows, :].rearrange("p (i t) -> p i t", i=4)[:, :, rows]), t_taken[0] if half else None)
            for lv in range(1, LEVELS):
                for tb in range(NTB):
                    cs = slice(4 * tb, 4 * tb + 4)
                    if lv < LEVELS - 1:
                        dve.wait_ge(pe2d.sem, pe2d.next("dve"))
                        do(v.tensor_tensor(TN[:, cs, :], TN[:, cs, :], G[:, 2 + tb, 0:4 * CHUNK].rearrange("p (i t) -> p i t", i=4), ALU.subtract), d2pe)
                    dve.wait_ge(pe2d.sem, pe2d.next("dve"))
                    do(v.tensor_tensor(TT[:, cs, :], TT[:, cs, :], Sp[:, tb, :].rearrange("p (i t) -> p i t", i=4), ALU.subtract), d2pe)
                if lv == 1:
                    do(v.tensor_tensor(AT_[:, :, :], AT_[:, :, :], DT, ALU.mult), lv_done)
                    do(v.tensor_tensor(bek8, BETA[:, :, :].rearrange("p t h -> p (t h)"), eg8, ALU.mult))
                    for tb in range(NTB):
                        q_ = CV[:, 0:4, tb * P:(tb + 1) * P]
                        do(v.tensor_tensor(q_, q_, EGB[:, tb, :].rearrange("p (h t) -> p h t", h=4), ALU.mult))
                if lv <= NTB:
                    t0()
                    src = T[0][:, :].rearrange("p (h d) -> p h d", h=4)
                    cs = slice(4 * (lv - 1), 4 * lv)
                    do(v.tensor_tensor(KBE[:, cs, :], src, bek8[:, cs].unsqueeze(2).to_broadcast([P, 4, P]), ALU.mult), lv_done if lv == 2 else None)
                    do(v.tensor_tensor(KD[:, cs, :], src, kds8[:, cs].unsqueeze(2).to_broadcast([P, 4, P]), ALU.mult), t_taken[0])
                if lv == 3:
                    do(v.memset(STATE[0], 0.0), lv_done)
                    evac(QKT2[:, 0:2, :])
                if lv >= LEVELS - 2:
                    dilated_masked(lv - (LEVELS - 2))
            dilated_sums(0)
            dve.wait_ge(pe2d.sem, pe2d.next("dve"))
            do(v.tensor_copy(DT[0:CHUNK, 0:4, :], g2[0:CHUNK, 0:4, :]), d2pe)
            do(v.tensor_copy(VB[CHUNK:, 0:4, :], g2[CHUNK:, 0:4, :]))
            dve.wait_ge(pe2d.sem, pe2d.next("dve"))
            do(v.tensor_copy(VB[:, 4:8, :], g2[:, 4:8, :]))
            t_state = T[0][:, :].rearrange("p (h e) -> p h e", h=4)
            for n in range(2 * NTB):
                tb, half = n // 2, n % 2
                rows = slice(half * CHUNK, (half + 1) * CHUNK)
                cs = slice(4 * tb, 4 * tb + 4)
                if n:
                    dve.wait_ge(pe2d.sem, pe2d.next("dve"))
                    do(v.tensor_tensor(DT[rows, cs, :], VB[rows, cs, :], G[rows, 0, :].rearrange("p (h e) -> p h e", h=4), ALU.subtract), d2pe)
                    if n < 2 * NTB - 1:
                        do(v.tensor_tensor(STATE[(n + 1) % 2], STATE[n % 2], EGL[:, tb, :, half].unsqueeze(2).to_broadcast([P, 4, P]), ALU.mult))
                if n < 2 * NTB - 1:
                    dve.wait_ge(pe2d.sem, pe2d.next("dve"))
                    behind = STATE[(n + 1) % 2]
                    do(v.tensor_tensor(behind, behind, t_state, ALU.add) if n else v.tensor_copy(behind, t_state), d2pe)
                if n == 1:
                    dilated_out(0)
                    dilated_sums(1)
                if n == 2:
                    gated(0)
            dilated_out(1)
            met(0, 1)
            gated(1, lambda: block_evac(0))
            met(0)
            block_evac(1)
            met(4, 1)
            post_norm(g_tokens, block_sum, X, d2pe)
            vec_free.append(d2pe.made)
            met(0)
            if l == 0:
                block_evac(1)
                for ch in range(NCH2 + 1):
                    if ch < NCH2:
                        met(2)
                        dve.wait_ge(silu_ready.sem, silu_ready.next("dve"))
                        b = 2 * (ch % 2)
                        do(v.tensor_tensor(HB2[:, ch % 2, :, :], HS[:, ch % 2, :, :], G[:, b:b + 2, CH2:2 * CH2], ALU.mult), hb_ready)
                    if ch:
                        ks = slice(2 * ch - 2, 2 * ch)
                        low_evac((ch - 1) % 2, hT2l[:, ks, :], hT2h[:, ks, :])
                met(FT2 // 2, 1)
                post_norm(g_tokens, block_sum, X, d2pe)
                vec_free.append(d2pe.made)
                met(0)

        block_evac(1)
        do(v.memset(RK, 1e6))
        do(v.memset(CW, 0.0))
        do(v.tensor_scalar(PmT[:, :, :], c("iota").unsqueeze(1).to_broadcast([P, NTB, P]), -1.0, None, ALU.is_equal))
        do(v.memset(ACC, 0.0), m_acc)
        dve.wait_ge(pe2d.sem, pe2d.next("dve"))
        do(v.tensor_copy(LG, Sp[:, 0, 0:16].rearrange("p (t e) -> p t e", t=2)))
        for tb in range(NTB):
            do(v.max(TOPV[:, tb, :], LG[:, tb, :]))
            do(v.max_index(IDX[:, tb, :], TOPV[:, tb, :], LG[:, tb, :]))
        do(v.tensor_copy(IDXF, IDX[:, :, :]))
        for tb in range(NTB):
            do(v.tensor_scalar(SEL[:, tb, :], c("iota")[:, 0:8], IDXF[:, tb, 0:1], None, ALU.is_equal))
            do(v.tensor_scalar(OH[:, tb, :], c("iota")[:, 0:8], IDXF[:, tb, 1:2], None, ALU.is_equal))
        do(v.tensor_tensor(ANY, SEL, OH, ALU.add), d2pe)
        do(v.tensor_tensor(PR[:, :, 0:1], TOPV[:, :, 1:2], TOPV[:, :, 0:1], ALU.subtract), d2a)
        do(v.tensor_scalar(LG, ANY, -1e6, 1e6, ALU.mult, ALU.add))
        dve.wait_ge(pe2d.sem, pe2d.next("dve"))
        do(v.tensor_tensor(RK[:, :, 0:8], LG, Sp[:, 1, 0:16].rearrange("p (t e) -> p t e", t=2), ALU.add))
        do(v.tensor_scalar(RK[:, :, 8:16], RK[:, :, 0:8], float(P), None, ALU.subtract))
        do(v.tensor_reduce(CNT[:, 0:1], Sp[:, 1, 16:24], AX_X, ALU.max))

        def slots(i):
            for tb in range(NTB):
                last = v.tensor_scalar(Pm[:, tb, :], c("iota"), RK[:, tb, bass.ds(i, 1)], None, ALU.is_equal)
            last.then_inc(m_p.sem, 1)

        def tokens_low():
            v.tensor_tensor(xgTl[:, :, :], Sp[:, :, :].rearrange("p b (k j) -> p (b k) j", k=4), xgTh[:, :, :].bitcast(F32), ALU.subtract).then_inc(m_gd.sem, 1)

        def add_back(i, tb):
            dve.wait_ge(m_sc.sem, i * 2 + (tb + 1))
            dve.wait_ge(m_acc.sem, i * 2 + (tb + 1))
            v.scalar_tensor_tensor(ACC[:, tb, :], Sp[:, :, :].rearrange("p b n -> p (b n)"), CW[:, tb, bass.ds(i, 1)], ACC[:, tb, :],
                                   ALU.mult, ALU.add).then_inc(m_acc.sem, 1)

        slots(0)
        do(v.tensor_scalar(CNT[:, 1:2], CNT[:, 0:1], float(P), None, ALU.is_gt))
        do(v.tensor_scalar(CNT[:, 2:3], CNT[:, 1:2], float(NE), float(NE), ALU.mult, ALU.add))
        do(v.tensor_copy(FLAG[:, :], CNT[:, 1:3]), m_flag)
        dve.wait_ge(a2d.sem, a2d.next("dve"))
        do(v.tensor_scalar(PR[:, :, 1:2], PR[:, :, 0:1], 1.0, None, ALU.add))
        do(v.reciprocal(PR[:, :, 2:3], PR[:, :, 1:2]))
        do(v.tensor_tensor(PR[:, :, 3:4], PR[:, :, 0:1], PR[:, :, 2:3], ALU.mult))
        for tb in range(NTB):
            do(v.tensor_scalar(CW[:, tb, 1:9], SEL[:, tb, :], PR[:, tb, 2:3], None, ALU.mult))
            do(v.scalar_tensor_tensor(CW[:, tb, 1:9], OH[:, tb, :], PR[:, tb, 3:4], CW[:, tb, 1:9], ALU.mult, ALU.add))
        do(v.tensor_copy(CW[:, :, 9:17], CW[:, :, 1:9]))
        dve.wait_ge(m_g.sem, 1)
        do(v.tensor_copy(xgTh[:, :, :], Sp[:, :, :].rearrange("p b (k j) -> p (b k) j", k=4)))
        tokens_low()

        def result_low():
            v.tensor_tensor(YBl[:, :], G[:, 2:4, :].rearrange("p b n -> p (b n)"), YBh[:, :].bitcast(F32), ALU.subtract).then_inc(m_y.sem, 1)

        def expert_dve(i):
            def low_part(j):
                q, m = (U0 + j) % R, of_dve(e_floats(j))
                dve.wait_ge(w_hi.sem, i * USES_E + (U0 + j + 1))
                v.tensor_tensor(ring_lo[:, q, 0:m], ring[:, q, 0:m], ring_hi[:, (U0 + j) % H, 0:m].bitcast(F32), ALU.subtract).then_inc(w_lo.sem, 1)

            def hidden_e(ch):
                k = ch % 2
                dve.wait_ge(m_th[k].sem, i * ((NCH2 + 1 - k) // 2) + (ch // 2 + 1))
                v.tensor_tensor(hEl[:, 2 * ch:2 * ch + 2, :], T[k][:, 0:2 * P].rearrange("p (k j) -> p k j", k=2),
                                hEh[:, 2 * ch:2 * ch + 2, :].bitcast(F32), ALU.subtract).then_inc(m_tt[k].sem, 1)

            for j in range(H - 1):
                low_part(j)
            dve.wait_ge(m_yh.sem, i + 1)
            result_low()
            for ch in range(NCH2):
                for j in range(2):
                    low_part(2 * ch + H - 1 + j)
                dve.wait_ge(m_silu.sem, i * NCH2 + (ch + 1))
                v.tensor_tensor(HB2[:, ch % 2, 0, :], HS[:, ch % 2, 0, :], G[:, ch % 2, CH2:2 * CH2], ALU.mult).then_inc(m_hb.sem, 1)
                if ch:
                    hidden_e(ch - 1)
                if ch == 2:
                    add_back(i, 0)
                if ch == 5:
                    add_back(i, 1)
            hidden_e(NCH2 - 1)
            dve.wait_ge(m_tf[1].sem, 6 * i + 6)
            slots(i + 1)
            for q in range(H - 1, len(DOWN2)):
                low_part(2 * NCH2 + q)
                if q == GATHER_AT + H - 1:
                    dve.wait_ge(m_ga.sem, i + 1)
                    tokens_low()

        with dve.Fori(0, NE) as i:
            expert_dve(i)
        over = dve.value_load(FLAG[0:1, 0:1], min_val=0, max_val=1)
        with dve.If(over > 0):
            with dve.Fori(NE, 2 * NE) as i:
                expert_dve(i)
        n_all = dve.value_load(FLAG[0:1, 1:2], min_val=NE, max_val=2 * NE)
        dve.wait_ge(m_yh.sem, n_all + 1)
        result_low()
        for tb in range(NTB):
            add_back(n_all, tb)
        dve.wait_ge(m_acc.sem, n_all * 2 + 3)
        post_norm(lambda tb: ACC[:, tb, :], lambda tb: None, XN, f_out, f_r, f_p)

    @block.gpsimd
    def _(pool):
        g = nc.gpsimd

        def load(dst, src, s=loaded):
            pool.dma_start(dst, src, allow_slow_non_contiguous=True).then_inc(s.sem, 16)

        def power(dst, src, n, s):
            g.tensor_tensor(dst, src, c("mhalf")[:, 0:n], ALU.pow).then_inc(s.sem, 1)

        def root(tb, src, eps, s):
            step(pool, g.tensor_scalar(ms[:, tb:tb + 1], src, eps, None, ALU.add), pstep)
            power(rstd[:, tb:tb + 1], ms[:, tb:tb + 1], 1, s)

        def rms():
            for tb in range(NTB):
                pool.wait_ge(s_ssq.sem, s_ssq.next("pool"))
                root(tb, ssq[:, tb:tb + 1], EPS, s_rstd)

        def rms_behind_rms():
            for tb in range(NTB):
                for _ in range(2):
                    pool.wait_ge(s_ssq.sem, s_ssq.next("pool"))
                    root(tb, ssq[:, tb:tb + 1], EPS, s_rstd)

        def layer_norm(s_in=d2p, s_out=p2d):
            for tb in range(NTB):
                pool.wait_ge(s_in.sem, s_in.next("pool"))
                root(tb, mv[:, tb, 1:2], 1e-5, s_out)

        def asked(dst, src, n, s_in=d2p, s_out=p2d):
            pool.wait_ge(s_in.sem, s_in.next("pool"))
            power(dst, src, n, s_out)

        n_lo = [0, 0]

        def met(n, ahead=H - 1):
            n_lo[1] += n
            while n_lo[0] < min(n_lo[1] + ahead, U0):
                t = n_lo[0]
                n_lo[0] += 1
                m = floats_of(TILES[t])
                cs = slice(of_dve(m), m)
                pool.wait_ge(w_hi.sem, t + 1)
                g.tensor_tensor(ring_lo[:, t % R, cs], ring[:, t % R, cs], ring_hi[:, t % H, cs].bitcast(F32), ALU.subtract).then_inc(w_lo_pool.sem, 1)

        def rope(x, cos, sin, heads, width, a, b, s=None):
            xv = x.rearrange("p (h d) -> p h d", h=heads)
            a, b = a.rearrange("p (h d) -> p h d", h=heads), b.rearrange("p (h d) -> p h d", h=heads)
            hw = width // 2
            step(pool, g.tensor_tensor(a, xv, cos.unsqueeze(1).to_broadcast([P, heads, width]), ALU.mult), pstep)
            step(pool, g.tensor_tensor(b[:, :, 0:hw], xv[:, :, hw:], sin[:, 0:hw].unsqueeze(1).to_broadcast([P, heads, hw]), ALU.mult), pstep)
            step(pool, g.tensor_tensor(b[:, :, hw:], xv[:, :, 0:hw], sin[:, hw:].unsqueeze(1).to_broadcast([P, heads, hw]), ALU.mult), pstep)
            step(pool, g.tensor_tensor(xv, a, b, ALU.add), s or pstep)

        def gains(q, name, l):
            vec_loaded[q].made += 16
            pool.dma_start(VEC[:, q, :], w[name][l].partition_broadcast(P)).then_inc(vec_loaded[q].sem, 16)

        def gains_loaded(q):
            pool.wait_ge(vec_loaded[q].sem, vec_loaded[q].made)

        gains(1, "norm_pre_mix", 0)
        pool.wait_ge(c_loaded[0].sem, 16)
        gains_loaded(1)
        rms()
        met(1)
        gains(0, "norm_post_mix", 0)
        for l in range(DEPTH):
            if l:
                gains_loaded(1)
                rms()
                gains(0, "norm_post_mix", l)
                met(1)
            for i, col in ((4, C_Q), (5, C_K)):
                if i == 4:
                    met(2 * (i + 1) - 1)
                else:
                    met(2 * (IN_N - 1 - 4), 0)
                pool.wait_ge(g_dve.sem, g_dve_in[l][i])
                pool.wait_ge(g_act.sem, l * G_ACT + i + 1)
                for tb in range(NTB):
                    rope(PROJ[:, tb, col:col + 256], RCOS32[:, tb, :], RSIN32[:, tb, :], 8, 32, XN[:, 0, 768:1024], XN[:, 1, 768:1024],
                         c_rotated if (i == 5 and tb) else None)
            pool.wait_ge(g_dve.sem, g_dve_in[l][IN_N - 1])
            pool.wait_ge(g_act.sem, l * G_ACT + IN_N)
            for tb in range(NTB):
                for col, heads in ((D_Q, 4), (D_K, 2)):
                    rope(PROJ[:, tb, col:col + 64 * heads], RCOS[:, tb, :], RSIN[:, tb, :], heads, 64, XN[:, 0, 768:768 + 64 * heads], XN[:, 1, 768:768 + 64 * heads])
            for q, col in enumerate((D_K, D_K + 64)):
                for tb in range(NTB):
                    last = g.tensor_copy(IKD[:, 1 + q, tb, :].rearrange("p (r d) -> p r d", r=2),
                                         PROJ[:, tb, col:col + 64].unsqueeze(1).to_broadcast([P, 2, 64]))
            last.then_inc(p2pe.sem, 1)
            gains(1, "norm_pre_mlp", l)
            asked(r8, ms8, 8)
            met(0)
            for q in range(2):
                gains_loaded(q)
            met(4, 1)
            rms_behind_rms()
            met(0)
            gains(0, "norm_post_mlp", l)
            load(PLE, w["p"][l, 0].rearrange("(t p) d -> p t d", p=P), misc_loaded)
            gains_loaded(0)
            met(32, 1)
            rms()
            gains(1, *(("norm_pre_mix", l + 1) if l + 1 < DEPTH else ("ln1_b_2", 0)))
            if l == DEPTH - 1:
                load(WSA, w["a_ws_2"][0].rearrange("g t s -> t g s"), misc_loaded)
            met(5, 1)
        for l in range(DEPTH):
            if l:
                pool.wait_ge(d2pe.sem, vec_free[2 * l - 1])
                gains(0, "ln1_g_2", l)
                gains(1, "ln1_b_2", l)
            met(2)
            layer_norm()
            if l == 0:
                gains(0, "ln1_g_2", 0)
            met(2 * len(IN2_CHUNKS) - 2, 0)
            pool.wait_ge(d2p.sem, d2p.next("pool"))
            for lv in range(1, LEVELS):
                if lv >= 2:
                    pool.wait_ge(lv_done.sem, lv_done.next("pool"))
                m = c(f"level{lv}").unsqueeze(1).to_broadcast([P, 8, P])
                g.tensor_tensor(MLV[lv % 2], MT, m, ALU.mult).then_inc(p2pe.sem, 1)
            pool.wait_ge(g_act.sem, DEPTH * G_ACT + (l + 1) * len(IN2_CHUNKS))
            z = P2[:, :, Z2:Z2 + 512].rearrange("p t (h e) -> p t h e", h=4)
            for tb in range(NTB):
                last = g.tensor_tensor(z[:, tb], z[:, tb], p_bn[:, l, :].unsqueeze(1).to_broadcast([P, 4, P]), ALU.mult)
            last.then_inc(z_ready.sem, 1)
            met(0)
            for tb in range(NTB):
                pool.wait_ge(o_ms.sem, o_ms.next("pool"))
                cs = slice(4 * tb, 4 * tb + 4)
                step(pool, g.tensor_scalar(ms8[:, cs], ms8[:, cs], 1e-6, None, ALU.add), pstep)
                power(r8[:, cs], ms8[:, cs], 4, o_root)
            for q in range(2):
                gains_loaded(q)
            met(4, 1)
            layer_norm()
            met(0)
            if l + 1 < DEPTH:
                load(WSA, w["a_ws_2"][l + 1].rearrange("g t s -> t g s"), misc_loaded)
            pool.wait_ge(d2pe.sem, vec_free[2 * l])
            gains(0, "ln2_g_2", l)
            gains(1, "ln2_b_2", l)
            for q in range(2):
                gains_loaded(q)
            if l == 0:
                met(2 * NCH2 + FT2 // 2, 1)
                layer_norm()
                met(0)

        def expert_pool(i):
            for j in range(USES_E):
                q, m = (U0 + j) % R, e_floats(j)
                pool.wait_ge(w_hi.sem, i * USES_E + (U0 + j + 1))
                cs = slice(of_dve(m), m)
                g.tensor_tensor(ring_lo[:, q, cs], ring[:, q, cs], ring_hi[:, (U0 + j) % H, cs].bitcast(F32), ALU.subtract).then_inc(w_lo_pool.sem, 1)

        with pool.Fori(0, NE) as i:
            expert_pool(i)
        pool.wait_ge(m_flag.sem, 1)
        over = pool.value_load(FLAG[0:1, 0:1], min_val=0, max_val=1)
        with pool.If(over > 0):
            with pool.Fori(NE, 2 * NE) as i:
                expert_pool(i)
        layer_norm(f_r, f_p)

    ctx.close()


_INS = ["x", "p", "positions", "w_in", "b_forget", "lambda_q1", "lambda_k1", "lambda_q2", "lambda_k2", "diff_subln",
        "sinks", "w_out", "norm_pre_mix", "norm_post_mix", "norm_pre_mlp", "norm_post_mlp", "w_mlp_up", "w_mlp_down",
        "w_ple_proj", "w_ple_gate", "w_in_2", "conv_w_2", "a_ln_g_2", "a_ln_b_2", "a_ws_2", "a_bs_2", "b_a_log_2",
        "b_dt_bias_2", "b_norm_g_2", "w_out_2", "ln1_g_2", "ln1_b_2", "ln2_g_2", "ln2_b_2", "ffn_w_gate_2", "ffn_w_up_2",
        "ffn_w_down_2", "moe_router_2", "moe_w_gate_2", "moe_w_up_2", "moe_w_down_2"]


def kernel(**inputs):
    import concourse.bacc as _bacc
    from concourse.bass_utils import run_bass_kernel_spmd as _run

    nc = _bacc.Bacc("TRN2", target_bir_lowering=False, num_devices=1)
    table, at = consts()
    arrays, w = {}, {}
    for name in _INS:
        a = np.ascontiguousarray(inputs[name])
        arrays[f"in_{name}"] = a
        w[name] = nc.dram_tensor(f"in_{name}", a.shape, mybir.dt.from_np(a.dtype), kind="ExternalInput").ap()
    arrays["shape_tables"] = table
    const_d = nc.dram_tensor("shape_tables", table.shape, F32, kind="ExternalInput").ap()
    out_d = nc.dram_tensor("out", (1, S, D), F32, kind="ExternalOutput").ap()
    build(nc, at, table.shape[1], const_d, w, out_d)
    r = _run(nc, [arrays], core_ids=[0])
    return r.results[0]["out"]
```
